# Optimizing a Trainium2 kernel written in Bass

```python
import math
import jax
import jax.numpy as jnp
from jax import lax
import numpy as np

D_MODEL = 1024
BATCH = 1
SEQ = 256
DEPTH = 2

EPS = 1e-6
PLE_DIM = 256
N_BRANCHES = 4

CONV_CH = 512
CONV_K = 31

SSM_HEADS = 8
SSM_HEAD_DIM = 64
SSM_INNER = SSM_HEADS * SSM_HEAD_DIM
SSM_GROUPS = 2
SSM_STATE = 64
SSM_CONV = 5
SSM_CONV_CH = SSM_INNER + 2 * SSM_GROUPS * SSM_STATE
SSM_CHUNK = 128

ATT_PATTERNS = ((128, 1), (512, 4), (2048, 16))
ATT_GROUPS = len(ATT_PATTERNS)
ATT_HEADS = 8
ATT_HEAD_DIM = 64
ATT_WIDTH = ATT_HEADS * ATT_HEAD_DIM
REL_BUCKETS = 32
REL_MAX_DIST = 1024

FNET_GROUPS = 4
FNET_GROUP_DIM = 128
FNET_WIDTH = FNET_GROUPS * FNET_GROUP_DIM

FFN_DIM = 2816
N_EXPERTS = 8
TOP_K = 2
EXPERT_DIM = 3584

ATT_IN_COLS = 3 * ATT_GROUPS * ATT_WIDTH
CONV_IN_COLS = 2 * CONV_CH
SSM_IN_COLS = SSM_INNER + SSM_CONV_CH + 2 * SSM_HEADS
FNET_IN_COLS = FNET_WIDTH
OFF_CONV = ATT_IN_COLS
OFF_SSM = OFF_CONV + CONV_IN_COLS
OFF_FNET = OFF_SSM + SSM_IN_COLS
IN_COLS = OFF_FNET + FNET_IN_COLS

kernel_name = 'hybrid_parallel_mixer_encoder'

def rmsnorm(x, g):
    xf = x.astype(jnp.float32)
    y = xf * lax.rsqrt(jnp.mean(xf * xf, axis=-1, keepdims=True) + EPS)
    return (y * g.astype(jnp.float32)).astype(x.dtype)

def layernorm(x, g, b):
    xf = x.astype(jnp.float32)
    mu = jnp.mean(xf, axis=-1, keepdims=True)
    var = jnp.mean(jnp.square(xf - mu), axis=-1, keepdims=True)
    y = (xf - mu) * lax.rsqrt(var + EPS)
    return (y * g.astype(jnp.float32) + b.astype(jnp.float32)).astype(x.dtype)

def depthwise_conv(x, w, b):
    y = lax.conv_general_dilated(
        x, w[:, None, :].astype(x.dtype), window_strides=(1,), padding='SAME',
        dimension_numbers=('NWC', 'WIO', 'NWC'), feature_group_count=x.shape[-1])
    return y + b.astype(x.dtype)

def swiglu(x, w1, w3, w2):
    return (jax.nn.silu(x @ w1) * (x @ w3)) @ w2

def t5_bucket(rel):
    half = REL_BUCKETS // 2
    max_exact = half // 2
    n = np.abs(rel)
    large = max_exact + (np.log(np.maximum(n, 1) / max_exact) / math.log(REL_MAX_DIST / max_exact)
                         * (half - max_exact)).astype(np.int32)
    large = np.minimum(large, half - 1)
    return np.where(rel > 0, half, 0) + np.where(n < max_exact, n, large)

def dilated_window_attention(q, k, v, bias, dilation, half):
    bsz, S, H, Dh = q.shape
    L = S // dilation
    W = half
    nb = -(-L // W)
    Lp = nb * W

    def to_sub(t):
        t = t.reshape(bsz, L, dilation, H, Dh).transpose(0, 2, 1, 3, 4)
        return jnp.pad(t, ((0, 0), (0, 0), (0, Lp - L), (0, 0), (0, 0)))

    def band(t):
        t = jnp.pad(to_sub(t), ((0, 0), (0, 0), (W, W), (0, 0), (0, 0)))
        t = t.reshape(bsz, dilation, nb + 2, W, H, Dh)
        return jnp.concatenate([t[:, :, :-2], t[:, :, 1:-1], t[:, :, 2:]], axis=3)

    qb = to_sub(q).reshape(bsz, dilation, nb, W, H, Dh)
    kb, vb = band(k), band(v)

    qi = np.arange(W)[:, None]
    kj = np.arange(3 * W)[None, :] - W
    rel = kj - qi
    key_pos = np.arange(nb)[:, None, None] * W + kj[None]
    valid = (np.abs(rel) <= W)[None] & (key_pos >= 0) & (key_pos < L)

    s = jnp.einsum('brnqhd,brnkhd->brnhqk', qb, kb, preferred_element_type=jnp.float32)
    s = s * (Dh ** -0.5) + bias.astype(jnp.float32)[None, None, None]
    s = jnp.where(valid[None, None, :, None], s, -1e30)
    m = jnp.max(s, axis=-1, keepdims=True)
    e = jnp.exp(s - m)
    den = jnp.sum(e, axis=-1)
    o = jnp.einsum('brnhqk,brnkhd->brnqhd', e, vb.astype(jnp.float32))
    o = o / den.transpose(0, 1, 2, 4, 3)[..., None]
    lse = (m[..., 0] + jnp.log(den)).transpose(0, 1, 2, 4, 3)

    def from_sub(t):
        t = t.reshape((bsz, dilation, Lp) + t.shape[4:])[:, :, :L]
        t = jnp.moveaxis(t, 1, 2)
        return t.reshape((bsz, S) + t.shape[3:])

    return from_sub(o), from_sub(lse)

def attention_branch(u, rel_bias, w_o):
    bsz, S, _ = u.shape
    qkv = u.reshape(bsz, S, 3, ATT_GROUPS, ATT_HEADS, ATT_HEAD_DIM)
    outs, lses = [], []
    for g, (window, dil) in enumerate(ATT_PATTERNS):
        half = window // (2 * dil)
        rel = np.arange(3 * half)[None, :] - half - np.arange(half)[:, None]
        bucket = t5_bucket(dil * rel)
        bias = rel_bias[bucket][:, :, g * ATT_HEADS:(g + 1) * ATT_HEADS].transpose(2, 0, 1)
        o, lse = dilated_window_attention(qkv[:, :, 0, g], qkv[:, :, 1, g], qkv[:, :, 2, g],
                                          bias, dil, half)
        outs.append(o)
        lses.append(lse)
    wts = jax.nn.softmax(jnp.stack(lses, axis=2), axis=2)
    o = jnp.einsum('bsghd,bsgh->bshd', jnp.stack(outs, axis=2), wts)
    return o.reshape(bsz, S, ATT_WIDTH).astype(u.dtype) @ w_o

def conformer_branch(u, dw, dw_b, ln_g, ln_b, w_o):
    a, gate = jnp.split(u, 2, axis=-1)
    hid = a * jax.nn.sigmoid(gate)
    hid = depthwise_conv(hid, dw, dw_b)
    hid = jax.nn.silu(layernorm(hid, ln_g, ln_b))
    return hid @ w_o

def ssd_scan(x, dt, a_log, b_in, c_in):
    bsz, L = x.shape[:2]
    nc = L // SSM_CHUNK
    hg = SSM_HEADS // SSM_GROUPS
    A = -jnp.exp(a_log.astype(jnp.float32)).reshape(SSM_GROUPS, hg)
    dt = dt.reshape(bsz, nc, SSM_CHUNK, SSM_GROUPS, hg)
    xd = x.astype(jnp.float32).reshape(bsz, nc, SSM_CHUNK, SSM_GROUPS, hg, SSM_HEAD_DIM) * dt[..., None]
    bb = b_in.astype(jnp.float32).reshape(bsz, nc, SSM_CHUNK, SSM_GROUPS, SSM_STATE)
    cc = c_in.astype(jnp.float32).reshape(bsz, nc, SSM_CHUNK, SSM_GROUPS, SSM_STATE)
    a_cs = jnp.cumsum(dt * A, axis=2)

    seg = a_cs[:, :, :, None] - a_cs[:, :, None, :]
    lower = np.tril(np.ones((SSM_CHUNK, SSM_CHUNK), dtype=bool))[:, :, None, None]
    decay = jnp.exp(jnp.where(lower, seg, -jnp.inf))
    scores = jnp.einsum('bclgn,bcsgn->bclsg', cc, bb)
    y_diag = jnp.einsum('bclsg,bclsgh,bcsghp->bclghp', scores, decay, xd)

    decay_st = jnp.exp(a_cs[:, :, -1:] - a_cs)
    states = jnp.einsum('bclgn,bclgh,bclghp->bcghpn', bb, decay_st, xd)
    chunk_decay = jnp.exp(a_cs[:, :, -1])

    def step(carry, inp):
        st, dec = inp
        return carry * dec[..., None, None] + st, carry

    init = jnp.zeros((bsz, SSM_GROUPS, hg, SSM_HEAD_DIM, SSM_STATE), jnp.float32)
    _, prev = lax.scan(step, init, (jnp.moveaxis(states, 1, 0), jnp.moveaxis(chunk_decay, 1, 0)))
    prev = jnp.moveaxis(prev, 0, 1)
    y_off = jnp.einsum('bclgn,bcghpn,bclgh->bclghp', cc, prev, jnp.exp(a_cs))
    return (y_diag + y_off).reshape(bsz, L, SSM_HEADS, SSM_HEAD_DIM)

def ssd_branch(u, conv_w, conv_b, a_log, dt_bias, d_skip, norm_g, w_o):
    bsz, L, _ = u.shape
    z = u[..., :SSM_INNER]
    xbc = u[..., SSM_INNER:SSM_INNER + SSM_CONV_CH]
    dt_raw = u[..., SSM_INNER + SSM_CONV_CH:]
    xbc = jax.nn.silu(depthwise_conv(xbc, conv_w, conv_b))
    xs = xbc[..., :SSM_INNER].reshape(bsz, L, SSM_HEADS, SSM_HEAD_DIM)
    bs = xbc[..., SSM_INNER:SSM_INNER + SSM_GROUPS * SSM_STATE].reshape(bsz, L, SSM_GROUPS, SSM_STATE)
    cs = xbc[..., SSM_INNER + SSM_GROUPS * SSM_STATE:].reshape(bsz, L, SSM_GROUPS, SSM_STATE)
    dt = jax.nn.softplus(dt_raw.astype(jnp.float32).reshape(bsz, L, 2, SSM_HEADS)
                         + dt_bias.astype(jnp.float32))
    flip = lambda t: jnp.flip(t, axis=1)
    y_fwd = ssd_scan(xs, dt[:, :, 0], a_log[0], bs, cs)
    y_bwd = flip(ssd_scan(flip(xs), flip(dt[:, :, 1]), a_log[1], flip(bs), flip(cs)))
    y = y_fwd + y_bwd + d_skip.astype(jnp.float32)[:, None] * xs.astype(jnp.float32)
    y = y.reshape(bsz, L, SSM_INNER) * jax.nn.silu(z.astype(jnp.float32))
    y = rmsnorm(y, norm_g)
    return y.astype(u.dtype) @ w_o

def fourier_branch(u, w_o):
    bsz, S, _ = u.shape
    t = u.astype(jnp.float32).reshape(bsz, S, FNET_GROUPS, FNET_GROUP_DIM)
    f = jnp.fft.fft2(t, axes=(1, 3), norm='ortho').real
    return f.reshape(bsz, S, FNET_WIDTH).astype(u.dtype) @ w_o

def moe_swiglu(x, router, w1, w3, w2):
    logits = jnp.einsum('bsd,de->bse', x, router, preferred_element_type=jnp.float32)
    top_val, top_idx = lax.top_k(logits, TOP_K)
    top_w = jax.nn.softmax(top_val, axis=-1)
    combine = jnp.einsum('bske,bsk->bse', jax.nn.one_hot(top_idx, N_EXPERTS, dtype=jnp.float32),
                         top_w).astype(x.dtype)
    out = jnp.zeros_like(x)
    for e in range(N_EXPERTS):
        out = out + combine[..., e:e + 1] * swiglu(x, w1[e], w3[e], w2[e])
    return out

def setup_inputs(seed: int = 0) -> dict:
    key = jax.random.key(seed)
    ks = iter(jax.random.split(key, 48))
    f32 = jnp.float32

    def nrm(shape, scale):
        return jax.random.normal(next(ks), shape, f32) * scale

    def gain(shape):
        return 1.0 + 0.02 * jax.random.normal(next(ks), shape, f32)

    n_dense = (DEPTH + 1) // 2
    n_moe = DEPTH // 2
    dt0 = jnp.exp(jax.random.uniform(next(ks), (DEPTH, 2, SSM_HEADS), f32,
                                     math.log(1e-3), math.log(1e-1)))
    return {
        'x': nrm((BATCH, SEQ, D_MODEL), 1.0),
        'p': nrm((DEPTH, BATCH, SEQ, PLE_DIM), 1.0),
        'rel_bias': nrm((REL_BUCKETS, ATT_GROUPS * ATT_HEADS), 0.2),
        'norm_mix': gain((DEPTH, D_MODEL)),
        'w_in': nrm((DEPTH, D_MODEL, IN_COLS), D_MODEL ** -0.5),
        'conv_dw': nrm((DEPTH, CONV_K, CONV_CH), CONV_K ** -0.5),
        'conv_dw_b': nrm((DEPTH, CONV_CH), 0.02),
        'conv_ln_g': gain((DEPTH, CONV_CH)),
        'conv_ln_b': nrm((DEPTH, CONV_CH), 0.02),
        'conv_out': nrm((DEPTH, CONV_CH, D_MODEL), CONV_CH ** -0.5),
        'ssm_conv_w': nrm((DEPTH, SSM_CONV, SSM_CONV_CH), SSM_CONV ** -0.5),
        'ssm_conv_b': nrm((DEPTH, SSM_CONV_CH), 0.02),
        'ssm_a_log': jnp.log(jax.random.uniform(next(ks), (DEPTH, 2, SSM_HEADS), f32, 1.0, 16.0)),
        'ssm_dt_bias': dt0 + jnp.log(-jnp.expm1(-dt0)),
        'ssm_d': gain((DEPTH, SSM_HEADS)),
        'ssm_norm': gain((DEPTH, SSM_INNER)),
        'ssm_out': nrm((DEPTH, SSM_INNER, D_MODEL), SSM_INNER ** -0.5),
        'attn_out': nrm((DEPTH, ATT_WIDTH, D_MODEL), ATT_WIDTH ** -0.5),
        'fnet_out': nrm((DEPTH, FNET_WIDTH, D_MODEL), FNET_WIDTH ** -0.5),
        'w_gate': nrm((DEPTH, N_BRANCHES, D_MODEL, D_MODEL), D_MODEL ** -0.5),
        'b_gate': nrm((DEPTH, N_BRANCHES, D_MODEL), 0.02),
        'w_out': nrm((DEPTH, D_MODEL, D_MODEL), D_MODEL ** -0.5),
        'norm_ffn': gain((DEPTH, D_MODEL)),
        'ffn_w1': nrm((n_dense, D_MODEL, FFN_DIM), D_MODEL ** -0.5),
        'ffn_w3': nrm((n_dense, D_MODEL, FFN_DIM), D_MODEL ** -0.5),
        'ffn_w2': nrm((n_dense, FFN_DIM, D_MODEL), FFN_DIM ** -0.5),
        'moe_router': nrm((n_moe, D_MODEL, N_EXPERTS), D_MODEL ** -0.5),
        'moe_w1': nrm((n_moe, N_EXPERTS, D_MODEL, EXPERT_DIM), D_MODEL ** -0.5),
        'moe_w3': nrm((n_moe, N_EXPERTS, D_MODEL, EXPERT_DIM), D_MODEL ** -0.5),
        'moe_w2': nrm((n_moe, N_EXPERTS, EXPERT_DIM, D_MODEL), EXPERT_DIM ** -0.5),
        'ple_gate': nrm((DEPTH, D_MODEL, D_MODEL), D_MODEL ** -0.5),
        'ple_proj': nrm((DEPTH, PLE_DIM, D_MODEL), PLE_DIM ** -0.5),
        'final_norm': gain((D_MODEL,)),
    }

def reference(x, p, rel_bias, norm_mix, w_in, conv_dw, conv_dw_b, conv_ln_g, conv_ln_b, conv_out,
              ssm_conv_w, ssm_conv_b, ssm_a_log, ssm_dt_bias, ssm_d, ssm_norm, ssm_out,
              attn_out, fnet_out, w_gate, b_gate, w_out, norm_ffn, ffn_w1, ffn_w3, ffn_w2,
              moe_router, moe_w1, moe_w3, moe_w2, ple_gate, ple_proj, final_norm):
    h = x
    for l in range(DEPTH):
        xn = rmsnorm(h, norm_mix[l])
        u = xn @ w_in[l]
        branches = (
            attention_branch(u[..., :OFF_CONV], rel_bias, attn_out[l]),
            conformer_branch(u[..., OFF_CONV:OFF_SSM], conv_dw[l], conv_dw_b[l],
                             conv_ln_g[l], conv_ln_b[l], conv_out[l]),
            ssd_branch(u[..., OFF_SSM:OFF_FNET], ssm_conv_w[l], ssm_conv_b[l], ssm_a_log[l],
                       ssm_dt_bias[l], ssm_d[l], ssm_norm[l], ssm_out[l]),
            fourier_branch(u[..., OFF_FNET:], fnet_out[l]),
        )
        mixed = jnp.zeros_like(h)
        for i, br in enumerate(branches):
            mixed = mixed + jax.nn.sigmoid(xn @ w_gate[l, i] + b_gate[l, i]) * br
        h = h + mixed @ w_out[l]

        xn = rmsnorm(h, norm_ffn[l])
        if l % 2 == 0:
            h = h + swiglu(xn, ffn_w1[l // 2], ffn_w3[l // 2], ffn_w2[l // 2])
        else:
            h = h + moe_swiglu(xn, moe_router[l // 2], moe_w1[l // 2], moe_w3[l // 2], moe_w2[l // 2])

        h = h + jax.nn.sigmoid(h @ ple_gate[l]) * (p[l] @ ple_proj[l])
    return rmsnorm(h, final_norm)


_drawn_inputs = setup_inputs


def setup_inputs(seed=0):
    import zlib

    import numpy as np

    out = dict(_drawn_inputs(seed))
    spreads = {}
    factors = {'conv_ln_g': 12.371,
     'conv_ln_b': 10.641,
     'ssm_d': 14.931,
     'b_gate': 6.622,
     'final_norm': 20.523,
     'rel_bias': 3.336,
     'ssm_conv_b': 4.339,
     'ssm_norm': 8.849,
     'ssm_a_log': 2.914,
     'norm_ffn': 3.486}
    for name, (base, spread) in spreads.items():
        noise = np.random.default_rng([zlib.crc32(name.encode()), seed]).standard_normal(out[name].shape)
        drawn = base * np.exp(spread * noise) if base else spread * noise
        out[name] = jnp.asarray(drawn.astype(out[name].dtype))
    for name, factor in factors.items():
        out[name] = (out[name] * factor).astype(out[name].dtype)
    return out
```

```python
from contextlib import ExitStack
import math

import numpy as np

import concourse.bass as bass
from concourse import mybir

F32 = mybir.dt.float32
I32 = mybir.dt.int32
U32 = mybir.dt.uint32
ACT = mybir.ActivationFunctionType
ALU = mybir.AluOpType
AX_X = mybir.AxisListType.X

P = 128
D_MODEL = 1024
SEQ = 256
DEPTH = 2
EPS = 1e-6
PLE_DIM = 256
N_BRANCHES = 4
CONV_CH, CONV_K = 512, 31
SSM_HEADS, SSM_HEAD_DIM, SSM_GROUPS, SSM_STATE, SSM_CONV = 8, 64, 2, 64, 5
SSM_INNER = SSM_HEADS * SSM_HEAD_DIM
SSM_CONV_CH = SSM_INNER + 2 * SSM_GROUPS * SSM_STATE
ATT_PATTERNS = ((128, 1), (512, 4), (2048, 16))
ATT_GROUPS, ATT_HEADS, ATT_HEAD_DIM = 3, 8, 64
ATT_WIDTH = ATT_HEADS * ATT_HEAD_DIM
REL_BUCKETS, REL_MAX_DIST = 32, 1024
FNET_GROUPS, FNET_GROUP_DIM = 4, 128
FNET_WIDTH = FNET_GROUPS * FNET_GROUP_DIM
FFN_DIM, N_EXPERTS, EXPERT_DIM = 2816, 8, 3584
OFF_CONV = 3 * ATT_GROUPS * ATT_WIDTH
OFF_SSM = OFF_CONV + 2 * CONV_CH
OFF_DT = OFF_SSM + SSM_INNER + SSM_CONV_CH
OFF_FNET = OFF_DT + 2 * SSM_HEADS
MASKED = -1e30

KT = D_MODEL // P
TT = SEQ // P
CT = CONV_CH // P
XT = SSM_CONV_CH // P
DT = 2 * SSM_HEADS
PAD = CONV_K // 2
SPAD = SSM_CONV // 2
HALF = SEQ

BLK = 2048
RING = 6
COLS = BLK // KT
PROJ_BLOCKS = 29
BRANCH_BLOCKS = 6
MIX_BLOCKS = PROJ_BLOCKS + N_BRANCHES * BRANCH_BLOCKS + 4
MIX_ROUNDS = 10
DENSE_CHUNKS = FFN_DIM // COLS
EXP_CHUNKS = EXPERT_DIM // COLS
DENSE_ROUNDS = (3 * DENSE_CHUNKS + RING - 1) // RING
PASS_ROUNDS = 3 * EXP_CHUNKS // RING
PLE_BLOCKS = 5
LAYER0_ROUNDS = MIX_ROUNDS + DENSE_ROUNDS + 1
assert MIX_BLOCKS <= MIX_ROUNDS * RING and PLE_BLOCKS < RING and 3 * EXP_CHUNKS % RING == 0

_PARAMS = (("norm_mix", KT), ("norm_ffn", KT), ("final_norm", KT), ("b_gate", N_BRANCHES * KT),
           ("conv_dw", CONV_K * CT), ("conv_b", CT), ("ln_g", CT), ("ln_b", CT),
           ("ssm_w", SSM_CONV * XT), ("ssm_b", XT), ("ssm_norm", CT),
           ("ssm_d", SSM_HEADS), ("a_log", DT), ("dt_bias", DT),
           ("w_dt", KT * DT), ("router", KT * N_EXPERTS),
           ("p", PLE_DIM // P * SEQ))
AT = {}
PK = 0
for _name, _n in _PARAMS:
    AT[_name] = PK
    PK += _n

_CONSTS = (("ident", P), ("upto", P), ("from", P), ("before", P), ("ones", P), ("slots", P),
           ("dft_ch", 2 * P), ("dft_cos", TT * SEQ), ("dft_sin", TT * SEQ), ("experts", N_EXPERTS))
CAT = {}
CK = 0
for _name, _n in _CONSTS:
    CAT[_name] = CK
    CK += _n

FNET, CONV, SSM, ATT = range(4)
BRANCH_OF = (3, 1, 2, 0)
N_PROJ = 59
DTC = 20
SSM_HC = 7
SSM_YC = 6
RC_EXP, RC_MASK = 6, 13
T_XBC, T_Z, T_DT, T_FN, T_Q = 8, 14, 18, 19, 23
T_V = T_Q + 24
UNITS = ATT_HEADS * TT
HP = ATT_HEADS // 2
GK = ATT_GROUPS * SEQ


def trunk_program(nc, x, wm, wd, we, wp, pk_in, cst_in, onehot, relb, out):
    ctx = ExitStack()
    with ctx:
        def sb(name, shape, dt=F32):
            return ctx.enter_context(nc.sbuf_tensor(name, shape, dt))

        def sem(name):
            return ctx.enter_context(nc.semaphore(name))

        scratch = nc.dram_tensor("bias_rows", [ATT_HEADS, ATT_GROUPS, 2 * SEQ], F32)

        ring = sb("ring", [P, RING, BLK])
        h = sb("h", [P, KT, SEQ])
        xn = sb("xn", [P, KT, SEQ])
        mix = sb("mix", [P, KT, SEQ])
        pk = sb("params_sb", [P, PK])
        cst = sb("constants_sb", [P, CK])
        rstd = sb("rstd", [P, SEQ])
        rms_t = sb("rms_t", [P, 2, SEQ])
        glu = sb("glu", [P, CT, SEQ + 2 * PAD])
        glu_a = sb("glu_a", [P, 2, 2, SEQ])
        glu_s = sb("glu_s", [P, 2, 2, SEQ])
        cvfa = sb("cvfa", [P, 2 * CT * SEQ])
        xbcp = sb("xbcp", [P, XT, SEQ + 2 * SPAD])
        xbc = sb("xbc", [P, XT, SEQ])
        qk = sb("qk", [P, 2 * ATT_GROUPS, HP, SEQ])
        v = sb("v", [P, TT, ATT_GROUPS * ATT_WIDTH])
        ybr = sb("ybr", [P, N_BRANCHES * CT, SEQ])
        dts = sb("dts", [P, 8, TT * DT])
        dt_ = sb("dt", [P, TT, DT])
        dta = sb("dta", [P, TT, DT])
        a_neg = sb("a_pos", [P, DT])
        sc = sb("sc", [P, SSM_GROUPS, 6, P])
        ua = sb("ua", [P, 2, 4, P])
        dg = sb("dg", [P, 4, P])
        nb = sb("nb", [P, 2, 6])
        ex = sb("ex", [P, 2, 6, P])
        mm_ = sb("mm", [P, 2, 6, P])
        yst = sb("yst", [P, 8])
        ast = sb("ast", [P, 2, 4])
        gs = sb("gs", [P, 2, SEQ])
        gt = sb("gt", [P, 2, SEQ])

        def view(buf, lo, shape, pattern, **sizes):
            n = int(np.prod(shape))
            flat = buf if len(buf.shape) == 2 else buf.rearrange("p a b -> p (a b)") if len(buf.shape) == 3 \
                else buf.rearrange("p a b c -> p (a b c)")
            return flat[:, lo:lo + n] if pattern == "p c -> p c" else flat[:, lo:lo + n].rearrange(pattern, **sizes)

        cv = view(cvfa[:, :], 0, [CT, SEQ], "p (c t) -> p c t", c=CT)
        fa = view(cvfa[:, :], CT * SEQ, [2, TT, 2 * P], "p (a t c) -> p a t c", a=2, t=TT)
        cvx = view(glu_a[:, :, :, :], 0, [CT, SEQ], "p (c t) -> p c t", c=CT)
        ys = view(glu_s[:, :, :, :], 0, [TT, SSM_INNER], "p (t c) -> p t c", t=TT)
        ysq = view(dg[:, :, :], 0, [SSM_INNER], "p c -> p c")
        fu = ybr[:, 0:CT, :]
        z = view(ybr[:, :, :], 2 * CT * SEQ, [TT, SSM_INNER], "p (t c) -> p t c", t=TT)
        xs = view(ybr[:, :, :], 3 * CT * SEQ, [TT, SSM_INNER], "p (t c) -> p t c", t=TT)
        bias = [view(b, 0, [TT, GK], "p (t k) -> p t k", t=TT) for b in (mix[:, :, :], cvfa[:, :])]
        qkp = view(sc[:, :, :, :], 0, [2, ATT_GROUPS, SEQ], "p (w g t) -> p w g t", w=2, g=ATT_GROUPS)
        sa = view(ex[:, :, :, :], 0, [2, GK], "p (u k) -> p u k", u=2)
        pt = view(mm_[:, :, :, :], 0, [2, GK], "p (u k) -> p u k", u=2)
        ao = view(xbc[:, :, :], 0, [TT, ATT_WIDTH], "p (t c) -> p t c", t=TT)
        hs, hid = gs, gt
        at_qk = 0

        def over_qk(shape, pattern, **sizes):
            nonlocal at_qk
            lo = at_qk
            at_qk += int(np.prod(shape))
            assert at_qk <= 2 * ATT_GROUPS * HP * SEQ
            return view(qk[:, :, :, :], lo, shape, pattern, **sizes)

        xg = over_qk([1, KT, P], "p (o k t) -> p o k t", o=1, k=KT)
        yx = over_qk([D_MODEL], "p c -> p c")
        gat = over_qk([1, TT, P], "p (o t s) -> p o t s", o=1, t=TT)
        gatw = over_qk([1, TT, P], "p (o t s) -> p o t s", o=1, t=TT)
        sca = over_qk([SEQ], "p c -> p c")
        lg = over_qk([TT, N_EXPERTS], "p (t e) -> p t e", t=TT)
        top = over_qk([TT, 8], "p (t e) -> p t e", t=TT)
        topf = over_qk([TT, 8], "p (t e) -> p t e", t=TT)
        rt = over_qk([TT, 8], "p (t e) -> p t e", t=TT)
        oh = over_qk([TT, 2, N_EXPERTS], "p (t c e) -> p t c e", t=TT, c=2)
        comb = over_qk([TT, N_EXPERTS], "p (t e) -> p t e", t=TT)
        msk = over_qk([TT, N_EXPERTS], "p (t e) -> p t e", t=TT)
        pos = over_qk([TT, N_EXPERTS], "p (t e) -> p t e", t=TT)
        topi = sb("topi", [P, TT, 8], U32)
        cnt = sb("cnt", [P, 4])
        rounds = sb("rounds", [P, 1], I32)

        n_oh = ATT_GROUPS * 2 * SEQ
        ybr_flat = ybr[:, :, :].rearrange("p c t -> p (c t)")
        onehot_sb = ybr_flat[0:REL_BUCKETS + 1, 0:n_oh].rearrange("p (g c) -> p g c", g=ATT_GROUPS)
        relb_sb = ybr_flat[0:REL_BUCKETS + 1, n_oh:n_oh + ATT_GROUPS * ATT_HEADS]
        rows_sb = ybr_flat[0:ATT_HEADS, 2048:2048 + n_oh].rearrange("p (g c) -> p g c", g=ATT_GROUPS)

        ps = ctx.enter_context(nc.psum_tensor("ps", [P, 8 * 512], F32))

        def bank(b, lo=0, n=512):
            return ps[:, 512 * b + lo:512 * b + lo + n]

        def par(name, i=0, n=1):
            return pk[:, AT[name] + i:AT[name] + i + n]

        def con(name, i=0, n=P):
            return cst[:, CAT[name] + i:CAT[name] + i + n]

        s_loaded = [sem(f"ring_loaded{i}") for i in range(RING)]
        s_cst = sem("constants_loaded")
        s_x = sem("x_loaded")
        s_zero = sem("pads_zeroed")
        s_relT = sem("bias_rows_product")
        s_relL = sem("bias_inputs_loaded")
        s_relC = sem("bias_rows_copied")
        s_relW = sem("bias_rows_written")
        s_pk = sem("params_loaded")
        s_h = sem("h_ready")
        s_sq = sem("squares_ready")
        s_ms = sem("mean_square_ready")
        s_var = sem("variance_ready")
        s_sd = sem("deviation_ready")
        s_rs = sem("rstd_ready")
        s_xn = sem("xn_ready")
        s_pj = sem("proj_tile_ready")
        s_pf = sem("proj_tile_copied")
        s_glu = sem("glu_ready")
        s_cvw = sem("conv_chain")
        s_xc = sem("ssm_conv_chain")
        s_xa = sem("ssm_conv_active")
        s_dtc = sem("dt_chain")
        s_dta = sem("dt_exp")
        s_lns = sem("ln_sum_ready")
        s_lnc = sem("ln_chain")
        s_lna = sem("ln_act")
        s_f1 = sem("fnet_channels_ready")
        s_f1c = sem("fnet_channels_copied")
        s_f2 = sem("fnet_tokens_ready")
        s_f2c = sem("fnet_tokens_copied")
        s_xt = sem("x_transposed")
        s_xtc = sem("x_transposed_copied")
        s_bc = sem("bc_scores_ready")
        s_sc = sem("bc_scores_masked")
        s_ua = sem("dta_rows_ready")
        s_r = sem("cumsum_ready")
        s_hc = sem("ssm_head_chain")
        s_ex = sem("decay_ready")
        s_mm = sem("ssm_mix_ready")
        s_y = sem("ssm_y_ready")
        s_yh = sem("ssm_head_y_done")
        s_yc = sem("ssm_y_chain")
        s_ya = sem("ssm_sd_ready")
        s_yt = sem("ssm_y_transposed")
        s_ybs = sem("ssm_branch_ready")
        s_bia = [sem(f"bias_loaded{i}") for i in range(2)]
        s_qkp = sem("head_pair_staged")
        s_s = sem("scores_ready")
        s_sb = sem("scores_biased")
        s_mx = sem("max_ready")
        s_am = sem("neg_max_ready")
        s_e = sem("probs_ready")
        s_t = sem("probs_transposed")
        s_tc = sem("probs_transposed_copied")
        s_o = sem("attn_out_ready")
        s_dn = sem("denominator_inverted")
        s_oc = sem("attn_out_scaled")
        s_ot = sem("attn_out_transposed")
        s_yba = sem("attn_branch_ready")
        s_br = sem("branch_tile_ready")
        s_sg = sem("gate_ready")
        s_bt = sem("gated_tile")
        s_bm = sem("mix_tile_ready")
        s_wo = sem("w_out_tile_ready")
        s_du = sem("dense_up_ready")
        s_ds = sem("dense_silu_ready")
        s_dh = sem("dense_hidden_ready")
        s_dr = sem("dense_hidden_read")
        s_rl = sem("router_ready")
        s_rc = sem("router_chain")
        s_re = sem("router_exp_ready")
        s_rp = sem("positions_ready")
        s_rr = sem("rounds_ready")
        s_xq = sem("xn_token_major_ready")
        s_xqc = sem("xn_token_major_copied")
        s_g = sem("gather_ready")
        s_gw = sem("gather_weighted")
        s_xg = sem("tokens_gathered")
        s_xgc = sem("tokens_gathered_copied")
        s_eu = sem("expert_up_ready")
        s_es = sem("expert_silu_ready")
        s_eh = sem("expert_hidden_ready")
        s_er = sem("expert_hidden_read")
        s_edc = sem("expert_down_copied")
        s_st = sem("scatter_transposed")
        s_stc = sem("scatter_copied")
        s_eo = sem("expert_out_tile")
        s_ea = sem("expert_out_added")
        s_pos = sem("places_shifted")
        s_pl = sem("ple_tile_ready")
        s_pg = sem("ple_gate_ready")
        s_pt = sem("ple_term_ready")
        s_out = sem("out_written")
        s_step = sem("pool_step")

        def wait_block(eng, r, j):
            eng.wait_ge(s_loaded[j % RING], (r + (j // RING + 1)) * 16)

        def load_block(eng, j, src, used=None):
            if used is not None:
                eng.wait_ge(*used)
            eng.dma_start(ring[:, j % RING, :], src).then_inc(s_loaded[j % RING], 16)

        def skip_block(eng, j, used):
            if used is not None:
                eng.wait_ge(*used)
            eng.sem_inc(s_loaded[j % RING], 16)

        def mixer_used(l, j):
            if j < PROJ_BLOCKS:
                return s_pj, l * N_PROJ + (2 * j + 2 + (1 if j >= 9 else 0))
            if j < PROJ_BLOCKS + N_BRANCHES * BRANCH_BLOCKS:
                b, k = divmod(j - PROJ_BLOCKS, BRANCH_BLOCKS)
                return s_br, l * (N_BRANCHES * KT) + (b * KT + (2, 4, 4, 6, 8, 8)[k])
            return s_wo, l * KT + 2 * (j + 5 - MIX_BLOCKS)

        def dense_used(c, k):
            return (s_dr, c * 2 + 4) if k == 2 else (s_du, c * 2 + 2)

        def expert_used(c, k):
            return (s_er, c * 2 + 4) if k == 2 else (s_eu, c * 2 + 2)

        def ple_used(l, j):
            return s_pl, l * KT + (KT + (KT if j == PLE_BLOCKS - 1 else 2 * j + 2))

        def tile_w(j, half):
            return [ring[:, j % RING, k * COLS + half * P:k * COLS + half * P + P] for k in range(KT)]

        block = ctx.enter_context(nc.Block())

        @block.sync
        def _(sp):
            sp.dma_start(h[:, :, :], x).then_inc(s_x, 16)
            sp.dma_start(cst[:, :], cst_in).then_inc(s_cst, 16)

            def load_ple(l, used):
                for j in range(PLE_BLOCKS):
                    load_block(sp, j, wp[l, j], used(j))
                for j in range(PLE_BLOCKS, RING):
                    skip_block(sp, j, used(j))

            with sp.Fori(0, DEPTH) as l:
                for j in range(MIX_BLOCKS):
                    if j < PLE_BLOCKS:
                        used = ple_used(l - 1, j)
                    else:
                        used = mixer_used(l, j - RING) if j >= RING else None
                    load_block(sp, j, wm[l, j], used)
                for j in range(MIX_BLOCKS, MIX_ROUNDS * RING):
                    skip_block(sp, j, mixer_used(l, j - RING))

                def first_used(j):
                    at = MIX_ROUNDS * RING - RING + j
                    return mixer_used(l, at) if at < MIX_BLOCKS else None

                with sp.If(l < 1):
                    for j in range(RING):
                        load_block(sp, j, wd[j], first_used(j))
                    with sp.Fori(1, DENSE_CHUNKS // 2) as i:
                        for j in range(RING):
                            load_block(sp, j, wd[i * RING + j], dense_used(i * 2 + (j // 3 - 2), j % 3))
                    for j in range(3):
                        load_block(sp, j, wd[DENSE_CHUNKS // 2 * RING + j], dense_used(DENSE_CHUNKS - 3, j % 3))
                    for j in range(3, RING):
                        skip_block(sp, j, dense_used(DENSE_CHUNKS - 2, j % 3))
                    load_ple(0, lambda j: dense_used(DENSE_CHUNKS - 1, j % 3) if j < 3 else None)
                with sp.Else():
                    for j in range(RING):
                        load_block(sp, j, we[j], first_used(j))
                    with sp.Fori(1, N_EXPERTS * PASS_ROUNDS) as i:
                        for j in range(RING):
                            load_block(sp, j, we[i * RING + j], expert_used(i * 2 + (j // 3 - 2), j % 3))
                    sp.wait_ge(s_rr, 1)
                    n = sp.value_load(rounds[0:1, 0:1], min_val=1, max_val=2)
                    with sp.If(n > 1):
                        with sp.Fori(0, N_EXPERTS * PASS_ROUNDS) as i:
                            for j in range(RING):
                                load_block(sp, j, we[i * RING + j],
                                           expert_used(i * 2 + (N_EXPERTS * EXP_CHUNKS + j // 3 - 2), j % 3))
                        load_ple(1, lambda j: expert_used(2 * N_EXPERTS * EXP_CHUNKS + j // 3 - 2, j % 3))
                    with sp.Else():
                        load_ple(1, lambda j: expert_used(N_EXPERTS * EXP_CHUNKS + j // 3 - 2, j % 3))
            sp.wait_ge(s_xn, KT * (2 * DEPTH + 1))
            sp.dma_start(out, xn[:, :, :]).then_inc(s_out, 16)
            sp.wait_ge(s_out, 16)

        @block.tensor
        def _(pe):
            def chain(dst, lhs, rhs):
                for k, (a, b) in enumerate(zip(lhs, rhs)):
                    m = pe.matmul(dst, a, b, start=k == 0, stop=k == len(lhs) - 1)
                return m

            def norm_sum(k):
                pe.wait_ge(s_sq, k * 2 + 1)
                for j in range(KT):
                    if j == KT // 2:
                        pe.wait_ge(s_sq, k * 2 + 2)
                    m = pe.matmul(bank(7, 0, SEQ), con("ones"), mix[:, j, :], start=j == 0, stop=j == KT - 1)
                m.then_inc(s_ms, 1)

            def project(l):
                r = l * LAYER0_ROUNDS
                base = l * N_PROJ

                def room(t):
                    if t >= 4:
                        pe.wait_ge(s_pf, base + (t - 3))

                def feature_major(j, t, rr=None, bb=None):
                    wait_block(pe, r if rr is None else rr, j)
                    for half in range(2):
                        if bb is None:
                            room(t + half)
                        else:
                            pe.wait_ge(s_pf, bb + (t + half - 3))
                        m = chain(bank((t + half) % 4, 0, SEQ), tile_w(j, half), [xn[:, k, :] for k in range(KT)])
                        m.then_inc(s_pj, 1)

                def token_major(j, t):
                    wait_block(pe, r, j)
                    for tt in range(TT):
                        room(t + tt)
                        m = chain(bank((t + tt) % 4, 0, COLS), [xn[:, k, tt * P:tt * P + P] for k in range(KT)],
                                  [ring[:, j % RING, k * COLS:(k + 1) * COLS] for k in range(KT)])
                        m.then_inc(s_pj, 1)

                pe.wait_ge(s_xn, l * (2 * KT) + KT)
                t = 0
                for j in range(7):
                    feature_major(j, t)
                    t += 2
                for j in range(7, 9):
                    token_major(j, t)
                    t += 2
                room(t)
                for tt in range(TT):
                    m = chain(bank(t % 4, tt * DT, DT), [xn[:, k, tt * P:tt * P + P] for k in range(KT)],
                              [par("w_dt", k * DT, DT) for k in range(KT)])
                m.then_inc(s_pj, 1)
                t += 1
                for j in range(9, 11):
                    feature_major(j, t)
                    t += 2
                assert t == T_Q
                with pe.Fori(0, 2) as i:
                    for jj in range(6):
                        feature_major(11 + jj, t + 2 * jj, r + i, base + i * 12)
                t += 24
                for jj in range(6):
                    token_major(23 + jj, t)
                    t += 2
                assert t == N_PROJ

            def fnet(l):
                pe.wait_ge(s_pf, l * N_PROJ + N_PROJ)
                for g in range(FNET_GROUPS):
                    if g >= 2:
                        pe.wait_ge(s_f1c, l * FNET_GROUPS + (g - 1))
                    for tt in range(TT):
                        m = pe.matmul(bank(4 + g % 2, tt * 2 * P, 2 * P), fu[:, g, tt * P:tt * P + P],
                                      con("dft_ch", 0, 2 * P), start=True, stop=True)
                    m.then_inc(s_f1, 1)
                    if g >= 1:
                        fnet_tokens(l, g - 1)
                fnet_tokens(l, FNET_GROUPS - 1)

            def fnet_tokens(l, g):
                pe.wait_ge(s_f1c, l * FNET_GROUPS + (g + 1))
                if g >= 2:
                    pe.wait_ge(s_f2c, l * FNET_GROUPS + (g - 1))
                lhs = [fa[:, g % 2, tt, part * P:part * P + P] for part in range(2) for tt in range(TT)]
                rhs = [con(name, tt * SEQ, SEQ) for name in ("dft_cos", "dft_sin") for tt in range(TT)]
                chain(bank(6 if g % 2 == 0 else 3, 0, SEQ), lhs, rhs).then_inc(s_f2, 1)

            def conv_norm(l):
                pe.wait_ge(s_cvw, l * (CT * CONV_K) + CT * CONV_K)
                chain(bank(7, 0, SEQ), [con("ones")] * CT, [cv[:, t, :] for t in range(CT)]).then_inc(s_lns, 1)
                pe.wait_ge(s_lnc, l * 5 + 2)
                chain(bank(7, SEQ, SEQ), [con("ones")] * CT, [cv[:, t, :] for t in range(CT)]).then_inc(s_lns, 1)

            def ssm_prep(l):
                pe.wait_ge(s_xa, l * XT + XT)
                pe.wait_ge(s_f1c, l * FNET_GROUPS + FNET_GROUPS)
                for tt in range(TT):
                    for c in range(CT):
                        m = pe.transpose(bank(4 + tt, c * P, P), xbc[:, c, tt * P:tt * P + P], con("ident"))
                    m.then_inc(s_xt, 1)
                pe.wait_ge(s_f2c, l * FNET_GROUPS + FNET_GROUPS)
                for g in range(SSM_GROUPS):
                    if g == 1:
                        pe.wait_ge(s_lnc, l * 5 + 3)
                    lo = g * SSM_STATE
                    for tt in range(TT):
                        m = pe.matmul(bank(6 + g, tt * SEQ, SEQ), xbc[lo:lo + SSM_STATE, CT, tt * P:tt * P + P],
                                      xbc[lo:lo + SSM_STATE, CT + 1, :], start=True, stop=True)
                    m.then_inc(s_bc, 1)

            def ssm_heads(l):
                with pe.Fori(0, SSM_HEADS // SSM_GROUPS) as hh:
                    pe.wait_ge(s_pf, l * N_PROJ + N_PROJ)
                    pe.wait_ge(s_sc, l * 2 + 2)
                    n = l * SSM_HEADS + hh * 2
                    for g in range(SSM_GROUPS):
                        pe.wait_ge(s_ua, n + (g + 1))
                        for part in range(4):
                            m = pe.matmul(bank(g, part * P, P), con("ones"), ua[:, g, part, :], start=True, stop=True)
                        m.then_inc(s_r, 1)
                    for g in range(SSM_GROUPS):
                        pe.wait_ge(s_mm, n + (g + 1))
                        for tt, parts in enumerate((((0, 0), (3, 0), (4, 1)), ((1, 0), (2, 1), (5, 1)))):
                            m = chain(bank(2 + g, tt * 64, 64), [mm_[:, g, b, :] for b, _ in parts],
                                      [xs[:, s, bass.ds(hh * 64 + g * 256, 64)] for _, s in parts])
                        m.then_inc(s_y, 1)

            def ssm_out(l):
                pe.wait_ge(s_yc, l * SSM_YC + SSM_YC)
                pe.wait_ge(s_xtc, l * TT + TT)
                for c in range(CT):
                    for tt in range(TT):
                        m = pe.transpose(bank(4 + c // 2, (c % 2) * SEQ + tt * P, P), ys[:, tt, c * P:c * P + P],
                                         con("ident"))
                m.then_inc(s_yt, 1)

            def attention(l):
                with pe.Fori(0, HP) as i:
                    pe.wait_ge(s_ybs, l + 1)
                    pe.wait_ge(s_sc, l * 2 + 2)
                    pe.wait_ge(s_yc, l * SSM_YC + 1)
                    n = l * UNITS + i * 4
                    pe.wait_ge(s_qkp, l * (2 * HP) + (i * 2 + 2))

                    def scores(u):
                        lo = 64 * (u // TT)
                        if u >= 2:
                            pe.wait_ge(s_sb, n + (u - 1))
                        for g in range(ATT_GROUPS):
                            m = pe.matmul(bank(4 + 2 * (u % 2), g * SEQ, SEQ),
                                          qkp[lo:lo + 64, 0, g, (u % TT) * P:(u % TT) * P + P],
                                          qkp[lo:lo + 64, 1, g, :], start=True, stop=True)
                        m.then_inc(s_s, 1)

                    def transposes(u):
                        pe.wait_ge(s_e, n + (u + 1))
                        for b in range(2 * ATT_GROUPS):
                            m = pe.transpose(bank(2 * (u % 2), b * P, P), sa[:, u % 2, b * P:b * P + P], con("ident"))
                        m.then_inc(s_t, 1)

                    def values(u):
                        pe.wait_ge(s_tc, n + (u + 1))
                        chain(bank(2 * (u % 2), GK, 64), [pt[:, u % 2, b * P:b * P + P] for b in range(6)],
                              [v[:, b % 2, bass.ds(i * P + (b // 2 * ATT_WIDTH + 64 * (u // TT)), 64)]
                               for b in range(6)]).then_inc(s_o, 1)

                    scores(0)
                    scores(1)
                    transposes(0)
                    scores(2)
                    transposes(1)
                    values(0)
                    scores(3)
                    values(1)
                    transposes(2)
                    transposes(3)
                    pe.wait_ge(s_oc, n + 1)
                    values(2)
                    pe.wait_ge(s_oc, n + 2)
                    values(3)
                pe.wait_ge(s_oc, l * UNITS + UNITS)
                for c in range(CT):
                    for tt in range(TT):
                        m = pe.transpose(bank(4 + c // 2, (c % 2) * SEQ + tt * P, P), ao[:, tt, c * P:c * P + P],
                                         con("ident"))
                m.then_inc(s_ot, 1)

            def branches(l):
                with pe.Fori(0, N_BRANCHES) as b:
                    pe.wait_ge(s_lna, l * (CT + 1) + (CT + 1))
                    pe.wait_ge(s_yba, l + 1)
                    r = l * LAYER0_ROUNDS + b
                    n = l * (N_BRANCHES * KT) + b * KT
                    for m_ in range(KT):
                        out_j = PROJ_BLOCKS + 3 * (m_ // 4) + 1
                        j = out_j + (1 if m_ % 4 >= 2 else -1)
                        if m_ % 2 == 0:
                            wait_block(pe, r, j)
                        if m_ % 4 == 0:
                            wait_block(pe, r, out_j)
                        pe.wait_ge(s_bm, n + (m_ + 1))
                        col = (m_ % 4) * P
                        m = chain(bank(2 * (m_ % 2), 0, SEQ),
                                  [ring[:, out_j % RING, c * 512 + col:c * 512 + col + P] for c in range(CT)],
                                  [ybr[:, b * CT + c, :] for c in range(CT)])
                        m = chain(bank(2 * (m_ % 2) + 1, 0, SEQ), tile_w(j, m_ % 2), [xn[:, k, :] for k in range(KT)])
                        m.then_inc(s_br, 1)

            def mix_out(l):
                n = l * (N_BRANCHES * KT)
                pe.wait_ge(s_bm, n + (N_BRANCHES * KT + 2))
                r = l * LAYER0_ROUNDS
                for jj in range(4):
                    j = MIX_BLOCKS - 4 + jj
                    wait_block(pe, r, j)
                    for half in range(2):
                        m_ = 2 * jj + half
                        m = chain(bank(m_, 0, SEQ), tile_w(j, half), [mix[:, k, :] for k in range(KT)])
                        m.then_inc(s_wo, 1)

            def dense():
                pe.wait_ge(s_xn, 2 * KT)

                def one(r, j, n, first, last):
                    wait_block(pe, r, j)
                    wait_block(pe, r, j + 1)
                    for half in range(2):
                        if half == 0:
                            pe.wait_ge(s_dh, n + 1)
                        else:
                            pe.wait_ge(s_dh, n + 2)
                        chain(bank(2 * half, 0, SEQ), tile_w(j, half), [xn[:, k, :] for k in range(KT)])
                        m = chain(bank(2 * half + 1, 0, SEQ), tile_w(j + 1, half), [xn[:, k, :] for k in range(KT)])
                        m.then_inc(s_du, 1)
                    wait_block(pe, r, j + 2)
                    for half in range(2):
                        pe.wait_ge(s_dh, n + (half + 3))
                        for m_ in range(KT):
                            m = pe.matmul(bank(4 + m_ // 2, (m_ % 2) * SEQ, SEQ),
                                          ring[:, (j + 2) % RING, half * D_MODEL + m_ * P:half * D_MODEL + m_ * P + P],
                                          hid[:, half, :], start=first and half == 0 and m_ % 2 == 0,
                                          stop=last and half == 1, skip_group_check=True)
                        m.then_inc(s_dr, 1)
                    return m

                one(MIX_ROUNDS, 0, 0, True, False)
                one(MIX_ROUNDS, 3, 2, False, False)
                with pe.Fori(1, DENSE_CHUNKS // 2) as i:
                    for c in range(2):
                        one(i + MIX_ROUNDS, 3 * c, i * 4 + 2 * c, False, False)
                one(MIX_ROUNDS + DENSE_CHUNKS // 2, 0, 2 * (DENSE_CHUNKS - 1), False, True)

            def route():
                pe.wait_ge(s_xn, 4 * KT)
                for tt in range(TT):
                    m = chain(bank(4, tt * N_EXPERTS, N_EXPERTS), [xn[:, k, tt * P:tt * P + P] for k in range(KT)],
                              [par("router", k * N_EXPERTS, N_EXPERTS) for k in range(KT)])
                m.then_inc(s_rl, 1)
                for tt in range(TT):
                    for k in range(KT):
                        m = pe.transpose(bank(2 * tt + k // 4, (k % 4) * P, P), xn[:, k, tt * P:tt * P + P], con("ident"))
                        if k % 4 == 3:
                            m.then_inc(s_xq, 1)
                pe.wait_ge(s_rc, RC_MASK)
                chain(bank(5, 0, N_EXPERTS), [con("before")], [msk[:, 0, :]])
                chain(bank(5, N_EXPERTS, N_EXPERTS), [con("ones"), con("before")], [msk[:, 0, :], msk[:, 1, :]])
                chain(bank(5, 2 * N_EXPERTS, N_EXPERTS), [con("ones")] * 2,
                      [msk[:, 0, :], msk[:, 1, :]]).then_inc(s_rp, 1)
                pe.wait_ge(s_xqc, 4)

            def experts(passes):
                pe.wait_ge(s_rr, 1)
                n_r = pe.value_load(rounds[0:1, 0:1], min_val=1, max_val=2)
                pe.reg_mov(passes, n_r * N_EXPERTS)
                with pe.Fori(0, n_r) as o:
                    with pe.Fori(0, N_EXPERTS) as e:
                        q = o * N_EXPERTS + e
                        pe.wait_ge(s_gw, q + 1)
                        pe.wait_ge(s_ea, q * KT + 2)
                        for k in range(KT):
                            m = chain(bank(6 + k // 4, (k % 4) * P, P), [mix[:, tt * 4 + k // 2, (k % 2) * P:(k % 2) * P + P]
                                                                        for tt in range(TT)],
                                      [gat[:, 0, tt, :] for tt in range(TT)])
                            if k % 4 == 3:
                                m.then_inc(s_xg, 1)
                        pe.wait_ge(s_xgc, q * 2 + 2)
                        for tt in range(TT):
                            m = pe.transpose(bank(6, tt * P, P), gatw[:, 0, tt, :], con("ident"))
                        m.then_inc(s_st, 1)

                        def one(r, j, n, first, last):
                            wait_block(pe, r, j)
                            wait_block(pe, r, j + 1)
                            for half in range(2):
                                pe.wait_ge(s_eh, n + (half + 1))
                                chain(bank(2 * half, 0, P), tile_w(j, half), [xg[:, 0, k, :] for k in range(KT)])
                                m = chain(bank(2 * half + 1, 0, P), tile_w(j + 1, half),
                                          [xg[:, 0, k, :] for k in range(KT)])
                                m.then_inc(s_eu, 1)
                            wait_block(pe, r, j + 2)
                            for half in range(2):
                                pe.wait_ge(s_eh, n + (half + 3))
                                for c in range(2):
                                    col = half * D_MODEL + c * 512
                                    m = pe.matmul(bank(4 + c), hid[:, half, 0:P],
                                                  ring[:, (j + 2) % RING, col:col + 512],
                                                  start=first and half == 0, stop=last and half == 1,
                                                  skip_group_check=True)
                                m.then_inc(s_er, 1)

                        r = q * PASS_ROUNDS + (LAYER0_ROUNDS + MIX_ROUNDS)
                        n = q * (2 * EXP_CHUNKS)
                        pe.wait_ge(s_edc, q + 1)
                        one(r, 0, n, True, False)
                        one(r, 3, n + 2, False, False)
                        with pe.Fori(1, PASS_ROUNDS - 1) as i:
                            for c in range(2):
                                one(r + i, 3 * c, n + (i * 4 + 2 * c), False, False)
                        one(r + (PASS_ROUNDS - 1), 0, n + (2 * EXP_CHUNKS - 4), False, False)
                        one(r + (PASS_ROUNDS - 1), 3, n + (2 * EXP_CHUNKS - 2), False, True)
                        pe.wait_ge(s_edc, q + 2)
                        pe.wait_ge(s_stc, q + 1)
                        for m_ in range(KT):
                            pe.wait_ge(s_ea, q * KT + (m_ + 1))
                            pe.matmul(bank(6 + m_ % 2, 0, SEQ), yx[:, m_ * P:m_ * P + P], sca[:, :],
                                      start=True, stop=True).then_inc(s_eo, 1)

            def ple(l, passes):
                pe.wait_ge(s_h, l * 3 + 3)
                r = l * (LAYER0_ROUNDS - DENSE_ROUNDS) + pe.snap(passes, min_val=0, max_val=16) * PASS_ROUNDS \
                    + (MIX_ROUNDS + DENSE_ROUNDS)
                wait_block(pe, r, 4)
                for m_ in range(KT):
                    if m_ % 2 == 0:
                        wait_block(pe, r, m_ // 2)
                    if m_ >= 2:
                        pe.wait_ge(s_pt, l * KT + (m_ - 1))
                    chain(bank(2 * (m_ % 2), 0, SEQ), [ring[:, 4, c * D_MODEL + m_ * P:c * D_MODEL + m_ * P + P]
                                                      for c in range(PLE_DIM // P)],
                          [par("p", c * SEQ, SEQ) for c in range(PLE_DIM // P)])
                    m = chain(bank(2 * (m_ % 2) + 1, 0, SEQ), tile_w(m_ // 2, m_ % 2), [h[:, k, :] for k in range(KT)])
                    m.then_inc(s_pl, 1)

            pe.sem_inc(s_pl, KT)
            pe.sem_inc(s_dr, 2)
            pe.sem_inc(s_er, 2)
            pe.sem_inc(s_r, 2)
            pe.sem_inc(s_s, 1)
            passes = pe.alloc_register("passes_pe")
            pe.wait_ge(s_relL, 32)
            for g in range(ATT_GROUPS):
                m = pe.matmul(ps[0:ATT_HEADS, g * 512:g * 512 + 512],
                              relb_sb[:, g * ATT_HEADS:(g + 1) * ATT_HEADS],
                              onehot_sb[:, g, :], start=True, stop=True)
            m.then_inc(s_relT, 1)
            pe.wait_ge(s_cst, 16)
            with pe.Fori(0, DEPTH) as l:
                norm_sum(l * 2)
                pe.wait_ge(s_pk, l * 16 + 16)
                project(l)
                fnet(l)
                conv_norm(l)
                ssm_prep(l)
                ssm_heads(l)
                ssm_out(l)
                attention(l)
                branches(l)
                mix_out(l)
                pe.wait_ge(s_h, l * 3 + 2)
                norm_sum(l * 2 + 1)
                pe.reg_mov(passes, 0)
                with pe.If(l < 1):
                    dense()
                with pe.Else():
                    route()
                    experts(passes)
                ple(l, passes)
            norm_sum(2 * DEPTH)

        @block.scalar
        def _(act):
            def norm_squares(k, ready):
                act.wait_ge(s_h, ready)
                for half in range(2):
                    sl = slice(half * KT // 2, (half + 1) * KT // 2)
                    act.activation(mix[:, sl, :], h[:, sl, :], ACT.Square).then_inc(s_sq, 1)
                act.wait_ge(s_var, k + 1)
                act.activation(rms_t[:, 1, :], rms_t[:, 0, :], ACT.Sqrt).then_inc(s_sd, 1)

            def project(l):
                base = l * N_PROJ

                def tile(t, dst, func=ACT.Copy, rows=(0, SEQ)):
                    act.wait_ge(s_pj, base + (t + 1))
                    act.activation(dst, bank(t % 4, *rows), func).then_inc(s_pf, 1)

                for pair in range(2):
                    for c in range(2):
                        tile(4 * pair + c, glu_a[:, pair, c, :])
                    for c in range(2):
                        tile(4 * pair + 2 + c, glu_s[:, pair, c, :], ACT.Sigmoid)
                for c in range(XT):
                    tile(T_XBC + c, xbcp[:, c, SPAD:SPAD + SEQ])
                for j in range(2):
                    for tt in range(TT):
                        tile(T_Z + 2 * j + tt, z[:, tt, j * COLS:(j + 1) * COLS], ACT.Silu)
                tile(T_DT, dts[:, 0, :], rows=(0, TT * DT))
                for g in range(FNET_GROUPS):
                    tile(T_FN + g, fu[:, g, :])
                dt_exps(l)
                ssm(l)
                with act.Fori(0, 2) as i:
                    for t in range(12):
                        act.wait_ge(s_pj, base + i * 12 + (T_Q + t + 1))
                        act.activation(qk[:, bass.ds(i * ATT_GROUPS + t // HP, 1), t % HP, :], bank((T_Q + t) % 4, 0, SEQ), ACT.Copy).then_inc(s_pf, 1)
                for j in range(6):
                    for tt in range(TT):
                        tile(T_V + 2 * j + tt, v[:, tt, j * COLS:(j + 1) * COLS])

            def dt_exps(l):
                act.wait_ge(s_dtc, l * DTC + 3)
                act.activation(dts[:, 3, :], dts[:, 2, :], ACT.Exp).then_inc(s_dta, 1)
                act.activation(a_neg[:, :], par("a_log", 0, DT), ACT.Exp).then_inc(s_dta, 1)

            def fnet(l):
                for g in range(FNET_GROUPS):
                    act.wait_ge(s_f1, l * FNET_GROUPS + (g + 1))
                    if g >= 2:
                        act.wait_ge(s_f2, l * FNET_GROUPS + (g - 1))
                    act.activation(fa[:, g % 2, :, :], bank(4 + g % 2).rearrange("p (t c) -> p t c", t=TT),
                                   ACT.Copy).then_inc(s_f1c, 1)
                    if g >= 1:
                        fnet_tokens(l, g - 1)
                fnet_tokens(l, FNET_GROUPS - 1)

            def fnet_tokens(l, g):
                act.wait_ge(s_f2, l * FNET_GROUPS + (g + 1))
                act.activation(ybr[:, FNET * CT + g, :], bank(6 if g % 2 == 0 else 3, 0, SEQ),
                               ACT.Copy).then_inc(s_f2c, 1)

            def ssm(l):
                for c in range(XT):
                    act.wait_ge(s_xc, l * (XT * SSM_CONV) + (c + 1) * SSM_CONV)
                    act.activation(xbc[:, c, :], xbc[:, c, :], ACT.Silu).then_inc(s_xa, 1)

            def conv_norm(l):
                act.wait_ge(s_lnc, l * 5 + 3)
                act.activation(rms_t[:, 1, :], rms_t[:, 0, :], ACT.Sqrt).then_inc(s_lna, 1)
                act.wait_ge(s_lnc, l * 5 + 5)
                for c in range(CT):
                    act.activation(ybr[:, CONV * CT + c, :], cvx[:, c, :], ACT.Silu, bias=par("ln_b", c),
                                   scale=par("ln_g", c)).then_inc(s_lna, 1)

            def ssm_heads(l):
                for tt in range(TT):
                    act.wait_ge(s_xt, l * TT + (tt + 1))
                    act.activation(xs[:, tt, :], bank(4 + tt), ACT.Copy).then_inc(s_xtc, 1)
                with act.Fori(0, SSM_HEADS // SSM_GROUPS) as hh:
                    n = l * SSM_HEADS + hh * 2
                    for g in range(SSM_GROUPS):
                        act.wait_ge(s_hc, (n + g) * SSM_HC + SSM_HC)
                        act.activation(ex[:, g, :, :], ex[:, g, :, :], ACT.Exp).then_inc(s_ex, 1)
                act.wait_ge(s_yc, l * SSM_YC + 4)
                act.activation(yst[:, 4:6], yst[:, 2:4], ACT.Sqrt).then_inc(s_ya, 1)
                act.wait_ge(s_yt, l + 1)
                for c in range(CT):
                    m = act.activation(ybr[:, SSM * CT + c, :], bank(4 + c // 2, (c % 2) * SEQ, SEQ), ACT.Copy,
                                       scale=par("ssm_norm", c))
                m.then_inc(s_ybs, 1)

            def attention(l):
                with act.Fori(0, HP) as i:
                    n = l * UNITS + i * 4

                    def probs(u):
                        act.wait_ge(s_am, n + (u + 1))
                        act.activation(sa[:, u % 2, :], sa[:, u % 2, :], ACT.Exp, bias=ast[:, u % 2, 0:1],
                                       accum_out=ast[:, u % 2, 1:2]).then_inc(s_e, 1)

                    def copy_t(u):
                        act.wait_ge(s_t, n + (u + 1))
                        act.activation(pt[:, u % 2, :], bank(2 * (u % 2), 0, GK), ACT.Copy).then_inc(s_tc, 1)

                    probs(0)
                    probs(1)
                    copy_t(0)
                    copy_t(1)
                    probs(2)
                    probs(3)
                    copy_t(2)
                    copy_t(3)
                act.wait_ge(s_ot, l + 1)
                for j in range(2):
                    m = act.activation(ybr[:, ATT * CT + 2 * j:ATT * CT + 2 * j + 2, ::-1],
                                       bank(4 + j).rearrange("p (c t) -> p c t", c=2), ACT.Copy)
                m.then_inc(s_yba, 1)

            def branches(l):
                with act.Fori(0, N_BRANCHES) as b:
                    n = l * (N_BRANCHES * KT) + b * KT
                    for m_ in range(KT):
                        act.wait_ge(s_br, n + (m_ + 1))
                        act.wait_ge(s_bm, n + (m_ + 1))
                        act.activation(gs[:, m_ % 2, :], bank(2 * (m_ % 2) + 1, 0, SEQ), ACT.Sigmoid,
                                       bias=pk[:, bass.ds(b * KT + (AT["b_gate"] + m_), 1)]).then_inc(s_sg, 1)

            def dense():
                def one(n, half):
                    act.wait_ge(s_du, n + (half + 1))
                    act.wait_ge(s_dh, n + (half + 1))
                    act.activation(hs[:, half, :], bank(2 * half, 0, SEQ), ACT.Silu).then_inc(s_ds, 1)

                with act.Fori(0, DENSE_CHUNKS) as i:
                    one(i * 2, 0)
                    one(i * 2, 1)

            def route():
                act.wait_ge(s_rc, RC_EXP)
                act.activation(rt[:, :, 1:2], rt[:, :, 0:1], ACT.Exp).then_inc(s_re, 1)
                for j in range(4):
                    act.wait_ge(s_xq, j + 1)
                    tt, half = j // 2, j % 2
                    act.activation(mix[:, tt * 4 + half * 2:tt * 4 + half * 2 + 2, :],
                                   bank(2 * tt + half).rearrange("p (c t) -> p c t", c=2), ACT.Copy).then_inc(s_xqc, 1)

            def experts():
                act.wait_ge(s_rr, 1)
                n_r = act.value_load(rounds[0:1, 0:1], min_val=1, max_val=2)
                with act.Fori(0, n_r) as o:
                    with act.Fori(0, N_EXPERTS) as e:
                        q = o * N_EXPERTS + e
                        for j in range(2):
                            act.wait_ge(s_xg, q * 2 + (j + 1))
                            act.activation(xg[:, 0, 4 * j:4 * j + 4, :], bank(6 + j).rearrange("p (c t) -> p c t", c=4),
                                           ACT.Copy).then_inc(s_xgc, 1)
                        act.wait_ge(s_st, q + 1)
                        act.activation(sca[:, :], bank(6, 0, SEQ), ACT.Copy).then_inc(s_stc, 1)
                        with act.Fori(0, EXP_CHUNKS) as i:
                            n = q * (2 * EXP_CHUNKS) + i * 2
                            for half in range(2):
                                act.wait_ge(s_eu, n + (half + 1))
                                act.wait_ge(s_eh, n + (half + 1))
                                act.activation(hs[:, half, 0:P], bank(2 * half, 0, P), ACT.Silu).then_inc(s_es, 1)
                        act.wait_ge(s_er, q * (2 * EXP_CHUNKS) + (2 * EXP_CHUNKS + 2))
                        act.activation(yx[:, :], ps[:, 4 * 512:6 * 512], ACT.Copy).then_inc(s_edc, 1)

            def ple(l):
                for m_ in range(KT):
                    act.wait_ge(s_pl, l * KT + (KT + m_ + 1))
                    if m_ >= 2:
                        act.wait_ge(s_pt, l * KT + (m_ - 1))
                    act.activation(gs[:, m_ % 2, :], bank(2 * (m_ % 2) + 1, 0, SEQ), ACT.Sigmoid).then_inc(s_pg, 1)

            act.sem_inc(s_edc, 1)
            act.dma_start(relb_sb, relb).then_inc(s_relL, 16)
            act.dma_start(onehot_sb, onehot).then_inc(s_relL, 16)
            act.wait_ge(s_relT, 1)
            act.activation(rows_sb, ps[0:ATT_HEADS, 0:3 * 512].rearrange("p (g c) -> p g c", g=3),
                           ACT.Copy).then_inc(s_relC, 1)
            act.wait_ge(s_relC, 1)
            act.dma_start(scratch.ap(), rows_sb).then_inc(s_relW, 16)
            with act.Fori(0, DEPTH) as l:
                act.wait_ge(s_h, l * 3 + 1)
                act.dma_start(pk[:, :], pk_in[l]).then_inc(s_pk, 16)
                norm_squares(l * 2, l * 3 + 1)
                act.wait_ge(s_pk, l * 16 + 16)
                project(l)
                fnet(l)
                conv_norm(l)
                ssm_heads(l)
                attention(l)
                branches(l)
                norm_squares(l * 2 + 1, l * 3 + 2)
                with act.If(l < 1):
                    dense()
                with act.Else():
                    route()
                    experts()
                ple(l)
            norm_squares(2 * DEPTH, 3 * DEPTH + 1)

        @block.vector
        def _(dve):
            def norm(k, gain):
                dve.wait_ge(s_ms, k + 1)
                dve.tensor_scalar(rms_t[:, 0, :], bank(7, 0, SEQ), 1.0 / D_MODEL, EPS, ALU.mult,
                                  ALU.add).then_inc(s_var, 1)
                dve.wait_ge(s_sd, k + 1)
                dve.reciprocal(rstd[:, :], rms_t[:, 1, :]).then_inc(s_rs, 1)
                dve.wait_ge(s_rs, k + 1)
                for j in range(KT):
                    dve.scalar_tensor_tensor(out=xn[:, j, :], in0=h[:, j, :], scalar=par(gain, j), in1=rstd[:, :],
                                             op0=ALU.mult, op1=ALU.mult).then_inc(s_xn, 1)

            def depthwise(dst, src, taps, w, b, tiles, s, n):
                for tap in range(taps):
                    for c in range(tiles):
                        col = par(w, tap * tiles + c)
                        if tap == 0:
                            i = dve.tensor_scalar(dst[:, c, :], src[:, c, 0:SEQ], col, par(b, c), ALU.mult, ALU.add)
                        else:
                            dve.wait_ge(s, n + ((tap - 1) * tiles + c + 1))
                            i = dve.scalar_tensor_tensor(out=dst[:, c, :], in0=src[:, c, tap:tap + SEQ], scalar=col,
                                                         in1=dst[:, c, :], op0=ALU.mult, op1=ALU.add)
                        i.then_inc(s, 1)

            def ssm_conv(l):
                n = l * (XT * SSM_CONV)
                for c in range(XT):
                    dve.wait_ge(s_pf, l * N_PROJ + (T_XBC + c + 1))
                    for tap in range(SSM_CONV):
                        col = par("ssm_w", tap * XT + c)
                        if tap == 0:
                            i = dve.tensor_scalar(xbc[:, c, :], xbcp[:, c, 0:SEQ], col, par("ssm_b", c), ALU.mult, ALU.add)
                        else:
                            dve.wait_ge(s_xc, n + (c * SSM_CONV + tap))
                            i = dve.scalar_tensor_tensor(out=xbc[:, c, :], in0=xbcp[:, c, tap:tap + SEQ], scalar=col,
                                                         in1=xbc[:, c, :], op0=ALU.mult, op1=ALU.add)
                        i.then_inc(s_xc, 1)

            def time_steps(l):
                dve.wait_ge(s_pf, l * N_PROJ + (T_DT + 1))
                done = 0

                def link(i):
                    nonlocal done
                    done += 1
                    i.then_inc(s_dtc, 1)
                    dve.wait_ge(s_dtc, l * DTC + done)

                raw = dts[:, 0, :].rearrange("p (t d) -> p t d", t=TT)
                bias_t = par("dt_bias", 0, DT)
                for tt in range(TT):
                    i = dve.tensor_tensor(raw[:, tt, :], raw[:, tt, :], bias_t, ALU.add)
                    if tt == 0:
                        i.then_inc(s_dtc, 1)
                        done += 1
                    else:
                        link(i)
                link(dve.scalar_tensor_tensor(out=dts[:, 2, :], in0=dts[:, 0, :], scalar=-1.0, in1=dts[:, 0, :],
                                              op0=ALU.mult, op1=ALU.min))
                dve.wait_ge(s_dta, l * 2 + 1)
                link(dve.tensor_scalar(dts[:, 4, :], dts[:, 3, :], 2.0, None, ALU.add))
                link(dve.reciprocal(dts[:, 5, :], dts[:, 4, :]))
                link(dve.tensor_tensor(dts[:, 6, :], dts[:, 3, :], dts[:, 5, :], ALU.mult))
                link(dve.tensor_tensor(dts[:, 7, :], dts[:, 6, :], dts[:, 6, :], ALU.mult))
                link(dve.tensor_scalar(dts[:, 1, :], dts[:, 7, :], 1.0 / 17, None, ALU.mult))
                for c in range(15, 1, -2):
                    link(dve.scalar_tensor_tensor(out=dts[:, 1, :], in0=dts[:, 1, :], scalar=1.0 / c,
                                                  in1=dts[:, 7, :], op0=ALU.add, op1=ALU.mult))
                link(dve.scalar_tensor_tensor(out=dts[:, 1, :], in0=dts[:, 1, :], scalar=1.0, in1=dts[:, 6, :],
                                              op0=ALU.add, op1=ALU.mult))
                link(dve.tensor_scalar(dts[:, 2, :], dts[:, 0, :], 0.0, None, ALU.max))
                dt_flat = dt_[:, :, :].rearrange("p t d -> p (t d)")
                link(dve.scalar_tensor_tensor(out=dt_flat, in0=dts[:, 1, :], scalar=2.0, in1=dts[:, 2, :],
                                              op0=ALU.mult, op1=ALU.add))
                dve.wait_ge(s_dta, l * 2 + 2)
                for tt in range(TT):
                    i = dve.scalar_tensor_tensor(out=dta[:, tt, :], in0=dt_[:, tt, :], scalar=-1.0, in1=a_neg[:, :],
                                                 op0=ALU.mult, op1=ALU.mult)
                    i.then_inc(s_dtc, 1)
                    done += 1
                assert done == DTC, done

            def conv(l):
                dve.wait_ge(s_glu, l * 2 + 2)
                depthwise(cv, glu, CONV_K, "conv_dw", "conv_b", CT, s_cvw, l * (CT * CONV_K))

            def conv_norm(l):
                dve.wait_ge(s_lns, l * 2 + 1)
                for c in range(CT):
                    i = dve.scalar_tensor_tensor(out=cvx[:, c, :], in0=bank(7, 0, SEQ), scalar=-1.0 / CONV_CH,
                                                 in1=cv[:, c, :], op0=ALU.mult, op1=ALU.add)
                i.then_inc(s_lnc, 1)
                dve.wait_ge(s_lnc, l * 5 + 1)
                dve.tensor_tensor(cv[:, :, :], cvx[:, :, :], cvx[:, :, :], ALU.mult).then_inc(s_lnc, 1)
                dve.wait_ge(s_lns, l * 2 + 2)
                dve.tensor_scalar(rms_t[:, 0, :], bank(7, SEQ, SEQ), 1.0 / CONV_CH, EPS, ALU.mult,
                                  ALU.add).then_inc(s_lnc, 1)
                dve.wait_ge(s_lna, l * (CT + 1) + 1)
                dve.reciprocal(rstd[:, :], rms_t[:, 1, :]).then_inc(s_lnc, 1)
                dve.wait_ge(s_lnc, l * 5 + 4)
                for c in range(CT):
                    i = dve.tensor_tensor(cvx[:, c, :], cvx[:, c, :], rstd[:, :], ALU.mult)
                i.then_inc(s_lnc, 1)

            def ssm_scores(l):
                for g in range(SSM_GROUPS):
                    dve.wait_ge(s_bc, l * 2 + (g + 1))
                    src = bank(6 + g)
                    dve.tensor_tensor(sc[:, g, 0, :], src[:, 0:P], con("upto"), ALU.mult)
                    dve.tensor_copy(sc[:, g, 1, :], src[:, P:2 * P])
                    dve.tensor_tensor(sc[:, g, 2, :], src[:, 3 * P:4 * P], con("upto"), ALU.mult)
                    dve.tensor_tensor(sc[:, g, 3, :], src[:, 0:P], con("from"), ALU.mult)
                    dve.tensor_copy(sc[:, g, 4, :], src[:, 2 * P:3 * P])
                    dve.tensor_tensor(sc[:, g, 5, :], src[:, 3 * P:4 * P], con("from"), ALU.mult).then_inc(s_sc, 1)

            def ssm_heads(l):
                with dve.Fori(0, SSM_HEADS // SSM_GROUPS) as hh:
                    dve.wait_ge(s_sc, l * 2 + 2)
                    dve.wait_ge(s_xtc, l * TT + TT)
                    n = l * SSM_HEADS + hh * 2
                    for g in range(SSM_GROUPS):
                        c0 = (n + g) * SSM_HC
                        dve.wait_ge(s_r, n + (g + 3))
                        for part in range(4):
                            dve.tensor_tensor_reduce(dg[:, part, :], bank(g, part * P, P), con("ident"), -1.0, 0.0, ALU.mult,
                                                     ALU.add, nb[:, g, part:part + 1]).then_inc(s_hc, 1)
                        dve.wait_ge(s_hc, c0 + 4)
                        dve.tensor_tensor(nb[:, g, 4:5], bank(g, P - 1, 1), nb[:, g, 0:1], ALU.add).then_inc(s_hc, 1)
                        dve.tensor_tensor(nb[:, g, 5:6], bank(g, 3 * P, 1), nb[:, g, 3:4], ALU.add).then_inc(s_hc, 1)
                        dve.wait_ge(s_hc, c0 + 6)
                        for b, (row, col) in enumerate(((0, 0), (1, 4), (1, 1), (2, 2), (2, 5), (3, 3))):
                            i = dve.tensor_scalar(ex[:, g, b, :], bank(g, row * P, P), nb[:, g, col:col + 1], 0.0,
                                                  ALU.add, ALU.min)
                        i.then_inc(s_hc, 1)
                        if g == 1:
                            head_mix(l, hh, n, 0)
                    head_mix(l, hh, n, 1)
                    for g in range(SSM_GROUPS):
                        head_y(l, hh, n, g)

            def head_mix(l, hh, n, g):
                dve.wait_ge(s_ex, n + (g + 1))
                for lo, hi, tt, d in ((0, 2, 0, 0), (2, 3, 1, 0), (3, 4, 0, 1), (4, 6, 1, 1)):
                    i = dve.scalar_tensor_tensor(out=mm_[:, g, lo:hi, :], in0=ex[:, g, lo:hi, :],
                                                 scalar=dt_[:, tt, bass.ds(hh + (d * SSM_HEADS + g * 4), 1)],
                                                 in1=sc[:, g, lo:hi, :], op0=ALU.mult, op1=ALU.mult)
                i.then_inc(s_mm, 1)
                dve.wait_ge(s_mm, n + (g + 1))

            def head_y(l, hh, n, g):
                dve.wait_ge(s_y, n + (g + 1))
                for tt in range(TT):
                    i = dve.scalar_tensor_tensor(out=ys[:, tt, bass.ds(hh * 64 + g * 256, 64)],
                                                 in0=xs[:, tt, bass.ds(hh * 64 + g * 256, 64)],
                                                 scalar=pk[:, bass.ds(hh + (AT["ssm_d"] + g * 4), 1)],
                                                 in1=bank(2 + g, tt * 64, 64), op0=ALU.mult, op1=ALU.add)
                i.then_inc(s_yh, 1)

            def ssm_out(l):
                c0 = l * SSM_YC
                dve.wait_ge(s_yh, l * SSM_HEADS + SSM_HEADS)
                dve.tensor_tensor(ys[:, :, :], ys[:, :, :], z[:, :, :], ALU.mult).then_inc(s_yc, 1)
                dve.wait_ge(s_yc, c0 + 1)
                for tt in range(TT):
                    if tt:
                        dve.wait_ge(s_yc, c0 + 1 + tt)
                    dve.tensor_tensor_reduce(ysq[:, :], ys[:, tt, :], ys[:, tt, :], 1.0, 0.0, ALU.mult, ALU.add,
                                             yst[:, tt:tt + 1]).then_inc(s_yc, 1)
                dve.wait_ge(s_yc, c0 + 3)
                dve.tensor_scalar(yst[:, 2:4], yst[:, 0:2], 1.0 / SSM_INNER, EPS, ALU.mult, ALU.add).then_inc(s_yc, 1)
                dve.wait_ge(s_ya, l + 1)
                dve.reciprocal(yst[:, 6:8], yst[:, 4:6]).then_inc(s_yc, 1)
                dve.wait_ge(s_yc, c0 + 5)
                for tt in range(TT):
                    i = dve.tensor_scalar(ys[:, tt, :], ys[:, tt, :], yst[:, 6 + tt:7 + tt], None, ALU.mult)
                i.then_inc(s_yc, 1)

            def attention(l):
                scale = float(ATT_HEAD_DIM) ** -0.5
                with dve.Fori(0, HP) as i:
                    n = l * UNITS + i * 4

                    def biased(u):
                        dve.wait_ge(s_s, n + (u + 2))
                        if u % TT == 0:
                            dve.wait_ge(s_bia[u // TT], (l * HP + i + 1) * (16 * TT))
                        if u >= 2:
                            dve.wait_ge(s_t, n + (u - 1))
                        dve.scalar_tensor_tensor(out=sa[:, u % 2, :], in0=bank(4 + 2 * (u % 2), 0, GK),
                                                 scalar=scale, in1=bias[u // TT][:, u % TT, :],
                                                 op0=ALU.mult, op1=ALU.add).then_inc(s_sb, 1)
                        dve.wait_ge(s_sb, n + (u + 1))
                        dve.tensor_reduce(ast[:, u % 2, 2:3], sa[:, u % 2, :], AX_X, ALU.max).then_inc(s_mx, 1)
                        dve.wait_ge(s_mx, n + (u + 1))
                        dve.tensor_scalar(ast[:, u % 2, 0:1], ast[:, u % 2, 2:3], -1.0, None, ALU.mult).then_inc(s_am, 1)

                    def scaled(u):
                        dve.wait_ge(s_e, n + (u + 1))
                        dve.reciprocal(ast[:, u % 2, 3:4], ast[:, u % 2, 1:2]).then_inc(s_dn, 1)
                        dve.wait_ge(s_dn, n + (u + 1))
                        dve.wait_ge(s_o, n + (u + 1))
                        dve.tensor_scalar(ao[:, u % TT, bass.ds(i * P + 64 * (u // TT), 64)],
                                          bank(2 * (u % 2), GK, 64), ast[:, u % 2, 3:4], None,
                                          ALU.mult).then_inc(s_oc, 1)

                    biased(0)
                    biased(1)
                    scaled(0)
                    biased(2)
                    scaled(1)
                    biased(3)
                    scaled(2)
                    scaled(3)

            def branches(l):
                for m_ in range(KT):
                    dve.wait_ge(s_sg, l * (N_BRANCHES * KT) + (m_ + 1))
                    dve.tensor_tensor(mix[:, m_, :], gs[:, m_ % 2, :], bank(2 * (m_ % 2), 0, SEQ),
                                      ALU.mult).then_inc(s_bm, 1)
                with dve.Fori(0, N_BRANCHES - 1) as b:
                    n = l * (N_BRANCHES * KT) + b * KT
                    for m_ in range(KT):
                        dve.wait_ge(s_sg, n + (KT + m_ + 1))
                        dve.tensor_tensor(gt[:, m_ % 2, :], gs[:, m_ % 2, :], bank(2 * (m_ % 2), 0, SEQ),
                                          ALU.mult).then_inc(s_bt, 1)
                        dve.wait_ge(s_bt, l * (3 * KT) + b * KT + (m_ + 1))
                        dve.wait_ge(s_bm, n + (m_ + 3))
                        dve.tensor_tensor(mix[:, m_, :], mix[:, m_, :], gt[:, m_ % 2, :], ALU.add).then_inc(s_bm, 1)

            def mix_out(l):
                for m_ in range(KT):
                    dve.wait_ge(s_wo, l * KT + (m_ + 1))
                    i = dve.tensor_tensor(h[:, m_, :], h[:, m_, :], bank(m_, 0, SEQ), ALU.add)
                i.then_inc(s_h, 1)
                dve.wait_ge(s_h, l * 3 + 2)

            def dense():
                with dve.Fori(0, DENSE_CHUNKS) as i:
                    for half in range(2):
                        dve.wait_ge(s_ds, i * 2 + (half + 1))
                        dve.wait_ge(s_dr, i * 2 + (half + 1))
                        dve.tensor_tensor(hid[:, half, :], hs[:, half, :], bank(2 * half + 1, 0, SEQ),
                                          ALU.mult).then_inc(s_dh, 1)
                dve.wait_ge(s_dr, 2 * DENSE_CHUNKS + 2)
                for m_ in range(KT):
                    i = dve.tensor_tensor(h[:, m_, :], h[:, m_, :], bank(4 + m_ // 2, (m_ % 2) * SEQ, SEQ), ALU.add)
                i.then_inc(s_h, 1)

            def route():
                done = 0

                def link(i, s=s_rc):
                    nonlocal done
                    done += 1
                    i.then_inc(s_rc, 1)
                    dve.wait_ge(s_rc, done)

                dve.wait_ge(s_rl, 1)
                link(dve.tensor_copy(lg[:, :, :], bank(4, 0, TT * N_EXPERTS).rearrange("p (t e) -> p t e", t=TT)))
                for tt in range(TT):
                    link(dve.max(top[:, tt, :], lg[:, tt, :]))
                    link(dve.max_index(topi[:, tt, :], top[:, tt, :], lg[:, tt, :]))
                link(dve.tensor_tensor(rt[:, :, 0:1], top[:, :, 1:2], top[:, :, 0:1], ALU.subtract))
                assert done == RC_EXP
                link(dve.tensor_copy(topf[:, :, :], topi[:, :, :]))
                for tt in range(TT):
                    for c in range(2):
                        link(dve.tensor_scalar(oh[:, tt, c, :], con("experts", 0, N_EXPERTS), topf[:, tt, c:c + 1], None,
                                               ALU.is_equal))
                    link(dve.tensor_tensor(msk[:, tt, :], oh[:, tt, 0, :], oh[:, tt, 1, :], ALU.add))
                assert done == RC_MASK, done
                dve.wait_ge(s_re, 1)
                link(dve.tensor_scalar(rt[:, :, 2:3], rt[:, :, 1:2], 1.0, None, ALU.add))
                link(dve.reciprocal(rt[:, :, 3:4], rt[:, :, 2:3]))
                link(dve.tensor_tensor(rt[:, :, 4:5], rt[:, :, 3:4], rt[:, :, 1:2], ALU.mult))
                for tt in range(TT):
                    link(dve.tensor_scalar(comb[:, tt, :], oh[:, tt, 0, :], rt[:, tt, 3:4], None, ALU.mult))
                    link(dve.scalar_tensor_tensor(out=comb[:, tt, :], in0=oh[:, tt, 1, :], scalar=rt[:, tt, 4:5],
                                                  in1=comb[:, tt, :], op0=ALU.mult, op1=ALU.add))
                dve.wait_ge(s_rp, 1)
                link(dve.tensor_scalar(pos[:, :, :], bank(5, 0, TT * N_EXPERTS).rearrange("p (t e) -> p t e", t=TT),
                                       1.0, None, ALU.add))
                link(dve.tensor_tensor(pos[:, :, :], pos[:, :, :], msk[:, :, :], ALU.mult))
                link(dve.tensor_scalar(pos[:, :, :], pos[:, :, :], -1.0, None, ALU.add))
                link(dve.tensor_reduce(cnt[:, 0:1], bank(5, 2 * N_EXPERTS, N_EXPERTS), AX_X, ALU.max))
                link(dve.tensor_scalar(cnt[:, 1:2], cnt[:, 0:1], float(P), 1.0, ALU.is_gt, ALU.add))
                dve.tensor_copy(rounds[:, :], cnt[:, 1:2]).then_inc(s_rr, 1)
                dve.wait_ge(s_rr, 1)

            def experts():
                n_r = dve.value_load(rounds[0:1, 0:1], min_val=1, max_val=2)
                with dve.Fori(0, n_r) as o:
                    with dve.Fori(0, N_EXPERTS) as e:
                        q = o * N_EXPERTS + e
                        for tt in range(TT):
                            i = dve.tensor_scalar(gat[:, 0, tt, :], con("slots"), pos[:, tt, bass.ds(e, 1)], None,
                                                  ALU.is_equal)
                        i.then_inc(s_g, 1)
                        dve.wait_ge(s_g, q + 1)
                        for tt in range(TT):
                            i = dve.tensor_scalar(gatw[:, 0, tt, :], gat[:, 0, tt, :], comb[:, tt, bass.ds(e, 1)], None,
                                                  ALU.mult)
                        i.then_inc(s_gw, 1)
                        with dve.Fori(0, EXP_CHUNKS) as i_:
                            n = q * (2 * EXP_CHUNKS) + i_ * 2
                            for half in range(2):
                                dve.wait_ge(s_es, n + (half + 1))
                                dve.wait_ge(s_er, n + (half + 1))
                                dve.tensor_tensor(hid[:, half, 0:P], hs[:, half, 0:P], bank(2 * half + 1, 0, P),
                                                  ALU.mult).then_inc(s_eh, 1)
                        for m_ in range(KT):
                            dve.wait_ge(s_eo, q * KT + (m_ + 1))
                            if m_ == 0:
                                dve.wait_ge(s_ea, q * KT + 2)
                            dve.tensor_tensor(h[:, m_, :], h[:, m_, :], bank(6 + m_ % 2, 0, SEQ),
                                              ALU.add).then_inc(s_ea, 1)
                    dve.wait_ge(s_gw, o * N_EXPERTS + N_EXPERTS)
                    dve.tensor_scalar(pos[:, :, :], pos[:, :, :], -float(P), None, ALU.add).then_inc(s_pos, 1)
                    dve.wait_ge(s_pos, o + 1)
                dve.memset(cnt[:, 3:4], 0.0).then_inc(s_h, 1)

            def ple(l):
                dve.wait_ge(s_h, l * 3 + 3)
                for m_ in range(KT):
                    dve.wait_ge(s_pg, l * KT + (m_ + 1))
                    dve.tensor_tensor(mix[:, m_, :], gs[:, m_ % 2, :], bank(2 * (m_ % 2), 0, SEQ),
                                      ALU.mult).then_inc(s_pt, 1)
                dve.wait_ge(s_pt, l * KT + KT)
                dve.tensor_tensor(h[:, :, :], h[:, :, :], mix[:, :, :], ALU.add).then_inc(s_h, 1)
                dve.wait_ge(s_h, l * 3 + 4)

            dve.sem_inc(s_bm, 2)
            dve.sem_inc(s_dh, 2)
            dve.sem_inc(s_eh, 2)
            dve.sem_inc(s_ea, 2)
            dve.wait_ge(s_x, 16)
            dve.memset(cnt[:, 2:3], 0.0).then_inc(s_h, 1)
            dve.wait_ge(s_zero, 2)
            dve.wait_ge(s_cst, 16)
            with dve.Fori(0, DEPTH) as l:
                dve.wait_ge(s_pk, l * 16 + 16)
                norm(l * 2, "norm_mix")
                ssm_conv(l)
                time_steps(l)
                conv(l)
                conv_norm(l)
                ssm_scores(l)
                ssm_heads(l)
                ssm_out(l)
                attention(l)
                branches(l)
                mix_out(l)
                norm(l * 2 + 1, "norm_ffn")
                with dve.If(l < 1):
                    dense()
                with dve.Else():
                    route()
                    experts()
                ple(l)
            norm(2 * DEPTH, "final_norm")

        @block.gpsimd
        def _(pool):
            for t in (glu, xbcp):
                pad = PAD if t is glu else SPAD
                pool.memset(t[:, :, 0:pad], 0.0)
                pool.memset(t[:, :, SEQ + pad:SEQ + 2 * pad], 0.0).then_inc(s_zero, 1)
            pool.wait_ge(s_zero, 2)
            pool.wait_ge(s_relW, 16)
            pool.wait_ge(s_cst, 16)

            def load_bias(l, i, slot):
                for tt in range(TT):
                    src = bass.AP(tensor=scratch.ap().tensor,
                                  offset=(i * 2 + slot) * (ATT_GROUPS * 2 * SEQ) + tt * P,
                                  ap=[[1, P], [2 * SEQ, ATT_GROUPS], [1, SEQ]])
                    dst = bias[slot][:, tt, :].rearrange("p (g k) -> p g k", g=ATT_GROUPS)
                    pool.dma_start(dst, src).then_inc(s_bia[slot], 16)

            with pool.Fori(0, DEPTH) as l:
                for pair in range(2):
                    pool.wait_ge(s_pf, l * N_PROJ + (4 * pair + 4))
                    pool.tensor_tensor(glu[:, 2 * pair:2 * pair + 2, PAD:PAD + SEQ], glu_a[:, pair, :, :],
                                       glu_s[:, pair, :, :], ALU.mult).then_inc(s_glu, 1)
                load_bias(l, 0, 0)
                with pool.Fori(0, SSM_HEADS // SSM_GROUPS) as hh:
                    pool.wait_ge(s_dtc, l * DTC + DTC)
                    n = l * SSM_HEADS + hh * 2
                    for g in range(SSM_GROUPS):
                        pool.wait_ge(s_r, n + (g + 1))
                        for d in range(2):
                            for tt in range(TT):
                                col = dta[:, tt, bass.ds(hh + (d * SSM_HEADS + g * 4), 1)]
                                k = pool.tensor_tensor(ua[:, g, 2 * d + tt, :], con("upto" if d == 0 else "from"),
                                                       col.to_broadcast([P, P]), ALU.mult)
                        k.then_inc(s_ua, 1)
                pool.wait_ge(s_lns, l * 2 + 2)
                pool.sem_inc(s_step, 1)
                load_bias(l, 0, 1)
                with pool.Fori(0, HP) as i:
                    pool.wait_ge(s_pf, l * N_PROJ + N_PROJ)
                    n = l * UNITS + i * 4
                    pool.wait_ge(s_s, n + 1)
                    pool.wait_ge(s_yc, l * SSM_YC + 1)
                    for which in range(2):
                        src = qk[:, which * ATT_GROUPS:(which + 1) * ATT_GROUPS, bass.ds(i, 1), :]
                        dst = qkp[:, which, :, :].rearrange("p g (o t) -> p g o t", o=1)
                        pool.tensor_copy(dst[:, :, :, ::-1] if which == 0 else dst, src).then_inc(s_qkp, 1)
                    with pool.If(i < HP - 1):
                        for slot in range(2):
                            pool.wait_ge(s_sb, n + (2 * slot + 2))
                            pool.sem_inc(s_step, 1)
                            load_bias(l, i + 1, slot)


def _cols(w, c0, c1, width=COLS):
    k = w.shape[0] // P
    return w[:, c0:c1].reshape(k, P, (c1 - c0) // width, width).transpose(2, 1, 0, 3).reshape(-1, P, k * width)


def _rows(w):
    return w.reshape(-1, 2, P, D_MODEL).transpose(0, 2, 1, 3).reshape(-1, P, BLK)


def _triples(w1, w3, w2):
    f = w1.shape[1]
    return np.stack([_cols(w1, 0, f), _cols(w3, 0, f), _rows(w2)], axis=1).reshape(-1, P, BLK)


def _mixer_blocks(w_in, w_gate, branch_out, w_out):
    c = OFF_CONV
    conv = [_cols(w_in, c + o, c + o + COLS) for o in (0, CONV_CH, COLS, CONV_CH + COLS)]
    xbc = OFF_SSM + SSM_INNER
    parts = conv + [_cols(w_in, xbc, OFF_DT), _cols(w_in, OFF_SSM, xbc),
                    _cols(w_in, OFF_FNET, OFF_FNET + FNET_WIDTH), _cols(w_in, 0, OFF_CONV)]
    for b, where in enumerate(BRANCH_OF):
        gate = _cols(w_gate[where], 0, D_MODEL)
        o = _cols(branch_out[b], 0, D_MODEL, 512)
        parts += [gate[0:1], o[0:1], gate[1:3], o[1:2], gate[3:4]]
    return np.concatenate(parts + [_cols(w_out, 0, D_MODEL)])


def _per_partition(a):
    return a.reshape(-1, P).T


def _everywhere(a):
    return np.broadcast_to(a.reshape(1, -1), (P, a.size))


def _constants():
    t = np.arange(P)
    s = np.arange(SEQ)
    ch = 2 * np.pi * np.outer(t, t) / FNET_GROUP_DIM
    tk = 2 * np.pi * (np.outer(s, s) % SEQ) / SEQ
    norm = 1.0 / math.sqrt(SEQ * FNET_GROUP_DIM)

    def tokens(m):
        return m.reshape(TT, P, SEQ).transpose(1, 0, 2).reshape(P, TT * SEQ)

    parts = {"ident": np.eye(P), "upto": t[:, None] <= t[None], "from": t[:, None] >= t[None],
             "before": t[:, None] < t[None], "ones": np.ones((P, P)), "slots": np.tile(t, (P, 1)),
             "dft_ch": np.concatenate([np.cos(ch), np.sin(ch)], 1), "dft_cos": tokens(np.cos(tk)) * norm,
             "dft_sin": -tokens(np.sin(tk)) * norm, "experts": np.tile(np.arange(N_EXPERTS), (P, 1))}
    return np.concatenate([np.asarray(parts[n], np.float64) for n, _ in _CONSTS], 1).astype(np.float32)


def _bucket_rows():
    oh = np.zeros((REL_BUCKETS + 1, ATT_GROUPS, 2 * SEQ), np.float32)
    for g, (window, dil) in enumerate(ATT_PATTERNS):
        half, hb = window // (2 * dil), REL_BUCKETS // 2
        for c in range(2 * SEQ):
            rel = c - (SEQ - 1)
            if rel % dil or abs(rel) > half * dil or rel >= SEQ:
                oh[REL_BUCKETS, g, c] = MASKED
                continue
            n, exact = abs(rel), hb // 2
            large = min(hb - 1, exact + int(math.log(max(n, 1) / exact) / math.log(REL_MAX_DIST / exact) * (hb - exact)))
            oh[(hb if rel > 0 else 0) + (n if n < exact else large), g, c] = 1.0
    return oh


def kernel(x, p, rel_bias, norm_mix, w_in, conv_dw, conv_dw_b, conv_ln_g, conv_ln_b, conv_out, ssm_conv_w,
           ssm_conv_b, ssm_a_log, ssm_dt_bias, ssm_d, ssm_norm, ssm_out, attn_out, fnet_out, w_gate, b_gate,
           w_out, norm_ffn, ffn_w1, ffn_w3, ffn_w2, moe_router, moe_w1, moe_w3, moe_w2, ple_gate, ple_proj,
           final_norm):
    from concourse import bacc
    from concourse.bass_utils import run_bass_kernel_spmd

    (x, p, rel_bias, norm_mix, w_in, conv_dw, conv_dw_b, conv_ln_g, conv_ln_b, conv_out, ssm_conv_w,
     ssm_conv_b, ssm_a_log, ssm_dt_bias, ssm_d, ssm_norm, ssm_out, attn_out, fnet_out, w_gate, b_gate,
     w_out, norm_ffn, ffn_w1, ffn_w3, ffn_w2, moe_router, moe_w1, moe_w3, moe_w2, ple_gate, ple_proj,
     final_norm) = [np.asarray(a) for a in (
         x, p, rel_bias, norm_mix, w_in, conv_dw, conv_dw_b, conv_ln_g, conv_ln_b, conv_out, ssm_conv_w,
         ssm_conv_b, ssm_a_log, ssm_dt_bias, ssm_d, ssm_norm, ssm_out, attn_out, fnet_out, w_gate, b_gate,
         w_out, norm_ffn, ffn_w1, ffn_w3, ffn_w2, moe_router, moe_w1, moe_w3, moe_w2, ple_gate, ple_proj,
         final_norm)]

    def by_token(a):
        return a.reshape(SEQ, -1, P).transpose(2, 1, 0)

    def params(l):
        parts = {
            "norm_mix": _per_partition(norm_mix[l]), "norm_ffn": _per_partition(norm_ffn[l]),
            "final_norm": _per_partition(final_norm), "b_gate": _per_partition(b_gate[l][list(BRANCH_OF)]),
            "conv_dw": _per_partition(conv_dw[l]), "conv_b": _per_partition(conv_dw_b[l]),
            "ln_g": _per_partition(conv_ln_g[l]), "ln_b": _per_partition(conv_ln_b[l]),
            "ssm_w": _per_partition(ssm_conv_w[l]), "ssm_b": _per_partition(ssm_conv_b[l]),
            "ssm_norm": _per_partition(ssm_norm[l]), "ssm_d": _everywhere(ssm_d[l]),
            "a_log": _everywhere(ssm_a_log[l]), "dt_bias": _everywhere(ssm_dt_bias[l]),
            "w_dt": _cols(w_in[l], OFF_DT, OFF_FNET, DT)[0],
            "router": _cols(moe_router[0], 0, N_EXPERTS, N_EXPERTS)[0],
            "p": by_token(p[l, 0]).reshape(P, -1)}
        return np.concatenate([parts[n] for n, _ in _PARAMS], 1)

    relb = np.concatenate([rel_bias, np.ones((1, rel_bias.shape[1]), rel_bias.dtype)])
    arrays = {
        "x_in": by_token(x[0]),
        "w_mixers": np.stack([_mixer_blocks(w_in[l], w_gate[l], (fnet_out[l], conv_out[l], ssm_out[l], attn_out[l]),
                                            w_out[l]) for l in range(DEPTH)]),
        "w_dense": _triples(ffn_w1[0], ffn_w3[0], ffn_w2[0]),
        "w_experts": np.concatenate([_triples(moe_w1[0, e], moe_w3[0, e], moe_w2[0, e]) for e in range(N_EXPERTS)]),
        "w_ple": np.stack([np.concatenate([_cols(ple_gate[l], 0, D_MODEL), _rows(ple_proj[l])]) for l in range(DEPTH)]),
        "params": np.stack([params(l) for l in range(DEPTH)]),
        "constants": _constants(),
        "buckets": _bucket_rows(),
        "bias_table": relb,
    }
    arrays = {n: np.ascontiguousarray(a) for n, a in arrays.items()}
    nc = bacc.Bacc("TRN2", target_bir_lowering=False, num_devices=1)
    ins = [nc.dram_tensor(n, a.shape, mybir.dt.from_np(a.dtype), kind="ExternalInput").ap() for n, a in arrays.items()]
    out = nc.dram_tensor("trunk_out", (P, KT, SEQ), F32, kind="ExternalOutput").ap()
    trunk_program(nc, *ins, out)
    got = run_bass_kernel_spmd(nc, [arrays], core_ids=[0]).results[0]["trunk_out"]
    return got.transpose(2, 1, 0).reshape(1, SEQ, D_MODEL)
```

```python
from contextlib import ExitStack
import math

import numpy as np

import concourse.bass as bass
from concourse import mybir

F32 = mybir.dt.float32
F32R = mybir.dt.float32r
I32 = mybir.dt.int32
U32 = mybir.dt.uint32
ACT = mybir.ActivationFunctionType
ALU = mybir.AluOpType
AX_X = mybir.AxisListType.X

P = 128
D_MODEL = 1024
SEQ = 256
DEPTH = 2
EPS = 1e-6
PLE_DIM = 256
N_BRANCHES = 4
CONV_CH, CONV_K = 512, 31
SSM_HEADS, SSM_HEAD_DIM, SSM_GROUPS, SSM_STATE, SSM_CONV = 8, 64, 2, 64, 5
SSM_INNER = SSM_HEADS * SSM_HEAD_DIM
SSM_CONV_CH = SSM_INNER + 2 * SSM_GROUPS * SSM_STATE
ATT_PATTERNS = ((128, 1), (512, 4), (2048, 16))
ATT_GROUPS, ATT_HEADS, ATT_HEAD_DIM = 3, 8, 64
ATT_WIDTH = ATT_HEADS * ATT_HEAD_DIM
REL_BUCKETS, REL_MAX_DIST = 32, 1024
FNET_GROUPS, FNET_GROUP_DIM = 4, 128
FNET_WIDTH = FNET_GROUPS * FNET_GROUP_DIM
FFN_DIM, N_EXPERTS, EXPERT_DIM = 2816, 8, 3584
OFF_CONV = 3 * ATT_GROUPS * ATT_WIDTH
OFF_SSM = OFF_CONV + 2 * CONV_CH
OFF_DT = OFF_SSM + SSM_INNER + SSM_CONV_CH
OFF_FNET = OFF_DT + 2 * SSM_HEADS
MASKED = -1e30

KT = D_MODEL // P
TT = SEQ // P
CT = CONV_CH // P
XT = SSM_CONV_CH // P
DT = 2 * SSM_HEADS
PAD = CONV_K // 2
SPAD = SSM_CONV // 2
HALF = SEQ

BLK = 2048
RING = 6
COLS = BLK // KT
PROJ_BLOCKS = 29
BRANCH_BLOCKS = 6
MIX_BLOCKS = PROJ_BLOCKS + N_BRANCHES * BRANCH_BLOCKS + 4
MIX_ROUNDS = 10
DENSE_CHUNKS = FFN_DIM // COLS
EXP_CHUNKS = EXPERT_DIM // COLS
DENSE_ROUNDS = (3 * DENSE_CHUNKS + RING - 1) // RING
PASS_ROUNDS = 3 * EXP_CHUNKS // RING
PLE_BLOCKS = 5
LAYER0_ROUNDS = MIX_ROUNDS + DENSE_ROUNDS + 1
UNIT = BLK // 2
SLOTS = 6
DENSE_UNITS, PASS_UNITS = 6 * DENSE_CHUNKS, 6 * EXP_CHUNKS
DENSE_BLOCKS = 3 * DENSE_CHUNKS
assert DENSE_UNITS % SLOTS == 0 and PASS_UNITS % SLOTS == 0
assert MIX_BLOCKS <= MIX_ROUNDS * RING and PLE_BLOCKS < RING and 3 * EXP_CHUNKS % RING == 0

_PARAMS = (("norm_mix", KT), ("norm_ffn", KT), ("final_norm", KT), ("b_gate", N_BRANCHES * KT),
           ("conv_dw", CONV_K * CT), ("conv_b", CT), ("ln_g", CT), ("ln_b", CT),
           ("ssm_w", SSM_CONV * XT), ("ssm_b", XT), ("ssm_norm", CT),
           ("ssm_d", SSM_HEADS), ("a_log", DT), ("dt_bias", DT),
           ("w_dt", KT * DT), ("router", KT * N_EXPERTS),
           ("p", PLE_DIM // P * SEQ))
AT = {}
PK = 0
for _name, _n in _PARAMS:
    AT[_name] = PK
    PK += _n

_CONSTS = (("ident", P), ("upto", P), ("from", P), ("before", P), ("ones", P), ("slots", P),
           ("dft_ch", 2 * P), ("dft_cos", TT * SEQ), ("dft_sin", TT * SEQ), ("experts", N_EXPERTS))
CAT = {}
CK = 0
for _name, _n in _CONSTS:
    CAT[_name] = CK
    CK += _n

FNET, CONV, SSM, ATT = range(4)
BRANCH_OF = (3, 1, 2, 0)
N_PROJ = 59
DTC = 20
SSM_HC = 7
SSM_YC = 6
RC_EXP, RC_MASK = 6, 13
T_XBC, T_Z, T_DT, T_FN, T_V = 8, 14, 18, 19, 23
T_Q = T_V + 12
HB = N_BRANCHES // 2
UNITS = ATT_HEADS * TT
HP = ATT_HEADS // 2
GK = ATT_GROUPS * SEQ


def trunk_program(nc, x, wm, wd, we, wp, pk_in, cst_in, onehot, relb, out):
    ctx = ExitStack()
    with ctx:
        def sb(name, shape, dt=F32):
            return ctx.enter_context(nc.sbuf_tensor(name, shape, dt))

        def sem(name):
            return ctx.enter_context(nc.semaphore(name))

        scratch = nc.dram_tensor("bias_rows", [ATT_HEADS, ATT_GROUPS, 2 * SEQ], F32)

        ring = sb("ring", [P, RING, BLK])
        h = sb("h", [P, KT, SEQ])
        xn = sb("xn", [P, KT, SEQ])
        mix = sb("mix", [P, KT, SEQ])
        pk = sb("params_sb", [P, PK])
        cst = sb("constants_sb", [P, CK])
        gs = sb("gs", [P, 2, SEQ])
        gt = sb("gt", [P, 2, SEQ])
        xbcp = sb("xbcp", [P, XT, SEQ + 2 * SPAD])
        glu = sb("glu", [P, CT, SEQ + 2 * PAD])
        topi = sb("topi", [P, TT, 8], U32)
        cnt = sb("cnt", [P, 4])
        rounds = sb("rounds", [P, 1], I32)
        rstd = sb("rstd", [P, SEQ])
        rms_t = sb("rms_t", [P, 2, SEQ])

        mixers = ExitStack()

        def msb(name, shape, dt=F32):
            return mixers.enter_context(nc.sbuf_tensor(name, shape, dt))

        glu_a = msb("glu_a", [P, 2, 2, SEQ])
        glu_s = msb("glu_s", [P, 2, 2, SEQ])
        cvfa = msb("cvfa", [P, 2 * CT * SEQ])
        xbc = msb("xbc", [P, XT, SEQ])
        qk = msb("qk", [P, 2 * ATT_GROUPS, HP, SEQ])
        v = msb("v", [P, TT, ATT_GROUPS * ATT_WIDTH])
        ybr = msb("ybr", [P, N_BRANCHES * CT, SEQ])
        dts = msb("dts", [P, 8, TT * DT])
        dt_ = msb("dt", [P, TT, DT])
        dta = msb("dta", [P, TT, DT])
        a_neg = msb("a_pos", [P, DT])
        sc = msb("sc", [P, SSM_GROUPS, 6, P])
        ua = msb("ua", [P, 2, 4, P])
        dg = msb("dg", [P, 4, P])
        nb = msb("nb", [P, 2, 6])
        ex = msb("ex", [P, 2, 6, P])
        mm_ = msb("mm", [P, 2, 6, P])
        yst = msb("yst", [P, 8])
        ast = msb("ast", [P, 2, 4])
        bias0 = msb("bias0", [P, TT, GK])

        def view(buf, lo, shape, pattern, **sizes):
            n = int(np.prod(shape))
            flat = buf if len(buf.shape) == 2 else buf.rearrange("p a b -> p (a b)") if len(buf.shape) == 3 \
                else buf.rearrange("p a b c -> p (a b c)")
            return flat[:, lo:lo + n] if pattern == "p c -> p c" else flat[:, lo:lo + n].rearrange(pattern, **sizes)

        cv = view(cvfa[:, :], 0, [CT, SEQ], "p (c t) -> p c t", c=CT)
        fa = view(cvfa[:, :], CT * SEQ, [2, TT, 2 * P], "p (a t c) -> p a t c", a=2, t=TT)
        cvx = view(glu_a[:, :, :, :], 0, [CT, SEQ], "p (c t) -> p c t", c=CT)
        ys = view(glu_s[:, :, :, :], 0, [TT, SSM_INNER], "p (t c) -> p t c", t=TT)
        ysq = view(dg[:, :, :], 0, [SSM_INNER], "p c -> p c")
        fu = ybr[:, 0:CT, :]
        z = view(ybr[:, :, :], 2 * CT * SEQ, [TT, SSM_INNER], "p (t c) -> p t c", t=TT)
        xs = view(ybr[:, :, :], 3 * CT * SEQ, [TT, SSM_INNER], "p (t c) -> p t c", t=TT)
        bias = [bias0, view(cvfa[:, :], 0, [TT, GK], "p (t k) -> p t k", t=TT)]
        qkp = view(sc[:, :, :, :], 0, [2, ATT_GROUPS, SEQ], "p (w g t) -> p w g t", w=2, g=ATT_GROUPS)
        sa = view(ex[:, :, :, :], 0, [2, GK], "p (u k) -> p u k", u=2)
        pt = view(mm_[:, :, :, :], 0, [2, GK], "p (u k) -> p u k", u=2)
        ao = view(xbc[:, :, :], 0, [TT, ATT_WIDTH], "p (t c) -> p t c", t=TT)
        mixers.close()

        whi = sb("whi", [P, SLOTS, UNIT], F32R)
        wlo = sb("wlo", [P, SLOTS, UNIT], F32R)
        xhi = sb("xhi", [P, KT, SEQ], F32R)
        xlo = sb("xlo", [P, KT, SEQ], F32R)
        hhi = sb("hhi", [P, 2, 2, SEQ], F32R)
        hlo = sb("hlo", [P, 2, 2, SEQ], F32R)
        hs, hid = gs, gt
        yx = sb("yx", [P, D_MODEL])
        gat = sb("gat", [P, TT, P])
        gatw = sb("gatw", [P, TT, P])
        sca = sb("sca", [P, SEQ])
        lg = sb("lg", [P, TT, N_EXPERTS])
        top = sb("top", [P, TT, 8])
        topf = sb("topf", [P, TT, 8])
        rt = sb("rt", [P, TT, 8])
        oh = sb("oh", [P, TT, 2, N_EXPERTS])
        comb = sb("comb", [P, TT, N_EXPERTS])
        msk = sb("msk", [P, TT, N_EXPERTS])
        pos = sb("pos", [P, TT, N_EXPERTS])

        n_oh = ATT_GROUPS * 2 * SEQ
        ybr_flat = ybr[:, :, :].rearrange("p c t -> p (c t)")
        onehot_sb = ybr_flat[0:REL_BUCKETS + 1, 0:n_oh].rearrange("p (g c) -> p g c", g=ATT_GROUPS)
        relb_sb = ybr_flat[0:REL_BUCKETS + 1, n_oh:n_oh + ATT_GROUPS * ATT_HEADS]
        rows_sb = ybr_flat[0:ATT_HEADS, 2048:2048 + n_oh].rearrange("p (g c) -> p g c", g=ATT_GROUPS)

        ps = ctx.enter_context(nc.psum_tensor("ps", [P, 8 * 512], F32))

        def bank(b, lo=0, n=512):
            return ps[:, 512 * b + lo:512 * b + lo + n]

        def par(name, i=0, n=1):
            return pk[:, AT[name] + i:AT[name] + i + n]

        def con(name, i=0, n=P):
            return cst[:, CAT[name] + i:CAT[name] + i + n]

        s_loaded = [sem(f"ring_loaded{i}") for i in range(RING)]
        s_cst = sem("constants_loaded")
        s_x = sem("x_loaded")
        s_zero = sem("pads_zeroed")
        s_relT = sem("bias_rows_product")
        s_relL = sem("bias_inputs_loaded")
        s_relC = sem("bias_rows_copied")
        s_relW = sem("bias_rows_written")
        s_pk = sem("params_loaded")
        s_h = sem("h_ready")
        s_sq = sem("squares_ready")
        s_ms = sem("mean_square_ready")
        s_var = sem("variance_ready")
        s_sd = sem("deviation_ready")
        s_rs = sem("rstd_ready")
        s_xn = sem("xn_ready")
        s_pj = sem("proj_tile_ready")
        s_pf = sem("proj_tile_copied")
        s_glu = sem("glu_ready")
        s_cvw = sem("conv_chain")
        s_xc = sem("ssm_conv_chain")
        s_xa = sem("ssm_conv_active")
        s_dtc = sem("dt_chain")
        s_dta = sem("dt_exp")
        s_lns = sem("ln_sum_ready")
        s_lnc = sem("ln_chain")
        s_lna = sem("ln_act")
        s_f1 = sem("fnet_channels_ready")
        s_f1c = sem("fnet_channels_copied")
        s_f2 = sem("fnet_tokens_ready")
        s_f2c = sem("fnet_tokens_copied")
        s_xt = sem("x_transposed")
        s_xtc = sem("x_transposed_copied")
        s_bc = sem("bc_scores_ready")
        s_sc = sem("bc_scores_masked")
        s_ua = sem("dta_rows_ready")
        s_r = sem("cumsum_ready")
        s_hc = sem("ssm_head_chain")
        s_ex = sem("decay_ready")
        s_mm = sem("ssm_mix_ready")
        s_y = sem("ssm_y_ready")
        s_yh = sem("ssm_head_y_done")
        s_yc = sem("ssm_y_chain")
        s_ya = sem("ssm_sd_ready")
        s_yt = sem("ssm_y_transposed")
        s_ybs = sem("ssm_branch_ready")
        s_bia = [sem(f"bias_loaded{i}") for i in range(2)]
        s_qkp = sem("head_pair_staged")
        s_s = sem("scores_ready")
        s_sb = sem("scores_biased")
        s_mx = sem("max_ready")
        s_am = sem("neg_max_ready")
        s_e = sem("probs_ready")
        s_t = sem("probs_transposed")
        s_tc = sem("probs_transposed_copied")
        s_o = sem("attn_out_ready")
        s_dn = sem("denominator_inverted")
        s_oc = sem("attn_out_scaled")
        s_ot = sem("attn_out_transposed")
        s_yba = sem("attn_branch_ready")
        s_br = sem("branch_tile_ready")
        s_sg = sem("gate_ready")
        s_bt = sem("gated_tile")
        s_mz = sem("mix_zeroed")
        s_bm = sem("mix_tile_ready")
        s_wo = sem("w_out_tile_ready")
        s_xh = sem("ffn_input_hi")
        s_xl = sem("ffn_input_lo")
        s_wh = sem("weight_unit_hi")
        s_wl = sem("weight_unit_lo")
        s_wu = sem("weight_unit_used")
        s_si = sem("silu_ready")
        s_hm = sem("hidden_ready")
        s_ht = sem("hidden_transposed")
        s_hh = sem("hidden_hi")
        s_hl = sem("hidden_lo")
        s_rl = sem("router_ready")
        s_rc = sem("router_chain")
        s_re = sem("router_exp_ready")
        s_rp = sem("positions_ready")
        s_rr = sem("rounds_ready")
        s_xq = sem("xn_token_major_ready")
        s_xqc = sem("xn_token_major_copied")
        s_g = sem("gather_ready")
        s_gw = sem("gather_weighted")
        s_xg = sem("tokens_gathered")
        s_xgc = sem("tokens_gathered_copied")
        s_edc = sem("expert_down_copied")
        s_st = sem("scatter_transposed")
        s_stc = sem("scatter_copied")
        s_eo = sem("expert_out_tile")
        s_ea = sem("expert_out_added")
        s_pos = sem("places_shifted")
        s_pl = sem("ple_tile_ready")
        s_pg = sem("ple_gate_ready")
        s_pt = sem("ple_term_ready")
        s_out = sem("out_written")
        s_step = sem("pool_step")

        def wait_block(eng, r, j):
            eng.wait_ge(s_loaded[j % RING], (r + (j // RING + 1)) * 16)

        def load_block(eng, j, src, used=None):
            if used is not None:
                eng.wait_ge(*used)
            eng.dma_start(ring[:, j % RING, :], src).then_inc(s_loaded[j % RING], 16)

        def skip_block(eng, j, used):
            if used is not None:
                eng.wait_ge(*used)
            eng.sem_inc(s_loaded[j % RING], 16)

        def mixer_used(l, j):
            if j < PROJ_BLOCKS:
                return s_pj, l * N_PROJ + (2 * j + 2 + (1 if j >= 9 else 0))
            if j < PROJ_BLOCKS + N_BRANCHES * BRANCH_BLOCKS:
                b, k = divmod(j - PROJ_BLOCKS, BRANCH_BLOCKS)
                return s_br, l * (N_BRANCHES * KT) + (b * KT + (2, 4, 4, 6, 8, 8)[k])
            return s_wo, l * KT + 2 * (j + 5 - MIX_BLOCKS)

        def split_used(block):
            return s_wl, 2 * block + (2 - 2 * RING)

        def ple_used(l, j):
            return s_pl, l * KT + (KT + (KT if j == PLE_BLOCKS - 1 else 2 * j + 2))

        def tile_w(j, half):
            return [ring[:, j % RING, k * COLS + half * P:k * COLS + half * P + P] for k in range(KT)]

        block = ctx.enter_context(nc.Block())

        @block.sync
        def _(sp):
            sp.dma_start(h[:, :, :], x).then_inc(s_x, 16)
            sp.dma_start(cst[:, :], cst_in).then_inc(s_cst, 16)

            def load_ple(l, used):
                for j in range(PLE_BLOCKS):
                    load_block(sp, j, wp[l, j], used(j))
                for j in range(PLE_BLOCKS, RING):
                    skip_block(sp, j, used(j))

            with sp.Fori(0, DEPTH) as l:
                for j in range(MIX_BLOCKS):
                    if j < PLE_BLOCKS:
                        used = ple_used(l - 1, j)
                    else:
                        used = mixer_used(l, j - RING) if j >= RING else None
                    load_block(sp, j, wm[l, j], used)
                for j in range(MIX_BLOCKS, MIX_ROUNDS * RING):
                    skip_block(sp, j, mixer_used(l, j - RING))

                def first_used(j):
                    at = MIX_ROUNDS * RING - RING + j
                    return mixer_used(l, at) if at < MIX_BLOCKS else None

                with sp.If(l < 1):
                    for j in range(RING):
                        load_block(sp, j, wd[j], first_used(j))
                    with sp.Fori(1, DENSE_CHUNKS // 2) as i:
                        for j in range(RING):
                            load_block(sp, j, wd[i * RING + j], split_used(i * RING + j))
                    for j in range(3):
                        load_block(sp, j, wd[DENSE_CHUNKS // 2 * RING + j], split_used(DENSE_BLOCKS - 3 + j))
                    for j in range(3, RING):
                        skip_block(sp, j, split_used(DENSE_BLOCKS - 3 + j))
                    load_ple(0, lambda j: split_used(DENSE_BLOCKS + 3 + j) if j < 3 else None)
                with sp.Else():
                    for j in range(RING):
                        load_block(sp, j, we[j], first_used(j))
                    with sp.Fori(1, N_EXPERTS * PASS_ROUNDS) as i:
                        for j in range(RING):
                            load_block(sp, j, we[i * RING + j], split_used(i * RING + (DENSE_BLOCKS + j)))
                    sp.wait_ge(s_rr, 1)
                    n = sp.value_load(rounds[0:1, 0:1], min_val=1, max_val=2)
                    all_blocks = N_EXPERTS * PASS_ROUNDS * RING
                    with sp.If(n > 1):
                        with sp.Fori(0, N_EXPERTS * PASS_ROUNDS) as i:
                            for j in range(RING):
                                load_block(sp, j, we[i * RING + j],
                                           split_used(i * RING + (DENSE_BLOCKS + all_blocks + j)))
                        load_ple(1, lambda j: split_used(DENSE_BLOCKS + 2 * all_blocks + j))
                    with sp.Else():
                        load_ple(1, lambda j: split_used(DENSE_BLOCKS + all_blocks + j))
            sp.wait_ge(s_xn, KT * (2 * DEPTH + 1))
            sp.dma_start(out, xn[:, :, :]).then_inc(s_out, 16)
            sp.wait_ge(s_out, 16)

        @block.tensor
        def _(pe):
            def chain(dst, lhs, rhs):
                for k, (a, b) in enumerate(zip(lhs, rhs)):
                    m = pe.matmul(dst, a, b, start=k == 0, stop=k == len(lhs) - 1)
                return m

            def norm_sum(k):
                pe.wait_ge(s_sq, k * 2 + 1)
                for j in range(KT):
                    if j == KT // 2:
                        pe.wait_ge(s_sq, k * 2 + 2)
                    m = pe.matmul(bank(7, 0, SEQ), con("ones"), mix[:, j, :], start=j == 0, stop=j == KT - 1)
                m.then_inc(s_ms, 1)

            def project(l):
                r = l * LAYER0_ROUNDS
                base = l * N_PROJ

                def room(t):
                    if t >= 4:
                        pe.wait_ge(s_pf, base + (t - 3))

                def feature_major(j, t):
                    wait_block(pe, r, j)
                    for half in range(2):
                        room(t + half)
                        m = chain(bank((t + half) % 4, 0, SEQ), tile_w(j, half), [xn[:, k, :] for k in range(KT)])
                        m.then_inc(s_pj, 1)

                def token_major(j, t):
                    wait_block(pe, r, j)
                    for tt in range(TT):
                        room(t + tt)
                        m = chain(bank((t + tt) % 4, 0, COLS), [xn[:, k, tt * P:tt * P + P] for k in range(KT)],
                                  [ring[:, j % RING, k * COLS:(k + 1) * COLS] for k in range(KT)])
                        m.then_inc(s_pj, 1)

                pe.wait_ge(s_xn, l * (2 * KT) + KT)
                t = 0
                for j in range(7):
                    feature_major(j, t)
                    t += 2
                for j in range(7, 9):
                    token_major(j, t)
                    t += 2
                room(t)
                for tt in range(TT):
                    m = chain(bank(t % 4, tt * DT, DT), [xn[:, k, tt * P:tt * P + P] for k in range(KT)],
                              [par("w_dt", k * DT, DT) for k in range(KT)])
                m.then_inc(s_pj, 1)
                t += 1
                for j in range(9, 11):
                    feature_major(j, t)
                    t += 2
                assert t == T_V
                for j in range(11, 17):
                    token_major(j, t)
                    t += 2
                    if j == 13:
                        conv_norm(l, 0)
                    if j == 15:
                        conv_norm(l, 1)
                assert t == T_Q

            def query_key(l, i, t):
                j = 17 + t // 2
                if t % 2 == 0:
                    wait_block(pe, l * LAYER0_ROUNDS + i, j)
                pe.wait_ge(s_pf, l * N_PROJ + i * 12 + (T_Q + t - 3))
                chain(bank(4 + t % 4, 0, SEQ), tile_w(j, t % 2),
                      [xn[:, k, :] for k in range(KT)]).then_inc(s_pj, 1)

            def fnet(l):
                pe.wait_ge(s_pf, l * N_PROJ + T_Q)
                for g in range(FNET_GROUPS):
                    if g >= 2:
                        pe.wait_ge(s_f1c, l * FNET_GROUPS + (g - 1))
                    for tt in range(TT):
                        m = pe.matmul(bank(4 + g % 2, tt * 2 * P, 2 * P), fu[:, g, tt * P:tt * P + P],
                                      con("dft_ch", 0, 2 * P), start=True, stop=True)
                    m.then_inc(s_f1, 1)
                    if g >= 1:
                        fnet_tokens(l, g - 1)
                fnet_tokens(l, FNET_GROUPS - 1)

            def fnet_tokens(l, g):
                pe.wait_ge(s_f1c, l * FNET_GROUPS + (g + 1))
                if g >= 2:
                    pe.wait_ge(s_f2c, l * FNET_GROUPS + (g - 1))
                lhs = [fa[:, g % 2, tt, part * P:part * P + P] for part in range(2) for tt in range(TT)]
                rhs = [con(name, tt * SEQ, SEQ) for name in ("dft_cos", "dft_sin") for tt in range(TT)]
                chain(bank(6 if g % 2 == 0 else 3, 0, SEQ), lhs, rhs).then_inc(s_f2, 1)

            def conv_norm(l, second):
                if second:
                    pe.wait_ge(s_lnc, l * 5 + 2)
                else:
                    pe.wait_ge(s_cvw, l * (CT * CONV_K) + CT * CONV_K)
                chain(bank(7, second * SEQ, SEQ), [con("ones")] * CT, [cv[:, t, :] for t in range(CT)]).then_inc(s_lns, 1)

            def ssm_prep(l):
                pe.wait_ge(s_xa, l * XT + XT)
                pe.wait_ge(s_f1c, l * FNET_GROUPS + FNET_GROUPS)
                for tt in range(TT):
                    for c in range(CT):
                        m = pe.transpose(bank(4 + tt, c * P, P), xbc[:, c, tt * P:tt * P + P], con("ident"))
                    m.then_inc(s_xt, 1)
                pe.wait_ge(s_f2c, l * FNET_GROUPS + FNET_GROUPS)
                for g in range(SSM_GROUPS):
                    if g == 1:
                        pe.wait_ge(s_lnc, l * 5 + 3)
                    lo = g * SSM_STATE
                    for tt in range(TT):
                        m = pe.matmul(bank(6 + g, tt * SEQ, SEQ), xbc[lo:lo + SSM_STATE, CT, tt * P:tt * P + P],
                                      xbc[lo:lo + SSM_STATE, CT + 1, :], start=True, stop=True)
                    m.then_inc(s_bc, 1)

            def ssm_heads(l):
                with pe.Fori(0, 2) as i:
                    pe.wait_ge(s_pf, l * N_PROJ + T_Q)
                    pe.wait_ge(s_xtc, l * TT + TT)
                    pe.wait_ge(s_sc, l * 2 + 2)
                    for step in range(2):
                        n = l * SSM_HEADS + i * 4 + 2 * step
                        for g in range(SSM_GROUPS):
                            pe.wait_ge(s_ua, n + (g + 1))
                            for part in range(4):
                                m = pe.matmul(bank(g, part * P, P), con("ones"), ua[:, g, part, :], start=True, stop=True)
                            m.then_inc(s_r, 1)
                        for t in range(4):
                            query_key(l, i, 4 * step + t)
                        for g in range(SSM_GROUPS):
                            pe.wait_ge(s_mm, n + (g + 1))
                            for tt, parts in enumerate((((0, 0), (3, 0), (4, 1)), ((1, 0), (2, 1), (5, 1)))):
                                m = chain(bank(2 + g, tt * 64, 64), [mm_[:, g, b, :] for b, _ in parts],
                                          [xs[:, s, bass.ds(i * P + (step * 64 + g * 256), 64)] for _, s in parts])
                            m.then_inc(s_y, 1)
                    for t in range(8, 12):
                        query_key(l, i, t)

            def ssm_out(l):
                pe.wait_ge(s_yc, l * SSM_YC + SSM_YC)
                pe.wait_ge(s_pf, l * N_PROJ + N_PROJ)
                for c in range(CT):
                    for tt in range(TT):
                        m = pe.transpose(bank(4 + c // 2, (c % 2) * SEQ + tt * P, P), ys[:, tt, c * P:c * P + P],
                                         con("ident"))
                m.then_inc(s_yt, 1)

            def branch_tile(l, b, m_):
                r = l * LAYER0_ROUNDS + b
                out_j = PROJ_BLOCKS + 3 * (m_ // 4) + 1
                j = out_j + (1 if m_ % 4 >= 2 else -1)
                if m_ % 2 == 0:
                    wait_block(pe, r, j)
                if m_ % 4 == 0:
                    wait_block(pe, r, out_j)
                pe.wait_ge(s_bm, l * (N_BRANCHES * KT) + b * KT + (m_ + 1))
                col = (m_ % 4) * P
                chain(bank(6 + m_ % 2, 0, SEQ),
                      [ring[:, out_j % RING, c * 512 + col:c * 512 + col + P] for c in range(CT)],
                      [ybr[:, b * CT + c, :] for c in range(CT)])
                chain(bank(6 + m_ % 2, SEQ, SEQ), tile_w(j, m_ % 2), [xn[:, k, :] for k in range(KT)]).then_inc(s_br, 1)

            def pair(l, i, half):
                n = l * UNITS + i * 8 + 4 * half
                pe.wait_ge(s_qkp, l * (2 * HP) + i * 4 + (2 * half + 2))

                def scores(u):
                    lo = 64 * (u // TT)
                    if u:
                        pe.wait_ge(s_sb, n + u)
                    for g in range(ATT_GROUPS):
                        m = pe.matmul(bank(4, g * SEQ, SEQ),
                                      qkp[lo:lo + 64, 0, g, (u % TT) * P:(u % TT) * P + P],
                                      qkp[lo:lo + 64, 1, g, :], start=True, stop=True)
                    m.then_inc(s_s, 1)

                def transposes(u):
                    pe.wait_ge(s_e, n + (u + 1))
                    if u >= 2:
                        pe.wait_ge(s_oc, n + (u - 1))
                    for b in range(2 * ATT_GROUPS):
                        m = pe.transpose(bank(2 * (u % 2), b * P, P), sa[:, u % 2, b * P:b * P + P], con("ident"))
                    m.then_inc(s_t, 1)

                def values(u):
                    pe.wait_ge(s_tc, n + (u + 1))
                    chain(bank(2 * (u % 2), GK, 64), [pt[:, u % 2, b * P:b * P + P] for b in range(6)],
                          [v[:, b % 2, bass.ds(i * (2 * P) + (half * P + b // 2 * ATT_WIDTH + 64 * (u // TT)), 64)]
                           for b in range(6)]).then_inc(s_o, 1)

                def tile(k):
                    branch_tile(l, i, 4 * half + k)

                scores(0)
                tile(0)
                scores(1)
                transposes(0)
                tile(1)
                scores(2)
                transposes(1)
                values(0)
                tile(2)
                scores(3)
                values(1)
                transposes(2)
                tile(3)
                transposes(3)
                values(2)
                values(3)

            def attention(l):
                with pe.Fori(0, HB) as i:
                    pe.wait_ge(s_ybs, l + 1)
                    pe.wait_ge(s_yc, l * SSM_YC + 1)
                    pe.wait_ge(s_lna, l * (CT + 1) + (CT + 1))
                    for half in range(2):
                        pair(l, i, half)
                pe.wait_ge(s_oc, l * UNITS + UNITS)
                for c in range(CT):
                    for tt in range(TT):
                        m = pe.transpose(bank(4 + c // 2, (c % 2) * SEQ + tt * P, P), ao[:, tt, c * P:c * P + P],
                                         con("ident"))
                m.then_inc(s_ot, 1)

            def branches(l):
                with pe.Fori(HB, N_BRANCHES) as b:
                    pe.wait_ge(s_yba, l + 1)
                    for m_ in range(KT):
                        branch_tile(l, b, m_)

            def mix_out(l):
                n = l * (N_BRANCHES * KT)
                pe.wait_ge(s_bm, n + (N_BRANCHES * KT + 2))
                r = l * LAYER0_ROUNDS
                for jj in range(4):
                    j = MIX_BLOCKS - 4 + jj
                    wait_block(pe, r, j)
                    for half in range(2):
                        m_ = 2 * jj + half
                        m = chain(bank(m_, 0, SEQ), tile_w(j, half), [mix[:, k, :] for k in range(KT)])
                        m.then_inc(s_wo, 1)

            def three(dst, lhs, rhs, first, last):
                pe.matmul(dst, lhs[0], rhs[0], start=first, stop=False, skip_group_check=True)
                pe.matmul(dst, lhs[0], rhs[1], start=False, stop=False, skip_group_check=True)
                return pe.matmul(dst, lhs[1], rhs[0], start=False, stop=last, skip_group_check=True)

            def both(hi, lo, *at):
                return hi[at], lo[at]

            def dense():
                def up(c, slot, units):
                    if c is not None:
                        pe.wait_ge(s_hm, c)
                    for u in range(4):
                        pe.wait_ge(s_wl, units + (u + 1))
                        for k in (2 * u, 2 * u + 1):
                            if slot == 0 and c is None and k % 2 == 0:
                                pe.wait_ge(s_xl, u + 1)
                            for t in range(4):
                                col = (k % 2) * 512 + t * P
                                m = three(bank(t, 0, SEQ), both(whi, wlo, slice(None), (slot + u) % SLOTS,
                                                                slice(col, col + P)),
                                          both(xhi, xlo, slice(None), k), k == 0, k == KT - 1)
                        m.then_inc(s_wu, 1)

                def down(c, slot, units, par_, first=False, last=False):
                    pe.wait_ge(s_hl, c + 1)
                    for half in range(2):
                        pe.wait_ge(s_wl, units + (half + 1))
                        for m_ in range(KT):
                            m = three(bank(4 + m_ // 2, (m_ % 2) * SEQ, SEQ),
                                      both(whi, wlo, slice(None), (slot + half) % SLOTS, slice(m_ * P, m_ * P + P)),
                                      both(hhi, hlo, slice(None), par_, half),
                                      first and half == 0 and m_ % 2 == 0, last and half == 1)
                        m.then_inc(s_wu, 1)

                up(None, 0, 0)
                up(1, 4, 4)
                down(0, 2, 8, 0, first=True)
                with pe.Fori(0, (DENSE_CHUNKS - 3) // 2) as i:
                    for c in range(2):
                        up(i * 2 + (c + 2), 4, i * 12 + (10 + 6 * c))
                        down(i * 2 + (c + 1), 2, i * 12 + (14 + 6 * c), (c + 1) % 2)
                c = DENSE_CHUNKS - 2
                up(c + 1, 4, 6 * c + 4)
                down(c, 2, 6 * c + 8, c % 2)
                down(c + 1, 4, 6 * c + 10, (c + 1) % 2, last=True)

            def route():
                pe.wait_ge(s_xn, 4 * KT)
                for tt in range(TT):
                    m = chain(bank(4, tt * N_EXPERTS, N_EXPERTS), [xn[:, k, tt * P:tt * P + P] for k in range(KT)],
                              [par("router", k * N_EXPERTS, N_EXPERTS) for k in range(KT)])
                m.then_inc(s_rl, 1)
                for tt in range(TT):
                    for k in range(KT):
                        m = pe.transpose(bank(2 * tt + k // 4, (k % 4) * P, P), xn[:, k, tt * P:tt * P + P], con("ident"))
                        if k % 4 == 3:
                            m.then_inc(s_xq, 1)
                pe.wait_ge(s_rc, RC_MASK)
                chain(bank(5, 0, N_EXPERTS), [con("before")], [msk[:, 0, :]])
                chain(bank(5, N_EXPERTS, N_EXPERTS), [con("ones"), con("before")], [msk[:, 0, :], msk[:, 1, :]])
                chain(bank(5, 2 * N_EXPERTS, N_EXPERTS), [con("ones")] * 2,
                      [msk[:, 0, :], msk[:, 1, :]]).then_inc(s_rp, 1)
                pe.wait_ge(s_xqc, 4)

            def experts(passes):
                pe.wait_ge(s_rr, 1)
                n_r = pe.value_load(rounds[0:1, 0:1], min_val=1, max_val=2)
                pe.reg_mov(passes, n_r * N_EXPERTS)
                with pe.Fori(0, n_r) as o:
                    with pe.Fori(0, N_EXPERTS) as e:
                        q = o * N_EXPERTS + e
                        pe.wait_ge(s_gw, q + 1)
                        pe.wait_ge(s_ea, q * KT + 2)
                        for k in range(KT):
                            m = chain(bank(6 + k // 4, (k % 4) * P, P),
                                      [mix[:, tt * 4 + k // 2, (k % 2) * P:(k % 2) * P + P] for tt in range(TT)],
                                      [gat[:, tt, :] for tt in range(TT)])
                            if k % 4 == 3:
                                m.then_inc(s_xg, 1)
                        c0 = q * EXP_CHUNKS + DENSE_CHUNKS
                        u0 = q * PASS_UNITS + DENSE_UNITS

                        def up(c, cc, units):
                            pe.wait_ge(s_hm, c - 1)
                            slot = 0 if cc == 0 else 4
                            for u in range(4):
                                pe.wait_ge(s_wl, units + (u + 1))
                                if cc == 0 and u % 2 == 0:
                                    pe.wait_ge(s_xl, q * 2 + (4 + u // 2 + 1))
                                for k in (2 * u, 2 * u + 1):
                                    col = (k % 2) * 512
                                    m = three(bank(cc % 2), both(xhi, xlo, slice(None), k, slice(0, P)),
                                              both(whi, wlo, slice(None), (slot + u) % SLOTS, slice(col, col + 512)),
                                              k == 0, k == KT - 1)
                                m.then_inc(s_wu, 1)
                                if cc > 0 and u == 1:
                                    turn(c - 1, cc - 1)

                        def turn(c, cc):
                            pe.wait_ge(s_hm, c + 1)
                            for half in range(2):
                                m = pe.transpose(bank(2 + cc % 2, half * P, P), gt[:, 0, half * P:half * P + P], con("ident"))
                            m.then_inc(s_ht, 1)

                        def down(c, cc, slot, units):
                            pe.wait_ge(s_hl, c + 1)
                            for half in range(2):
                                pe.wait_ge(s_wl, units + (half + 1))
                                for col in range(0, D_MODEL, 512):
                                    m = three(bank(4 + col // 512), both(hhi, hlo, slice(None), cc % 2, half, slice(0, P)),
                                              both(whi, wlo, slice(None), (slot + half) % SLOTS, slice(col, col + 512)),
                                              cc == 0 and half == 0, cc == EXP_CHUNKS - 1 and half == 1)
                                m.then_inc(s_wu, 1)

                        up(c0, 0, u0)
                        pe.wait_ge(s_xgc, q * 2 + 2)
                        pe.wait_ge(s_xl, q * 2 + (4 + 2))
                        for tt in range(TT):
                            m = pe.transpose(bank(6, tt * P, P), gatw[:, tt, :], con("ident"))
                        m.then_inc(s_st, 1)
                        up(c0 + 1, 1, u0 + 4)
                        pe.wait_ge(s_edc, q + 1)
                        down(c0, 0, 2, u0 + 8)
                        with pe.Fori(0, (EXP_CHUNKS - 2) // 2) as i:
                            for c in range(2):
                                up(c0 + (i * 2 + (c + 2)), 2 + c, u0 + (i * 12 + (10 + 6 * c)))
                                down(c0 + (i * 2 + (c + 1)), 1 + c, 2, u0 + (i * 12 + (14 + 6 * c)))
                        c = EXP_CHUNKS - 1
                        turn(c0 + c, c)
                        down(c0 + c, c, 4, u0 + (PASS_UNITS - 2))
                        pe.wait_ge(s_edc, q + 2)
                        pe.wait_ge(s_stc, q + 1)
                        for m_ in range(KT):
                            pe.wait_ge(s_ea, q * KT + (m_ + 1))
                            pe.matmul(bank(6 + m_ % 2, 0, SEQ), yx[:, m_ * P:m_ * P + P], sca[:, :],
                                      start=True, stop=True).then_inc(s_eo, 1)

            def ple(l, passes):
                pe.wait_ge(s_h, l * 3 + 3)
                r = l * (LAYER0_ROUNDS - DENSE_ROUNDS) + pe.snap(passes, min_val=0, max_val=16) * PASS_ROUNDS \
                    + (MIX_ROUNDS + DENSE_ROUNDS)
                wait_block(pe, r, 4)
                for m_ in range(KT):
                    if m_ % 2 == 0:
                        wait_block(pe, r, m_ // 2)
                    if m_ >= 2:
                        pe.wait_ge(s_pt, l * KT + (m_ - 1))
                    chain(bank(2 * (m_ % 2), 0, SEQ), [ring[:, 4, c * D_MODEL + m_ * P:c * D_MODEL + m_ * P + P]
                                                      for c in range(PLE_DIM // P)],
                          [par("p", c * SEQ, SEQ) for c in range(PLE_DIM // P)])
                    m = chain(bank(2 * (m_ % 2) + 1, 0, SEQ), tile_w(m_ // 2, m_ % 2), [h[:, k, :] for k in range(KT)])
                    m.then_inc(s_pl, 1)

            pe.sem_inc(s_pl, KT)
            pe.sem_inc(s_wu, SLOTS)
            pe.sem_inc(s_r, 2)
            pe.sem_inc(s_s, 1)
            passes = pe.alloc_register("passes_pe")
            pe.wait_ge(s_relL, 32)
            for g in range(ATT_GROUPS):
                m = pe.matmul(ps[0:ATT_HEADS, g * 512:g * 512 + 512],
                              relb_sb[:, g * ATT_HEADS:(g + 1) * ATT_HEADS],
                              onehot_sb[:, g, :], start=True, stop=True)
            m.then_inc(s_relT, 1)
            pe.wait_ge(s_cst, 16)
            with pe.Fori(0, DEPTH) as l:
                norm_sum(l * 2)
                pe.wait_ge(s_pk, l * 16 + 16)
                project(l)
                fnet(l)
                ssm_prep(l)
                ssm_heads(l)
                ssm_out(l)
                attention(l)
                branches(l)
                mix_out(l)
                pe.wait_ge(s_h, l * 3 + 2)
                norm_sum(l * 2 + 1)
                pe.reg_mov(passes, 0)
                with pe.If(l < 1):
                    dense()
                with pe.Else():
                    route()
                    experts(passes)
                ple(l, passes)
            norm_sum(2 * DEPTH)

        @block.scalar
        def _(act):
            def norm_squares(k, ready):
                act.wait_ge(s_h, ready)
                for half in range(2):
                    sl = slice(half * KT // 2, (half + 1) * KT // 2)
                    act.activation(mix[:, sl, :], h[:, sl, :], ACT.Square).then_inc(s_sq, 1)
                act.wait_ge(s_var, k + 1)
                act.activation(rms_t[:, 1, :], rms_t[:, 0, :], ACT.Sqrt).then_inc(s_sd, 1)

            def project(l):
                base = l * N_PROJ

                def tile(t, dst, func=ACT.Copy, rows=(0, SEQ)):
                    act.wait_ge(s_pj, base + (t + 1))
                    act.activation(dst, bank(t % 4, *rows), func).then_inc(s_pf, 1)

                for pair in range(2):
                    for c in range(2):
                        tile(4 * pair + c, glu_a[:, pair, c, :])
                    for c in range(2):
                        tile(4 * pair + 2 + c, glu_s[:, pair, c, :], ACT.Sigmoid)
                for c in range(XT):
                    tile(T_XBC + c, xbcp[:, c, SPAD:SPAD + SEQ])
                for j in range(2):
                    for tt in range(TT):
                        tile(T_Z + 2 * j + tt, z[:, tt, j * COLS:(j + 1) * COLS], ACT.Silu)
                tile(T_DT, dts[:, 0, :], rows=(0, TT * DT))
                for g in range(FNET_GROUPS):
                    tile(T_FN + g, fu[:, g, :])
                for j in range(6):
                    if j == 4:
                        ssm(l)
                        dt_exps(l)
                    for tt in range(TT):
                        tile(T_V + 2 * j + tt, v[:, tt, j * COLS:(j + 1) * COLS])

            def dt_exps(l):
                act.wait_ge(s_dtc, l * DTC + 3)
                act.activation(dts[:, 3, :], dts[:, 2, :], ACT.Exp).then_inc(s_dta, 1)
                act.activation(a_neg[:, :], par("a_log", 0, DT), ACT.Exp).then_inc(s_dta, 1)

            def fnet(l):
                for g in range(FNET_GROUPS):
                    act.wait_ge(s_f1, l * FNET_GROUPS + (g + 1))
                    if g >= 2:
                        act.wait_ge(s_f2, l * FNET_GROUPS + (g - 1))
                    act.activation(fa[:, g % 2, :, :], bank(4 + g % 2).rearrange("p (t c) -> p t c", t=TT),
                                   ACT.Copy).then_inc(s_f1c, 1)
                    if g >= 1:
                        fnet_tokens(l, g - 1)
                fnet_tokens(l, FNET_GROUPS - 1)

            def fnet_tokens(l, g):
                act.wait_ge(s_f2, l * FNET_GROUPS + (g + 1))
                act.activation(ybr[:, FNET * CT + g, :], bank(6 if g % 2 == 0 else 3, 0, SEQ),
                               ACT.Copy).then_inc(s_f2c, 1)

            def ssm(l):
                for c in range(XT):
                    act.wait_ge(s_xc, l * (XT * SSM_CONV) + (c + 1) * SSM_CONV)
                    act.activation(xbc[:, c, :], xbc[:, c, :], ACT.Silu).then_inc(s_xa, 1)

            def conv_norm(l):
                act.wait_ge(s_lnc, l * 5 + 3)
                act.activation(rms_t[:, 1, :], rms_t[:, 0, :], ACT.Sqrt).then_inc(s_lna, 1)
                act.wait_ge(s_lnc, l * 5 + 5)
                for c in range(CT):
                    act.activation(ybr[:, CONV * CT + c, :], cvx[:, c, :], ACT.Silu, bias=par("ln_b", c),
                                   scale=par("ln_g", c)).then_inc(s_lna, 1)

            def ssm_heads(l):
                for tt in range(TT):
                    act.wait_ge(s_xt, l * TT + (tt + 1))
                    act.activation(xs[:, tt, :], bank(4 + tt), ACT.Copy).then_inc(s_xtc, 1)
                with act.Fori(0, 2) as i:
                    def query_key(t):
                        act.wait_ge(s_pj, l * N_PROJ + i * 12 + (T_Q + t + 1))
                        act.activation(qk[:, bass.ds(i * ATT_GROUPS + t // HP, 1), t % HP, :], bank(4 + t % 4, 0, SEQ),
                                       ACT.Copy).then_inc(s_pf, 1)

                    for step in range(2):
                        n = l * SSM_HEADS + i * 4 + 2 * step
                        for g in range(SSM_GROUPS):
                            query_key(4 * step + g)
                            act.wait_ge(s_hc, (n + g) * SSM_HC + SSM_HC)
                            act.activation(ex[:, g, :, :], ex[:, g, :, :], ACT.Exp).then_inc(s_ex, 1)
                        query_key(4 * step + 2)
                        query_key(4 * step + 3)
                    for t in range(8, 12):
                        query_key(t)
                act.wait_ge(s_yc, l * SSM_YC + 4)
                act.activation(yst[:, 4:6], yst[:, 2:4], ACT.Sqrt).then_inc(s_ya, 1)
                act.wait_ge(s_yt, l + 1)
                for c in range(CT):
                    m = act.activation(ybr[:, SSM * CT + c, :], bank(4 + c // 2, (c % 2) * SEQ, SEQ), ACT.Copy,
                                       scale=par("ssm_norm", c))
                m.then_inc(s_ybs, 1)

            def gate(l, b, m_):
                n = l * (N_BRANCHES * KT) + b * KT
                act.wait_ge(s_br, n + (m_ + 1))
                act.wait_ge(s_bm, n + (m_ + 1))
                act.activation(gs[:, m_ % 2, :], bank(6 + m_ % 2, SEQ, SEQ), ACT.Sigmoid,
                               bias=pk[:, bass.ds(b * KT + (AT["b_gate"] + m_), 1)]).then_inc(s_sg, 1)

            def pair(l, i, half):
                n = l * UNITS + i * 8 + 4 * half

                def probs(u):
                    act.wait_ge(s_am, n + (u + 1))
                    act.activation(sa[:, u % 2, :], sa[:, u % 2, :], ACT.Exp, bias=ast[:, u % 2, 0:1],
                                   accum_out=ast[:, u % 2, 1:2]).then_inc(s_e, 1)

                def copy_t(u):
                    act.wait_ge(s_t, n + (u + 1))
                    act.activation(pt[:, u % 2, :], bank(2 * (u % 2), 0, GK), ACT.Copy).then_inc(s_tc, 1)

                def tile(k):
                    gate(l, i, 4 * half + k)

                probs(0)
                tile(0)
                probs(1)
                copy_t(0)
                tile(1)
                copy_t(1)
                probs(2)
                tile(2)
                probs(3)
                copy_t(2)
                tile(3)
                copy_t(3)

            def attention(l):
                with act.Fori(0, HB) as i:
                    for half in range(2):
                        pair(l, i, half)
                act.wait_ge(s_ot, l + 1)
                for j in range(2):
                    m = act.activation(ybr[:, ATT * CT + 2 * j:ATT * CT + 2 * j + 2, ::-1],
                                       bank(4 + j).rearrange("p (c t) -> p c t", c=2), ACT.Copy)
                m.then_inc(s_yba, 1)

            def branches(l):
                with act.Fori(HB, N_BRANCHES) as b:
                    for m_ in range(KT):
                        gate(l, b, m_)

            def high(units, first, u, r, j):
                slot = (first + u) % SLOTS
                act.wait_ge(s_loaded[j % RING], (r + (j // RING + 1)) * 16)
                act.wait_ge(s_wu, units + (u + 1))
                lo = (first + u) % 2 * UNIT
                act.activation(whi[:, slot, :], ring[:, j % RING, lo:lo + UNIT], ACT.Copy).then_inc(s_wh, 1)

            def highs(units, first, n, r, j):
                for u in range(n):
                    high(units, first, u, r, j + (first % 2 + u) // 2)

            def dense():
                for k in range(4):
                    act.wait_ge(s_xn, 2 * KT)
                    act.activation(xhi[:, 2 * k:2 * k + 2, :], xn[:, 2 * k:2 * k + 2, :], ACT.Copy).then_inc(s_xh, 1)
                highs(0, 0, 8, MIX_ROUNDS, 0)

                def chunk(c, par_, n, units, r, j, first=False):
                    act.wait_ge(s_wu, (4 if first else c * 6 + 2) + SLOTS)
                    if not first:
                        act.wait_ge(s_hm, c)
                    act.activation(hs[:, :, :], ps[:, 0:1024].rearrange("p (b t) -> p b t", b=2)[:, :, 0:SEQ],
                                   ACT.Silu).then_inc(s_si, 1)
                    if n:
                        highs(units, 2, 1, r, j)
                    act.wait_ge(s_hm, c + 1)
                    act.activation(hhi[:, par_, :, :], hid[:, :, :], ACT.Copy).then_inc(s_hh, 1)
                    for u in range(1, n):
                        high(units, 2, u, r, j + u // 2)

                chunk(0, 0, 6, 8, MIX_ROUNDS, 4, first=True)
                with act.Fori(0, (DENSE_CHUNKS - 3) // 2) as i:
                    for c in range(2):
                        chunk(i * 2 + (c + 1), (c + 1) % 2, 6, i * 12 + (14 + 6 * c), i + MIX_ROUNDS, 7 + 3 * c)
                c = DENSE_CHUNKS - 2
                chunk(c, c % 2, 4, 8 + 6 * c, MIX_ROUNDS, 4 + 3 * c)
                chunk(c + 1, (c + 1) % 2, 0, 0, 0, 0)

            def route():
                act.wait_ge(s_rc, RC_EXP)
                act.activation(rt[:, :, 1:2], rt[:, :, 0:1], ACT.Exp).then_inc(s_re, 1)
                for j in range(4):
                    act.wait_ge(s_xq, j + 1)
                    tt, half = j // 2, j % 2
                    act.activation(mix[:, tt * 4 + half * 2:tt * 4 + half * 2 + 2, :],
                                   bank(2 * tt + half).rearrange("p (c t) -> p c t", c=2), ACT.Copy).then_inc(s_xqc, 1)

            def experts():
                act.wait_ge(s_rr, 1)
                n_r = act.value_load(rounds[0:1, 0:1], min_val=1, max_val=2)
                with act.Fori(0, n_r) as o:
                    with act.Fori(0, N_EXPERTS) as e:
                        q = o * N_EXPERTS + e
                        c0 = q * EXP_CHUNKS + DENSE_CHUNKS
                        u0 = q * PASS_UNITS + DENSE_UNITS
                        r = q * PASS_ROUNDS + (LAYER0_ROUNDS + MIX_ROUNDS)
                        highs(u0, 0, 4, r, 0)
                        for j in range(2):
                            act.wait_ge(s_xg, q * 2 + (j + 1))
                            act.activation(xhi[:, 4 * j:4 * j + 4, 0:P], bank(6 + j).rearrange("p (c t) -> p c t", c=4),
                                           ACT.Copy).then_inc(s_xgc, 1)
                        highs(u0 + 4, 4, 4, r, 2)
                        act.wait_ge(s_st, q + 1)
                        act.activation(sca[:, :], bank(6, 0, SEQ), ACT.Copy).then_inc(s_stc, 1)

                        def chunk(k, cc, n, j=0, rr=0):
                            act.wait_ge(s_wu, u0 + ((4 if cc == 0 else k * 6 + 2) + SLOTS))
                            act.wait_ge(s_hm, c0 + k)
                            act.activation(hs[:, 0, :], bank(cc % 2, 0, SEQ), ACT.Silu).then_inc(s_si, 1)
                            if n:
                                highs(u0 + (k * 6 + 8), 2, 2, rr, j)
                            act.wait_ge(s_ht, c0 + k + (1 - DENSE_CHUNKS))
                            act.activation(hhi[:, cc % 2, :, 0:P], bank(2 + cc % 2, 0, SEQ).rearrange(
                                "p (h t) -> p h t", h=2), ACT.Copy).then_inc(s_hh, 1)
                            for u in range(2, n):
                                high(u0 + (k * 6 + 8), 2, u, rr, j + u // 2)

                        chunk(0, 0, 6, 4, r)
                        with act.Fori(0, (EXP_CHUNKS - 4) // 2) as i:
                            for c in range(2):
                                chunk(i * 2 + (c + 1), c + 1, 6, 7 + 3 * c, r + i)
                        c = EXP_CHUNKS - 3
                        chunk(c, c, 6, 4 + 3 * c, r)
                        chunk(c + 1, c + 1, 4, 7 + 3 * c, r)
                        chunk(c + 2, c + 2, 0)
                        act.wait_ge(s_wu, u0 + (PASS_UNITS + SLOTS))
                        act.activation(yx[:, :], ps[:, 4 * 512:6 * 512], ACT.Copy).then_inc(s_edc, 1)

            def ple(l):
                for m_ in range(KT):
                    act.wait_ge(s_pl, l * KT + (KT + m_ + 1))
                    if m_ >= 2:
                        act.wait_ge(s_pt, l * KT + (m_ - 1))
                    act.activation(gs[:, m_ % 2, :], bank(2 * (m_ % 2) + 1, 0, SEQ), ACT.Sigmoid).then_inc(s_pg, 1)

            act.sem_inc(s_edc, 1)
            act.dma_start(relb_sb, relb).then_inc(s_relL, 16)
            act.dma_start(onehot_sb, onehot).then_inc(s_relL, 16)
            act.wait_ge(s_relT, 1)
            act.activation(rows_sb, ps[0:ATT_HEADS, 0:3 * 512].rearrange("p (g c) -> p g c", g=3),
                           ACT.Copy).then_inc(s_relC, 1)
            act.wait_ge(s_relC, 1)
            act.dma_start(scratch.ap(), rows_sb).then_inc(s_relW, 16)
            with act.Fori(0, DEPTH) as l:
                act.wait_ge(s_h, l * 3 + 1)
                act.dma_start(pk[:, :], pk_in[l]).then_inc(s_pk, 16)
                norm_squares(l * 2, l * 3 + 1)
                act.wait_ge(s_pk, l * 16 + 16)
                project(l)
                fnet(l)
                conv_norm(l)
                ssm_heads(l)
                attention(l)
                branches(l)
                norm_squares(l * 2 + 1, l * 3 + 2)
                with act.If(l < 1):
                    dense()
                with act.Else():
                    route()
                    experts()
                ple(l)
            norm_squares(2 * DEPTH, 3 * DEPTH + 1)

        @block.vector
        def _(dve):
            def norm(k, gain):
                dve.wait_ge(s_ms, k + 1)
                dve.tensor_scalar(rms_t[:, 0, :], bank(7, 0, SEQ), 1.0 / D_MODEL, EPS, ALU.mult,
                                  ALU.add).then_inc(s_var, 1)
                dve.wait_ge(s_sd, k + 1)
                dve.reciprocal(rstd[:, :], rms_t[:, 1, :]).then_inc(s_rs, 1)
                dve.wait_ge(s_rs, k + 1)
                for j in range(KT):
                    dve.scalar_tensor_tensor(out=xn[:, j, :], in0=h[:, j, :], scalar=par(gain, j), in1=rstd[:, :],
                                             op0=ALU.mult, op1=ALU.mult).then_inc(s_xn, 1)

            def depthwise(dst, src, taps, w, b, tiles, s, n):
                for tap in range(taps):
                    for c in range(tiles):
                        col = par(w, tap * tiles + c)
                        if tap == 0:
                            i = dve.tensor_scalar(dst[:, c, :], src[:, c, 0:SEQ], col, par(b, c), ALU.mult, ALU.add)
                        else:
                            dve.wait_ge(s, n + ((tap - 1) * tiles + c + 1))
                            i = dve.scalar_tensor_tensor(out=dst[:, c, :], in0=src[:, c, tap:tap + SEQ], scalar=col,
                                                         in1=dst[:, c, :], op0=ALU.mult, op1=ALU.add)
                        i.then_inc(s, 1)

            def ssm_conv(l):
                n = l * (XT * SSM_CONV)
                for c in range(XT):
                    dve.wait_ge(s_pf, l * N_PROJ + (T_XBC + c + 1))
                    for tap in range(SSM_CONV):
                        col = par("ssm_w", tap * XT + c)
                        if tap == 0:
                            i = dve.tensor_scalar(xbc[:, c, :], xbcp[:, c, 0:SEQ], col, par("ssm_b", c), ALU.mult, ALU.add)
                        else:
                            dve.wait_ge(s_xc, n + (c * SSM_CONV + tap))
                            i = dve.scalar_tensor_tensor(out=xbc[:, c, :], in0=xbcp[:, c, tap:tap + SEQ], scalar=col,
                                                         in1=xbc[:, c, :], op0=ALU.mult, op1=ALU.add)
                        i.then_inc(s_xc, 1)

            def time_steps(l):
                dve.wait_ge(s_pf, l * N_PROJ + (T_DT + 1))
                done = 0

                def link(i):
                    nonlocal done
                    done += 1
                    i.then_inc(s_dtc, 1)
                    dve.wait_ge(s_dtc, l * DTC + done)

                raw = dts[:, 0, :].rearrange("p (t d) -> p t d", t=TT)
                bias_t = par("dt_bias", 0, DT)
                for tt in range(TT):
                    i = dve.tensor_tensor(raw[:, tt, :], raw[:, tt, :], bias_t, ALU.add)
                    if tt == 0:
                        i.then_inc(s_dtc, 1)
                        done += 1
                    else:
                        link(i)
                link(dve.scalar_tensor_tensor(out=dts[:, 2, :], in0=dts[:, 0, :], scalar=-1.0, in1=dts[:, 0, :],
                                              op0=ALU.mult, op1=ALU.min))
                dve.wait_ge(s_dta, l * 2 + 1)
                link(dve.tensor_scalar(dts[:, 4, :], dts[:, 3, :], 2.0, None, ALU.add))
                link(dve.reciprocal(dts[:, 5, :], dts[:, 4, :]))
                link(dve.tensor_tensor(dts[:, 6, :], dts[:, 3, :], dts[:, 5, :], ALU.mult))
                link(dve.tensor_tensor(dts[:, 7, :], dts[:, 6, :], dts[:, 6, :], ALU.mult))
                link(dve.tensor_scalar(dts[:, 1, :], dts[:, 7, :], 1.0 / 17, None, ALU.mult))
                for c in range(15, 1, -2):
                    link(dve.scalar_tensor_tensor(out=dts[:, 1, :], in0=dts[:, 1, :], scalar=1.0 / c,
                                                  in1=dts[:, 7, :], op0=ALU.add, op1=ALU.mult))
                link(dve.scalar_tensor_tensor(out=dts[:, 1, :], in0=dts[:, 1, :], scalar=1.0, in1=dts[:, 6, :],
                                              op0=ALU.add, op1=ALU.mult))
                link(dve.tensor_scalar(dts[:, 2, :], dts[:, 0, :], 0.0, None, ALU.max))
                dt_flat = dt_[:, :, :].rearrange("p t d -> p (t d)")
                link(dve.scalar_tensor_tensor(out=dt_flat, in0=dts[:, 1, :], scalar=2.0, in1=dts[:, 2, :],
                                              op0=ALU.mult, op1=ALU.add))
                dve.wait_ge(s_dta, l * 2 + 2)
                for tt in range(TT):
                    i = dve.scalar_tensor_tensor(out=dta[:, tt, :], in0=dt_[:, tt, :], scalar=-1.0, in1=a_neg[:, :],
                                                 op0=ALU.mult, op1=ALU.mult)
                    i.then_inc(s_dtc, 1)
                    done += 1
                assert done == DTC, done

            def conv(l):
                dve.wait_ge(s_glu, l * 2 + 2)
                depthwise(cv, glu, CONV_K, "conv_dw", "conv_b", CT, s_cvw, l * (CT * CONV_K))

            def conv_norm(l):
                dve.wait_ge(s_lns, l * 2 + 1)
                for c in range(CT):
                    i = dve.scalar_tensor_tensor(out=cvx[:, c, :], in0=bank(7, 0, SEQ), scalar=-1.0 / CONV_CH,
                                                 in1=cv[:, c, :], op0=ALU.mult, op1=ALU.add)
                i.then_inc(s_lnc, 1)
                dve.wait_ge(s_lnc, l * 5 + 1)
                dve.tensor_tensor(cv[:, :, :], cvx[:, :, :], cvx[:, :, :], ALU.mult).then_inc(s_lnc, 1)
                dve.wait_ge(s_lns, l * 2 + 2)
                dve.tensor_scalar(rms_t[:, 0, :], bank(7, SEQ, SEQ), 1.0 / CONV_CH, EPS, ALU.mult,
                                  ALU.add).then_inc(s_lnc, 1)
                dve.wait_ge(s_lna, l * (CT + 1) + 1)
                dve.reciprocal(rstd[:, :], rms_t[:, 1, :]).then_inc(s_lnc, 1)
                dve.wait_ge(s_lnc, l * 5 + 4)
                for c in range(CT):
                    i = dve.tensor_tensor(cvx[:, c, :], cvx[:, c, :], rstd[:, :], ALU.mult)
                i.then_inc(s_lnc, 1)

            def ssm_scores(l):
                for g in range(SSM_GROUPS):
                    dve.wait_ge(s_bc, l * 2 + (g + 1))
                    src = bank(6 + g)
                    dve.tensor_tensor(sc[:, g, 0, :], src[:, 0:P], con("upto"), ALU.mult)
                    dve.tensor_copy(sc[:, g, 1, :], src[:, P:2 * P])
                    dve.tensor_tensor(sc[:, g, 2, :], src[:, 3 * P:4 * P], con("upto"), ALU.mult)
                    dve.tensor_tensor(sc[:, g, 3, :], src[:, 0:P], con("from"), ALU.mult)
                    dve.tensor_copy(sc[:, g, 4, :], src[:, 2 * P:3 * P])
                    dve.tensor_tensor(sc[:, g, 5, :], src[:, 3 * P:4 * P], con("from"), ALU.mult).then_inc(s_sc, 1)

            def ssm_heads(l):
                with dve.Fori(0, SSM_HEADS // SSM_GROUPS) as hh:
                    dve.wait_ge(s_sc, l * 2 + 2)
                    dve.wait_ge(s_xtc, l * TT + TT)
                    n = l * SSM_HEADS + hh * 2
                    for g in range(SSM_GROUPS):
                        c0 = (n + g) * SSM_HC
                        dve.wait_ge(s_r, n + (g + 3))
                        for part in range(4):
                            dve.tensor_tensor_reduce(dg[:, part, :], bank(g, part * P, P), con("ident"), -1.0, 0.0, ALU.mult,
                                                     ALU.add, nb[:, g, part:part + 1]).then_inc(s_hc, 1)
                        dve.wait_ge(s_hc, c0 + 4)
                        dve.tensor_tensor(nb[:, g, 4:5], bank(g, P - 1, 1), nb[:, g, 0:1], ALU.add).then_inc(s_hc, 1)
                        dve.tensor_tensor(nb[:, g, 5:6], bank(g, 3 * P, 1), nb[:, g, 3:4], ALU.add).then_inc(s_hc, 1)
                        dve.wait_ge(s_hc, c0 + 6)
                        for b, (row, col) in enumerate(((0, 0), (1, 4), (1, 1), (2, 2), (2, 5), (3, 3))):
                            i = dve.tensor_scalar(ex[:, g, b, :], bank(g, row * P, P), nb[:, g, col:col + 1], 0.0,
                                                  ALU.add, ALU.min)
                        i.then_inc(s_hc, 1)
                        if g == 1:
                            head_mix(l, hh, n, 0)
                    head_mix(l, hh, n, 1)
                    for g in range(SSM_GROUPS):
                        head_y(l, hh, n, g)

            def head_mix(l, hh, n, g):
                dve.wait_ge(s_ex, n + (g + 1))
                for lo, hi, tt, d in ((0, 2, 0, 0), (2, 3, 1, 0), (3, 4, 0, 1), (4, 6, 1, 1)):
                    i = dve.scalar_tensor_tensor(out=mm_[:, g, lo:hi, :], in0=ex[:, g, lo:hi, :],
                                                 scalar=dt_[:, tt, bass.ds(hh + (d * SSM_HEADS + g * 4), 1)],
                                                 in1=sc[:, g, lo:hi, :], op0=ALU.mult, op1=ALU.mult)
                i.then_inc(s_mm, 1)
                dve.wait_ge(s_mm, n + (g + 1))

            def head_y(l, hh, n, g):
                dve.wait_ge(s_y, n + (g + 1))
                for tt in range(TT):
                    i = dve.scalar_tensor_tensor(out=ys[:, tt, bass.ds(hh * 64 + g * 256, 64)],
                                                 in0=xs[:, tt, bass.ds(hh * 64 + g * 256, 64)],
                                                 scalar=pk[:, bass.ds(hh + (AT["ssm_d"] + g * 4), 1)],
                                                 in1=bank(2 + g, tt * 64, 64), op0=ALU.mult, op1=ALU.add)
                i.then_inc(s_yh, 1)

            def ssm_out(l):
                c0 = l * SSM_YC
                dve.wait_ge(s_yh, l * SSM_HEADS + SSM_HEADS)
                dve.tensor_tensor(ys[:, :, :], ys[:, :, :], z[:, :, :], ALU.mult).then_inc(s_yc, 1)
                dve.wait_ge(s_yc, c0 + 1)
                for tt in range(TT):
                    if tt:
                        dve.wait_ge(s_yc, c0 + 1 + tt)
                    dve.tensor_tensor_reduce(ysq[:, :], ys[:, tt, :], ys[:, tt, :], 1.0, 0.0, ALU.mult, ALU.add,
                                             yst[:, tt:tt + 1]).then_inc(s_yc, 1)
                dve.wait_ge(s_yc, c0 + 3)
                dve.tensor_scalar(yst[:, 2:4], yst[:, 0:2], 1.0 / SSM_INNER, EPS, ALU.mult, ALU.add).then_inc(s_yc, 1)
                dve.wait_ge(s_ya, l + 1)
                dve.reciprocal(yst[:, 6:8], yst[:, 4:6]).then_inc(s_yc, 1)
                dve.wait_ge(s_yc, c0 + 5)
                for tt in range(TT):
                    i = dve.tensor_scalar(ys[:, tt, :], ys[:, tt, :], yst[:, 6 + tt:7 + tt], None, ALU.mult)
                i.then_inc(s_yc, 1)

            def gated(l, b, m_):
                n = l * (N_BRANCHES * KT) + b * KT
                dve.wait_ge(s_sg, n + (m_ + 1))
                dve.tensor_tensor(gt[:, m_ % 2, :], gs[:, m_ % 2, :], bank(6 + m_ % 2, 0, SEQ), ALU.mult).then_inc(s_bt, 1)
                dve.wait_ge(s_bt, n + (m_ + 1))
                dve.tensor_tensor(mix[:, m_, :], mix[:, m_, :], gt[:, m_ % 2, :], ALU.add).then_inc(s_bm, 1)

            def pair(l, i, half):
                n = l * UNITS + i * 8 + 4 * half

                def biased(u):
                    dve.wait_ge(s_s, n + (u + 2))
                    if u % TT == 0:
                        dve.wait_ge(s_bia[u // TT], (l * HP + i * 2 + (half + 1)) * (16 * TT))
                    if u >= 2:
                        dve.wait_ge(s_t, n + (u - 1))
                    dve.scalar_tensor_tensor(out=sa[:, u % 2, :], in0=bank(4, 0, GK),
                                             scalar=float(ATT_HEAD_DIM) ** -0.5, in1=bias[u // TT][:, u % TT, :],
                                             op0=ALU.mult, op1=ALU.add).then_inc(s_sb, 1)
                    dve.wait_ge(s_sb, n + (u + 1))
                    dve.tensor_reduce(ast[:, u % 2, 2:3], sa[:, u % 2, :], AX_X, ALU.max).then_inc(s_mx, 1)
                    dve.wait_ge(s_mx, n + (u + 1))
                    dve.tensor_scalar(ast[:, u % 2, 0:1], ast[:, u % 2, 2:3], -1.0, None, ALU.mult).then_inc(s_am, 1)

                def inverse(u):
                    dve.wait_ge(s_e, n + (u + 1))
                    dve.reciprocal(ast[:, u % 2, 3:4], ast[:, u % 2, 1:2]).then_inc(s_dn, 1)

                def scaled(u):
                    dve.wait_ge(s_dn, n + (u + 1))
                    dve.wait_ge(s_o, n + (u + 1))
                    dve.tensor_scalar(ao[:, u % TT, bass.ds(i * (2 * P) + (half * P + 64 * (u // TT)), 64)],
                                      bank(2 * (u % 2), GK, 64), ast[:, u % 2, 3:4], None,
                                      ALU.mult).then_inc(s_oc, 1)

                def tile(k):
                    gated(l, i, 4 * half + k)

                biased(0)
                tile(0)
                biased(1)
                inverse(0)
                tile(1)
                biased(2)
                scaled(0)
                inverse(1)
                tile(2)
                biased(3)
                scaled(1)
                inverse(2)
                tile(3)
                scaled(2)
                inverse(3)
                scaled(3)

            def attention(l):
                dve.memset(mix[:, :, :], 0.0).then_inc(s_mz, 1)
                with dve.Fori(0, HB) as i:
                    dve.wait_ge(s_mz, l + 1)
                    for half in range(2):
                        pair(l, i, half)

            def branches(l):
                with dve.Fori(HB, N_BRANCHES) as b:
                    for m_ in range(KT):
                        gated(l, b, m_)
                dve.wait_ge(s_bm, (l + 1) * (N_BRANCHES * KT) + 2)

            def mix_out(l):
                for m_ in range(KT):
                    dve.wait_ge(s_wo, l * KT + (m_ + 1))
                    i = dve.tensor_tensor(h[:, m_, :], h[:, m_, :], bank(m_, 0, SEQ), ALU.add)
                i.then_inc(s_h, 1)
                dve.wait_ge(s_h, l * 3 + 2)

            def low(units, first, u, r, j):
                slot = (first + u) % SLOTS
                dve.wait_ge(s_wh, units + (u + 1))
                lo = (first + u) % 2 * UNIT
                dve.tensor_tensor(wlo[:, slot, :], ring[:, j % RING, lo:lo + UNIT], whi[:, slot, :],
                                  ALU.subtract).then_inc(s_wl, 1)

            def lows(units, first, n, j):
                for u in range(n):
                    low(units, first, u, 0, j + (first % 2 + u) // 2)

            def dense():
                for k in range(4):
                    dve.wait_ge(s_xh, k + 1)
                    dve.tensor_tensor(xlo[:, 2 * k:2 * k + 2, :], xn[:, 2 * k:2 * k + 2, :], xhi[:, 2 * k:2 * k + 2, :],
                                      ALU.subtract).then_inc(s_xl, 1)
                lows(0, 0, 8, 0)

                def chunk(c, par_, n, units, j, first=False):
                    dve.wait_ge(s_si, c + 1)
                    if not first:
                        dve.wait_ge(s_hl, c)
                    dve.tensor_tensor(hid[:, :, :], hs[:, :, :],
                                      ps[:, 1024:2048].rearrange("p (b t) -> p b t", b=2)[:, :, 0:SEQ],
                                      ALU.mult).then_inc(s_hm, 1)
                    if n:
                        lows(units, 2, 1, j)
                    dve.wait_ge(s_hh, c + 1)
                    dve.tensor_tensor(hlo[:, par_, :, :], hid[:, :, :], hhi[:, par_, :, :],
                                      ALU.subtract).then_inc(s_hl, 1)
                    for u in range(1, n):
                        low(units, 2, u, 0, j + u // 2)

                chunk(0, 0, 6, 8, 4, first=True)
                with dve.Fori(0, (DENSE_CHUNKS - 3) // 2) as i:
                    for c in range(2):
                        chunk(i * 2 + (c + 1), (c + 1) % 2, 6, i * 12 + (14 + 6 * c), 7 + 3 * c)
                c = DENSE_CHUNKS - 2
                chunk(c, c % 2, 4, 8 + 6 * c, 4 + 3 * c)
                chunk(c + 1, (c + 1) % 2, 0, 0, 0)
                dve.wait_ge(s_wu, DENSE_UNITS + SLOTS)
                for m_ in range(KT):
                    i = dve.tensor_tensor(h[:, m_, :], h[:, m_, :], bank(4 + m_ // 2, (m_ % 2) * SEQ, SEQ), ALU.add)
                i.then_inc(s_h, 1)

            def route():
                done = 0

                def link(i, s=s_rc):
                    nonlocal done
                    done += 1
                    i.then_inc(s_rc, 1)
                    dve.wait_ge(s_rc, done)

                dve.wait_ge(s_rl, 1)
                link(dve.tensor_copy(lg[:, :, :], bank(4, 0, TT * N_EXPERTS).rearrange("p (t e) -> p t e", t=TT)))
                for tt in range(TT):
                    link(dve.max(top[:, tt, :], lg[:, tt, :]))
                    link(dve.max_index(topi[:, tt, :], top[:, tt, :], lg[:, tt, :]))
                link(dve.tensor_tensor(rt[:, :, 0:1], top[:, :, 1:2], top[:, :, 0:1], ALU.subtract))
                assert done == RC_EXP
                link(dve.tensor_copy(topf[:, :, :], topi[:, :, :]))
                for tt in range(TT):
                    for c in range(2):
                        link(dve.tensor_scalar(oh[:, tt, c, :], con("experts", 0, N_EXPERTS), topf[:, tt, c:c + 1], None,
                                               ALU.is_equal))
                    link(dve.tensor_tensor(msk[:, tt, :], oh[:, tt, 0, :], oh[:, tt, 1, :], ALU.add))
                assert done == RC_MASK, done
                dve.wait_ge(s_re, 1)
                link(dve.tensor_scalar(rt[:, :, 2:3], rt[:, :, 1:2], 1.0, None, ALU.add))
                link(dve.reciprocal(rt[:, :, 3:4], rt[:, :, 2:3]))
                link(dve.tensor_tensor(rt[:, :, 4:5], rt[:, :, 3:4], rt[:, :, 1:2], ALU.mult))
                for tt in range(TT):
                    link(dve.tensor_scalar(comb[:, tt, :], oh[:, tt, 0, :], rt[:, tt, 3:4], None, ALU.mult))
                    link(dve.scalar_tensor_tensor(out=comb[:, tt, :], in0=oh[:, tt, 1, :], scalar=rt[:, tt, 4:5],
                                                  in1=comb[:, tt, :], op0=ALU.mult, op1=ALU.add))
                dve.wait_ge(s_rp, 1)
                link(dve.tensor_scalar(pos[:, :, :], bank(5, 0, TT * N_EXPERTS).rearrange("p (t e) -> p t e", t=TT),
                                       1.0, None, ALU.add))
                link(dve.tensor_tensor(pos[:, :, :], pos[:, :, :], msk[:, :, :], ALU.mult))
                link(dve.tensor_scalar(pos[:, :, :], pos[:, :, :], -1.0, None, ALU.add))
                link(dve.tensor_reduce(cnt[:, 0:1], bank(5, 2 * N_EXPERTS, N_EXPERTS), AX_X, ALU.max))
                link(dve.tensor_scalar(cnt[:, 1:2], cnt[:, 0:1], float(P), 1.0, ALU.is_gt, ALU.add))
                dve.tensor_copy(rounds[:, :], cnt[:, 1:2]).then_inc(s_rr, 1)
                dve.wait_ge(s_rr, 1)

            def experts():
                n_r = dve.value_load(rounds[0:1, 0:1], min_val=1, max_val=2)
                with dve.Fori(0, n_r) as o:
                    with dve.Fori(0, N_EXPERTS) as e:
                        q = o * N_EXPERTS + e
                        c0 = q * EXP_CHUNKS + DENSE_CHUNKS
                        u0 = q * PASS_UNITS + DENSE_UNITS
                        for tt in range(TT):
                            i = dve.tensor_scalar(gat[:, tt, :], con("slots"), pos[:, tt, bass.ds(e, 1)], None,
                                                  ALU.is_equal)
                        i.then_inc(s_g, 1)
                        dve.wait_ge(s_g, q + 1)
                        for tt in range(TT):
                            i = dve.tensor_scalar(gatw[:, tt, :], gat[:, tt, :], comb[:, tt, bass.ds(e, 1)], None,
                                                  ALU.mult)
                        i.then_inc(s_gw, 1)
                        lows(u0, 0, 4, 0)
                        for j in range(2):
                            dve.wait_ge(s_xgc, q * 2 + (j + 1))
                            dve.tensor_tensor(xlo[:, 4 * j:4 * j + 4, 0:P], bank(6 + j).rearrange("p (c t) -> p c t", c=4),
                                              xhi[:, 4 * j:4 * j + 4, 0:P], ALU.subtract).then_inc(s_xl, 1)
                        lows(u0 + 4, 4, 4, 2)

                        def chunk(k, cc, n, j=0):
                            dve.wait_ge(s_si, c0 + k + 1)
                            dve.tensor_tensor(hid[:, 0, :], hs[:, 0, :], bank(cc % 2, SEQ, SEQ), ALU.mult).then_inc(s_hm, 1)
                            if n:
                                lows(u0 + (k * 6 + 8), 2, 2, j)
                            dve.wait_ge(s_hh, c0 + k + 1)
                            dve.tensor_tensor(hlo[:, cc % 2, :, 0:P], bank(2 + cc % 2, 0, SEQ).rearrange(
                                "p (h t) -> p h t", h=2), hhi[:, cc % 2, :, 0:P], ALU.subtract).then_inc(s_hl, 1)
                            for u in range(2, n):
                                low(u0 + (k * 6 + 8), 2, u, 0, j + u // 2)

                        chunk(0, 0, 6, 4)
                        with dve.Fori(0, (EXP_CHUNKS - 4) // 2) as i_:
                            for c in range(2):
                                chunk(i_ * 2 + (c + 1), c + 1, 6, 7 + 3 * c)
                        c = EXP_CHUNKS - 3
                        chunk(c, c, 6, 4 + 3 * c)
                        chunk(c + 1, c + 1, 4, 7 + 3 * c)
                        chunk(c + 2, c + 2, 0)
                        for m_ in range(KT):
                            dve.wait_ge(s_eo, q * KT + (m_ + 1))
                            if m_ == 0:
                                dve.wait_ge(s_ea, q * KT + 2)
                            dve.tensor_tensor(h[:, m_, :], h[:, m_, :], bank(6 + m_ % 2, 0, SEQ),
                                              ALU.add).then_inc(s_ea, 1)
                    dve.wait_ge(s_gw, o * N_EXPERTS + N_EXPERTS)
                    dve.tensor_scalar(pos[:, :, :], pos[:, :, :], -float(P), None, ALU.add).then_inc(s_pos, 1)
                    dve.wait_ge(s_pos, o + 1)
                dve.memset(cnt[:, 3:4], 0.0).then_inc(s_h, 1)

            def ple(l):
                dve.wait_ge(s_h, l * 3 + 3)
                for m_ in range(KT):
                    dve.wait_ge(s_pg, l * KT + (m_ + 1))
                    dve.tensor_tensor(mix[:, m_, :], gs[:, m_ % 2, :], bank(2 * (m_ % 2), 0, SEQ),
                                      ALU.mult).then_inc(s_pt, 1)
                dve.wait_ge(s_pt, l * KT + KT)
                dve.tensor_tensor(h[:, :, :], h[:, :, :], mix[:, :, :], ALU.add).then_inc(s_h, 1)
                dve.wait_ge(s_h, l * 3 + 4)

            dve.sem_inc(s_bm, 2)
            dve.sem_inc(s_ea, 2)
            dve.wait_ge(s_x, 16)
            dve.memset(cnt[:, 2:3], 0.0).then_inc(s_h, 1)
            dve.wait_ge(s_zero, 2)
            dve.wait_ge(s_cst, 16)
            with dve.Fori(0, DEPTH) as l:
                dve.wait_ge(s_pk, l * 16 + 16)
                norm(l * 2, "norm_mix")
                conv(l)
                ssm_conv(l)
                time_steps(l)
                conv_norm(l)
                ssm_scores(l)
                ssm_heads(l)
                ssm_out(l)
                attention(l)
                branches(l)
                mix_out(l)
                norm(l * 2 + 1, "norm_ffn")
                with dve.If(l < 1):
                    dense()
                with dve.Else():
                    route()
                    experts()
                ple(l)
            norm(2 * DEPTH, "final_norm")

        @block.gpsimd
        def _(pool):
            for t in (glu, xbcp):
                pad = PAD if t is glu else SPAD
                pool.memset(t[:, :, 0:pad], 0.0)
                pool.memset(t[:, :, SEQ + pad:SEQ + 2 * pad], 0.0).then_inc(s_zero, 1)
            pool.wait_ge(s_zero, 2)
            pool.wait_ge(s_relW, 16)
            pool.wait_ge(s_cst, 16)

            def load_bias(l, i, slot):
                for tt in range(TT):
                    src = bass.AP(tensor=scratch.ap().tensor,
                                  offset=(i * 2 + slot) * (ATT_GROUPS * 2 * SEQ) + tt * P,
                                  ap=[[1, P], [2 * SEQ, ATT_GROUPS], [1, SEQ]])
                    dst = bias[slot][:, tt, :].rearrange("p (g k) -> p g k", g=ATT_GROUPS)
                    pool.dma_start(dst, src).then_inc(s_bia[slot], 16)

            with pool.Fori(0, DEPTH) as l:
                for pair in range(2):
                    pool.wait_ge(s_pf, l * N_PROJ + (4 * pair + 4))
                    pool.tensor_tensor(glu[:, 2 * pair:2 * pair + 2, PAD:PAD + SEQ], glu_a[:, pair, :, :],
                                       glu_s[:, pair, :, :], ALU.mult).then_inc(s_glu, 1)
                load_bias(l, 0, 0)
                with pool.Fori(0, SSM_HEADS // SSM_GROUPS) as hh:
                    pool.wait_ge(s_dtc, l * DTC + DTC)
                    n = l * SSM_HEADS + hh * 2
                    for g in range(SSM_GROUPS):
                        pool.wait_ge(s_r, n + (g + 1))
                        for d in range(2):
                            for tt in range(TT):
                                col = dta[:, tt, bass.ds(hh + (d * SSM_HEADS + g * 4), 1)]
                                k = pool.tensor_tensor(ua[:, g, 2 * d + tt, :], con("upto" if d == 0 else "from"),
                                                       col.to_broadcast([P, P]), ALU.mult)
                        k.then_inc(s_ua, 1)
                pool.wait_ge(s_f2, l * FNET_GROUPS + FNET_GROUPS)
                pool.sem_inc(s_step, 1)
                load_bias(l, 0, 1)
                with pool.Fori(0, HP) as i:
                    pool.wait_ge(s_pf, l * N_PROJ + N_PROJ)
                    n = l * UNITS + i * 4
                    pool.wait_ge(s_s, n + 1)
                    pool.wait_ge(s_yc, l * SSM_YC + 1)
                    for which in range(2):
                        src = qk[:, which * ATT_GROUPS:(which + 1) * ATT_GROUPS, bass.ds(i, 1), :]
                        dst = qkp[:, which, :, :].rearrange("p g (o t) -> p g o t", o=1)
                        pool.tensor_copy(dst[:, :, :, ::-1] if which == 0 else dst, src).then_inc(s_qkp, 1)
                    with pool.If(i < HP - 1):
                        for slot in range(2):
                            pool.wait_ge(s_sb, n + (2 * slot + 2))
                            pool.sem_inc(s_step, 1)
                            load_bias(l, i + 1, slot)


def _cols(w, c0, c1, width=COLS):
    k = w.shape[0] // P
    return w[:, c0:c1].reshape(k, P, (c1 - c0) // width, width).transpose(2, 1, 0, 3).reshape(-1, P, k * width)


def _rows(w):
    return w.reshape(-1, 2, P, D_MODEL).transpose(0, 2, 1, 3).reshape(-1, P, BLK)


def _swiglu_blocks(w1, w3, w2):
    f = w1.shape[1]
    up = np.stack([_cols(w, 0, f).reshape(-1, P, KT, COLS) for w in (w1, w3)], axis=3)
    up = up.reshape(-1, P, 2, BLK).transpose(0, 2, 1, 3)
    down = _rows(w2)
    order = [up[0]] + [b for c in range(1, f // COLS) for b in (up[c], down[c - 1:c])] + [down[-1:]]
    return np.concatenate(order)


def _mixer_blocks(w_in, w_gate, branch_out, w_out):
    c = OFF_CONV
    conv = [_cols(w_in, c + o, c + o + COLS) for o in (0, CONV_CH, COLS, CONV_CH + COLS)]
    xbc = OFF_SSM + SSM_INNER
    parts = conv + [_cols(w_in, xbc, OFF_DT), _cols(w_in, OFF_SSM, xbc),
                    _cols(w_in, OFF_FNET, OFF_FNET + FNET_WIDTH), _cols(w_in, 2 * OFF_CONV // 3, OFF_CONV),
                    _cols(w_in, 0, 2 * OFF_CONV // 3)]
    for b, where in enumerate(BRANCH_OF):
        gate = _cols(w_gate[where], 0, D_MODEL)
        o = _cols(branch_out[b], 0, D_MODEL, 512)
        parts += [gate[0:1], o[0:1], gate[1:3], o[1:2], gate[3:4]]
    return np.concatenate(parts + [_cols(w_out, 0, D_MODEL)])


def _per_partition(a):
    return a.reshape(-1, P).T


def _everywhere(a):
    return np.broadcast_to(a.reshape(1, -1), (P, a.size))


def _constants():
    t = np.arange(P)
    s = np.arange(SEQ)
    ch = 2 * np.pi * np.outer(t, t) / FNET_GROUP_DIM
    tk = 2 * np.pi * (np.outer(s, s) % SEQ) / SEQ
    norm = 1.0 / math.sqrt(SEQ * FNET_GROUP_DIM)

    def tokens(m):
        return m.reshape(TT, P, SEQ).transpose(1, 0, 2).reshape(P, TT * SEQ)

    parts = {"ident": np.eye(P), "upto": t[:, None] <= t[None], "from": t[:, None] >= t[None],
             "before": t[:, None] < t[None], "ones": np.ones((P, P)), "slots": np.tile(t, (P, 1)),
             "dft_ch": np.concatenate([np.cos(ch), np.sin(ch)], 1), "dft_cos": tokens(np.cos(tk)) * norm,
             "dft_sin": -tokens(np.sin(tk)) * norm, "experts": np.tile(np.arange(N_EXPERTS), (P, 1))}
    return np.concatenate([np.asarray(parts[n], np.float64) for n, _ in _CONSTS], 1).astype(np.float32)


def _bucket_rows():
    oh = np.zeros((REL_BUCKETS + 1, ATT_GROUPS, 2 * SEQ), np.float32)
    for g, (window, dil) in enumerate(ATT_PATTERNS):
        half, hb = window // (2 * dil), REL_BUCKETS // 2
        for c in range(2 * SEQ):
            rel = c - (SEQ - 1)
            if rel % dil or abs(rel) > half * dil or rel >= SEQ:
                oh[REL_BUCKETS, g, c] = MASKED
                continue
            n, exact = abs(rel), hb // 2
            large = min(hb - 1, exact + int(math.log(max(n, 1) / exact) / math.log(REL_MAX_DIST / exact) * (hb - exact)))
            oh[(hb if rel > 0 else 0) + (n if n < exact else large), g, c] = 1.0
    return oh


def kernel(x, p, rel_bias, norm_mix, w_in, conv_dw, conv_dw_b, conv_ln_g, conv_ln_b, conv_out, ssm_conv_w,
           ssm_conv_b, ssm_a_log, ssm_dt_bias, ssm_d, ssm_norm, ssm_out, attn_out, fnet_out, w_gate, b_gate,
           w_out, norm_ffn, ffn_w1, ffn_w3, ffn_w2, moe_router, moe_w1, moe_w3, moe_w2, ple_gate, ple_proj,
           final_norm):
    from concourse import bacc
    from concourse.bass_utils import run_bass_kernel_spmd

    (x, p, rel_bias, norm_mix, w_in, conv_dw, conv_dw_b, conv_ln_g, conv_ln_b, conv_out, ssm_conv_w,
     ssm_conv_b, ssm_a_log, ssm_dt_bias, ssm_d, ssm_norm, ssm_out, attn_out, fnet_out, w_gate, b_gate,
     w_out, norm_ffn, ffn_w1, ffn_w3, ffn_w2, moe_router, moe_w1, moe_w3, moe_w2, ple_gate, ple_proj,
     final_norm) = [np.asarray(a) for a in (
         x, p, rel_bias, norm_mix, w_in, conv_dw, conv_dw_b, conv_ln_g, conv_ln_b, conv_out, ssm_conv_w,
         ssm_conv_b, ssm_a_log, ssm_dt_bias, ssm_d, ssm_norm, ssm_out, attn_out, fnet_out, w_gate, b_gate,
         w_out, norm_ffn, ffn_w1, ffn_w3, ffn_w2, moe_router, moe_w1, moe_w3, moe_w2, ple_gate, ple_proj,
         final_norm)]

    def by_token(a):
        return a.reshape(SEQ, -1, P).transpose(2, 1, 0)

    def params(l):
        parts = {
            "norm_mix": _per_partition(norm_mix[l]), "norm_ffn": _per_partition(norm_ffn[l]),
            "final_norm": _per_partition(final_norm), "b_gate": _per_partition(b_gate[l][list(BRANCH_OF)]),
            "conv_dw": _per_partition(conv_dw[l]), "conv_b": _per_partition(conv_dw_b[l]),
            "ln_g": _per_partition(conv_ln_g[l]), "ln_b": _per_partition(conv_ln_b[l]),
            "ssm_w": _per_partition(ssm_conv_w[l]), "ssm_b": _per_partition(ssm_conv_b[l]),
            "ssm_norm": _per_partition(ssm_norm[l]), "ssm_d": _everywhere(ssm_d[l]),
            "a_log": _everywhere(ssm_a_log[l]), "dt_bias": _everywhere(ssm_dt_bias[l]),
            "w_dt": _cols(w_in[l], OFF_DT, OFF_FNET, DT)[0],
            "router": _cols(moe_router[0], 0, N_EXPERTS, N_EXPERTS)[0],
            "p": by_token(p[l, 0]).reshape(P, -1)}
        return np.concatenate([parts[n] for n, _ in _PARAMS], 1)

    relb = np.concatenate([rel_bias, np.ones((1, rel_bias.shape[1]), rel_bias.dtype)])
    arrays = {
        "x_in": by_token(x[0]),
        "w_mixers": np.stack([_mixer_blocks(w_in[l], w_gate[l], (fnet_out[l], conv_out[l], ssm_out[l], attn_out[l]),
                                            w_out[l]) for l in range(DEPTH)]),
        "w_dense": _swiglu_blocks(ffn_w1[0], ffn_w3[0], ffn_w2[0]),
        "w_experts": np.concatenate([_swiglu_blocks(moe_w1[0, e], moe_w3[0, e], moe_w2[0, e]) for e in range(N_EXPERTS)]),
        "w_ple": np.stack([np.concatenate([_cols(ple_gate[l], 0, D_MODEL), _rows(ple_proj[l])]) for l in range(DEPTH)]),
        "params": np.stack([params(l) for l in range(DEPTH)]),
        "constants": _constants(),
        "buckets": _bucket_rows(),
        "bias_table": relb,
    }
    arrays = {n: np.ascontiguousarray(a) for n, a in arrays.items()}
    nc = bacc.Bacc("TRN2", target_bir_lowering=False, num_devices=1)
    ins = [nc.dram_tensor(n, a.shape, mybir.dt.from_np(a.dtype), kind="ExternalInput").ap() for n, a in arrays.items()]
    out = nc.dram_tensor("trunk_out", (P, KT, SEQ), F32, kind="ExternalOutput").ap()
    trunk_program(nc, *ins, out)
    got = run_bass_kernel_spmd(nc, [arrays], core_ids=[0]).results[0]["trunk_out"]
    return got.transpose(2, 1, 0).reshape(1, SEQ, D_MODEL)
```

```python
from contextlib import ExitStack
import math

import numpy as np

import concourse.bass as bass
from concourse import mybir

F32 = mybir.dt.float32
F32R = mybir.dt.float32r
I32 = mybir.dt.int32
U32 = mybir.dt.uint32
ACT = mybir.ActivationFunctionType
ALU = mybir.AluOpType
AX_X = mybir.AxisListType.X

P = 128
D_MODEL = 1024
SEQ = 256
DEPTH = 2
EPS = 1e-6
PLE_DIM = 256
N_BRANCHES = 4
CONV_CH, CONV_K = 512, 31
SSM_HEADS, SSM_HEAD_DIM, SSM_GROUPS, SSM_STATE, SSM_CONV = 8, 64, 2, 64, 5
SSM_INNER = SSM_HEADS * SSM_HEAD_DIM
SSM_CONV_CH = SSM_INNER + 2 * SSM_GROUPS * SSM_STATE
ATT_PATTERNS = ((128, 1), (512, 4), (2048, 16))
ATT_GROUPS, ATT_HEADS, ATT_HEAD_DIM = 3, 8, 64
ATT_WIDTH = ATT_HEADS * ATT_HEAD_DIM
REL_BUCKETS, REL_MAX_DIST = 32, 1024
FNET_GROUPS, FNET_GROUP_DIM = 4, 128
FNET_WIDTH = FNET_GROUPS * FNET_GROUP_DIM
FFN_DIM, N_EXPERTS, EXPERT_DIM = 2816, 8, 3584
OFF_CONV = 3 * ATT_GROUPS * ATT_WIDTH
OFF_SSM = OFF_CONV + 2 * CONV_CH
OFF_DT = OFF_SSM + SSM_INNER + SSM_CONV_CH
OFF_FNET = OFF_DT + 2 * SSM_HEADS
MASKED = -1e30

KT = D_MODEL // P
TT = SEQ // P
CT = CONV_CH // P
XT = SSM_CONV_CH // P
DT = 2 * SSM_HEADS
PAD = CONV_K // 2
SPAD = SSM_CONV // 2
HALF = SEQ

BLK = 2048
RING = 6
COLS = BLK // KT
PROJ_BLOCKS = 29
BRANCH_BLOCKS = 6
MIX_BLOCKS = PROJ_BLOCKS + N_BRANCHES * BRANCH_BLOCKS + 4
MIX_ROUNDS = 10
DENSE_CHUNKS = FFN_DIM // COLS
EXP_CHUNKS = EXPERT_DIM // COLS
DENSE_ROUNDS = (3 * DENSE_CHUNKS + RING - 1) // RING
PASS_ROUNDS = 3 * EXP_CHUNKS // RING
PLE_BLOCKS = 5
LAYER0_ROUNDS = MIX_ROUNDS + DENSE_ROUNDS + 1
UNIT = BLK // 2
SLOTS = 6
DENSE_UNITS, PASS_UNITS = 6 * DENSE_CHUNKS, 6 * EXP_CHUNKS
DENSE_BLOCKS = 3 * DENSE_CHUNKS
FIRST_BLOCKS = 4
FIRST_UNITS = 4
MAX_PASSES = 2 * N_EXPERTS
assert DENSE_UNITS % SLOTS == 0 and PASS_UNITS % SLOTS == 0
assert MIX_BLOCKS <= MIX_ROUNDS * RING and PLE_BLOCKS < RING and 3 * EXP_CHUNKS % RING == 0

_PARAMS = (("b_gate", N_BRANCHES * KT),
           ("conv_dw", CONV_K * CT), ("conv_b", CT), ("ln_g", CT), ("ln_b", CT),
           ("ssm_w", SSM_CONV * XT), ("ssm_b", XT), ("ssm_norm", CT),
           ("ssm_d", SSM_HEADS), ("a_log", DT), ("dt_bias", DT),
           ("w_dt", KT * DT), ("router", KT * N_EXPERTS),
           ("p", PLE_DIM // P * SEQ))
AT = {}
PK = 0
for _name, _n in _PARAMS:
    AT[_name] = PK
    PK += _n

_CONSTS = (("ident", P), ("upto", P), ("from", P), ("before", P), ("ones", P), ("slots", P),
           ("dft_ch", 2 * P), ("dft_cos", TT * SEQ), ("dft_sin", TT * SEQ), ("experts", N_EXPERTS),
           ("gains", (2 * DEPTH + 1) * KT))
CAT = {}
CK = 0
for _name, _n in _CONSTS:
    CAT[_name] = CK
    CK += _n

FNET, CONV, SSM, ATT = range(4)
BRANCH_OF = (3, 1, 2, 0)
N_PROJ = 59
DTC = 20
SSM_HC = 7
SSM_YC = 6
RC_EXP, RC_MASK = 6, 13
T_XBC, T_Z, T_DT, T_FN, T_V = 8, 14, 18, 19, 23
T_Q = T_V + 12
HB = N_BRANCHES // 2
LATE_BLOCKS = HB * BRANCH_BLOCKS + 4
EARLY_BLOCKS = 17
EARLY_DVE = (EARLY_BLOCKS + 1) // 2
EARLY_POOL = [(j, u) for j in range(EARLY_BLOCKS) for u in range(2) if u or j % 2]
BRANCH_UNITS, LATE_UNITS = 2 * BRANCH_BLOCKS, 2 * LATE_BLOCKS
UNITS = ATT_HEADS * TT
HP = ATT_HEADS // 2
GK = ATT_GROUPS * SEQ


def trunk_program(nc, x, wm, wd, we, wp, pk_in, cst_in, onehot, relb, out):
    ctx = ExitStack()
    with ctx:
        def sb(name, shape, dt=F32):
            return ctx.enter_context(nc.sbuf_tensor(name, shape, dt))

        def sem(name):
            return ctx.enter_context(nc.semaphore(name))

        scratch = nc.dram_tensor("bias_rows", [ATT_HEADS, ATT_GROUPS, 2 * SEQ], F32)

        with nc.sbuf_tensor("ring", [P, RING, BLK], F32) as ring:
            pass
        ring_lo = sb("ring_lo", [P, RING, BLK], F32R)
        h = sb("h", [P, KT, SEQ])
        xn = sb("xn", [P, KT, SEQ])
        mix = sb("mix", [P, KT, SEQ])
        pk = sb("params_sb", [P, PK])
        cst = sb("constants_sb", [P, CK])
        gs = sb("gs", [P, 2, SEQ])
        gt = sb("gt", [P, 2, SEQ])
        xbcp = sb("xbcp", [P, XT, SEQ + 2 * SPAD])
        glu = sb("glu", [P, CT, SEQ + 2 * PAD])
        topi = sb("topi", [P, TT, 8], U32)
        cnt = sb("cnt", [P, 4])
        passes_sb = sb("passes", [P, 1], I32)
        rstd = sb("rstd", [P, SEQ])
        rms_t = sb("rms_t", [P, 2, SEQ])

        mixers = ExitStack()

        def msb(name, shape, dt=F32):
            return mixers.enter_context(nc.sbuf_tensor(name, shape, dt))

        glu_a = msb("glu_a", [P, 2, 2, SEQ])
        glu_s = msb("glu_s", [P, 2, 2, SEQ])
        qk = msb("qk", [P, 2 * ATT_GROUPS, HP, SEQ])
        cvfa = msb("cvfa", [P, 2 * CT * SEQ])
        v = msb("v", [P, TT, ATT_GROUPS * ATT_WIDTH])
        ex = msb("ex", [P, 2, 6, P])
        mm_ = msb("mm", [P, 2, 6, P])
        sc = msb("sc", [P, SSM_GROUPS, 6, P])
        ua = msb("ua", [P, 2, 4, P])
        dts = msb("dts", [P, 8, TT * DT])
        dt_ = msb("dt", [P, TT, DT])
        dta = msb("dta", [P, TT, DT])
        a_neg = msb("a_pos", [P, DT])
        dg = msb("dg", [P, 4, P])
        nb = msb("nb", [P, 2, 6])
        yst = msb("yst", [P, 8])
        ast = msb("ast", [P, 2, 4])
        bias0 = msb("bias0", [P, TT, GK])
        xbc = msb("xbc", [P, XT, SEQ])
        ybr = msb("ybr", [P, N_BRANCHES * CT, SEQ])

        def view(buf, lo, shape, pattern, **sizes):
            n = int(np.prod(shape))
            flat = buf if len(buf.shape) == 2 else buf.rearrange("p a b -> p (a b)") if len(buf.shape) == 3 \
                else buf.rearrange("p a b c -> p (a b c)")
            return flat[:, lo:lo + n] if pattern == "p c -> p c" else flat[:, lo:lo + n].rearrange(pattern, **sizes)

        cv = view(cvfa[:, :], 0, [CT, SEQ], "p (c t) -> p c t", c=CT)
        fa = view(cvfa[:, :], CT * SEQ, [2, TT, 2 * P], "p (a t c) -> p a t c", a=2, t=TT)
        cvx = view(glu_a[:, :, :, :], 0, [CT, SEQ], "p (c t) -> p c t", c=CT)
        ys = view(glu_s[:, :, :, :], 0, [TT, SSM_INNER], "p (t c) -> p t c", t=TT)
        ysq = view(dg[:, :, :], 0, [SSM_INNER], "p c -> p c")
        fu = ybr[:, 0:CT, :]
        z = view(ybr[:, :, :], 2 * CT * SEQ, [TT, SSM_INNER], "p (t c) -> p t c", t=TT)
        xs = view(ybr[:, :, :], 3 * CT * SEQ, [TT, SSM_INNER], "p (t c) -> p t c", t=TT)
        bias = [bias0, view(cvfa[:, :], 0, [TT, GK], "p (t k) -> p t k", t=TT)]
        qkp = view(sc[:, :, :, :], 0, [2, ATT_GROUPS, SEQ], "p (w g t) -> p w g t", w=2, g=ATT_GROUPS)
        sa = view(ex[:, :, :, :], 0, [2, GK], "p (u k) -> p u k", u=2)
        pt = view(mm_[:, :, :, :], 0, [2, GK], "p (u k) -> p u k", u=2)
        ao = view(xbc[:, :, :], 0, [TT, ATT_WIDTH], "p (t c) -> p t c", t=TT)
        mixers.close()

        xhi = sb("xhi", [P, KT, SEQ], F32R)
        whi = sb("whi", [P, SLOTS, UNIT], F32R)
        wlo = sb("wlo", [P, SLOTS, UNIT], F32R)
        xlo = sb("xlo", [P, KT, SEQ], F32R)
        hhi = sb("hhi", [P, 2, 2, SEQ], F32R)
        hlo = sb("hlo", [P, 2, 2, SEQ], F32R)
        hs, hid = gs, gt
        yx = sb("yx", [P, D_MODEL])
        gat = sb("gat", [P, TT, P])
        gatw = sb("gatw", [P, TT, P])
        sca = sb("sca", [P, SEQ])
        lg = sb("lg", [P, TT, N_EXPERTS])
        top = sb("top", [P, TT, 8])
        topf = sb("topf", [P, TT, 8])
        rt = sb("rt", [P, TT, 8])
        oh = sb("oh", [P, TT, 2, N_EXPERTS])
        comb = sb("comb", [P, TT, MAX_PASSES + 1])
        msk = sb("msk", [P, TT, N_EXPERTS])
        pos = sb("pos", [P, TT, MAX_PASSES + 1])

        n_oh = ATT_GROUPS * 2 * SEQ
        ybr_flat = ybr[:, :, :].rearrange("p c t -> p (c t)")
        onehot_sb = ybr_flat[0:REL_BUCKETS + 1, 0:n_oh].rearrange("p (g c) -> p g c", g=ATT_GROUPS)
        relb_sb = ybr_flat[0:REL_BUCKETS + 1, n_oh:n_oh + ATT_GROUPS * ATT_HEADS]
        rows_sb = ybr_flat[0:ATT_HEADS, 2048:2048 + n_oh].rearrange("p (g c) -> p g c", g=ATT_GROUPS)

        ps = ctx.enter_context(nc.psum_tensor("ps", [P, 8 * 512], F32))

        def bank(b, lo=0, n=512):
            return ps[:, 512 * b + lo:512 * b + lo + n]

        def par(name, i=0, n=1):
            return pk[:, AT[name] + i:AT[name] + i + n]

        def con(name, i=0, n=P):
            return cst[:, CAT[name] + i:CAT[name] + i + n]

        s_loaded = [sem(f"ring_loaded{i}") for i in range(RING)]
        s_cst = sem("constants_loaded")
        s_x = sem("x_loaded")
        s_zero = sem("pads_zeroed")
        s_relT = sem("bias_rows_product")
        s_relL = sem("bias_inputs_loaded")
        s_relC = sem("bias_rows_copied")
        s_relW = sem("bias_rows_written")
        s_pk = sem("params_loaded")
        s_h = sem("h_with_ffn")
        s_hr = sem("h_tile_ready")
        s_sq = sem("squares_ready")
        s_ms = sem("mean_square_ready")
        s_var = sem("variance_ready")
        s_sd = sem("deviation_ready")
        s_rs = sem("rstd_ready")
        s_xn = sem("xn_ready")
        s_pj = sem("proj_tile_ready")
        s_pf = sem("proj_tile_copied")
        s_glu = sem("glu_ready")
        s_cvw = sem("conv_chain")
        s_xc = sem("ssm_conv_chain")
        s_xa = sem("ssm_conv_active")
        s_dtc = sem("dt_chain")
        s_dta = sem("dt_exp")
        s_lns = sem("ln_sum_ready")
        s_lnc = sem("ln_chain")
        s_lna = sem("ln_act")
        s_f1 = sem("fnet_channels_ready")
        s_f1c = sem("fnet_channels_copied")
        s_f2 = sem("fnet_tokens_ready")
        s_f2c = sem("fnet_tokens_copied")
        s_xt = sem("x_transposed")
        s_xtc = sem("x_transposed_copied")
        s_bc = sem("bc_scores_ready")
        s_sc = sem("bc_scores_masked")
        s_ua = sem("dta_rows_ready")
        s_r = sem("cumsum_ready")
        s_hc = sem("ssm_head_chain")
        s_ex = sem("decay_ready")
        s_mm = sem("ssm_mix_ready")
        s_y = sem("ssm_y_ready")
        s_yh = sem("ssm_head_y_done")
        s_yc = sem("ssm_y_chain")
        s_ya = sem("ssm_sd_ready")
        s_yt = sem("ssm_y_transposed")
        s_ybs = sem("ssm_branch_ready")
        s_bia = [sem(f"bias_loaded{i}") for i in range(2)]
        s_qkp = sem("head_pair_staged")
        s_s = sem("scores_ready")
        s_sb = sem("scores_biased")
        s_mx = sem("max_ready")
        s_am = sem("neg_max_ready")
        s_e = sem("probs_ready")
        s_t = sem("probs_transposed")
        s_tc = sem("probs_transposed_copied")
        s_o = sem("attn_out_ready")
        s_dn = sem("denominator_inverted")
        s_oc = sem("attn_out_scaled")
        s_ot = sem("attn_out_transposed")
        s_yba = sem("attn_branch_ready")
        s_br = sem("branch_tile_ready")
        s_sg = sem("gate_ready")
        s_bt = sem("gated_tile")
        s_mz = sem("mix_zeroed")
        s_bm = sem("mix_tile_ready")
        s_wo = sem("w_out_tile_ready")
        s_th = sem("late_unit_hi")
        s_tl = sem("late_unit_lo")
        s_eh = sem("early_unit_hi")
        s_ed = sem("early_unit_lo_vector")
        s_ep = sem("early_unit_lo_gpsimd")
        s_eih = sem("early_input_hi")
        s_eil = sem("early_input_lo")
        s_ih = sem("late_input_hi")
        s_il = sem("late_input_lo")
        s_lbh = sem("late_branch_hi")
        s_lbl = sem("late_branch_lo")
        s_xh = sem("ffn_input_hi")
        s_xl = sem("ffn_input_lo")
        s_wh = sem("weight_unit_hi")
        s_wl = sem("weight_unit_lo")
        s_wu = sem("weight_unit_used")
        s_si = sem("silu_ready")
        s_hm = sem("hidden_ready")
        s_ht = sem("hidden_transposed")
        s_hh = sem("hidden_hi")
        s_hl = sem("hidden_lo")
        s_rl = sem("router_ready")
        s_rc = sem("router_chain")
        s_re = sem("router_exp_ready")
        s_rp = sem("positions_ready")
        s_rr = sem("passes_ready")
        s_xq = sem("xn_token_major_ready")
        s_xqc = sem("xn_token_major_copied")
        s_g = sem("gather_ready")
        s_gw = sem("gather_weighted")
        s_xg = sem("tokens_gathered")
        s_xgc = sem("tokens_gathered_copied")
        s_edc = sem("expert_down_copied")
        s_st = sem("scatter_transposed")
        s_stc = sem("scatter_copied")
        s_eo = sem("expert_out_tile")
        s_ea = sem("expert_out_added")
        s_pl = sem("ple_tile_ready")
        s_pg = sem("ple_gate_ready")
        s_pt = sem("ple_term_ready")
        s_out = sem("out_written")
        s_step = sem("pool_step")

        def wait_block(eng, r, j):
            eng.wait_ge(s_loaded[j % RING], (r + (j // RING + 1)) * 16)

        def load_block(eng, j, src, used=None):
            if used is not None:
                eng.wait_ge(*used)
            eng.dma_start(ring[:, j % RING, :], src).then_inc(s_loaded[j % RING], 16)

        def skip_block(eng, j, used):
            if used is not None:
                eng.wait_ge(*used)
            eng.sem_inc(s_loaded[j % RING], 16)

        def mixer_used(l, j):
            if j < PROJ_BLOCKS:
                return s_pj, l * N_PROJ + (2 * j + 2 + (1 if j >= 9 else 0))
            if j < MIX_BLOCKS - LATE_BLOCKS:
                b, k = divmod(j - PROJ_BLOCKS, BRANCH_BLOCKS)
                return s_br, l * (N_BRANCHES * KT) + (b * KT + (2, 4, 4, 6, 8, 8)[k])
            return s_tl, l * LATE_UNITS + 2 * (j - (MIX_BLOCKS - LATE_BLOCKS) + 1)

        def split_used(block):
            return s_wl, 2 * block + (2 - 2 * RING)

        def ple_used(l, j):
            return s_pl, l * KT + (KT + (KT if j == PLE_BLOCKS - 1 else 2 * j + 2))

        def xn_high(k):
            return (hhi if k < KT // 2 else hlo)[:, k % 4 // 2, k % 2, :]

        def proj_tiles(j):
            return 2 * j + 2 + (1 if j >= 9 else 0)

        def tile_w(j, half):
            return [ring[:, j % RING, k * COLS + half * P:k * COLS + half * P + P] for k in range(KT)]

        block = ctx.enter_context(nc.Block())

        @block.sync
        def _(sp):
            sp.dma_start(h[:, :, :], x).then_inc(s_x, 16)
            sp.dma_start(onehot_sb, onehot).then_inc(s_relL, 16)
            sp.dma_start(cst[:, :], cst_in).then_inc(s_cst, 16)
            sp.dma_start(pk[:, :], pk_in[0]).then_inc(s_pk, 16)

            def load_ple(l, used):
                for j in range(PLE_BLOCKS):
                    load_block(sp, j, wp[l, j], used(j))
                for j in range(PLE_BLOCKS, RING):
                    skip_block(sp, j, used(j))

            with sp.Fori(0, DEPTH) as l:
                for j in range(MIX_BLOCKS):
                    if j < PLE_BLOCKS:
                        used = ple_used(l - 1, j)
                    else:
                        used = mixer_used(l, j - RING) if j >= RING else None
                    load_block(sp, j, wm[l, j], used)
                for j in range(MIX_BLOCKS, MIX_ROUNDS * RING):
                    skip_block(sp, j, mixer_used(l, j - RING))

                def first_used(j):
                    at = MIX_ROUNDS * RING - RING + j
                    return mixer_used(l, at) if at < MIX_BLOCKS else None

                with sp.If(l < 1):
                    for j in range(RING):
                        load_block(sp, j, wd[j], first_used(j))
                    with sp.Fori(1, DENSE_CHUNKS // 2) as i:
                        for j in range(RING):
                            load_block(sp, j, wd[i * RING + j], split_used(i * RING + j))
                    for j in range(3):
                        load_block(sp, j, wd[DENSE_CHUNKS // 2 * RING + j], split_used(DENSE_BLOCKS - 3 + j))
                    for j in range(3, RING):
                        skip_block(sp, j, split_used(DENSE_BLOCKS - 3 + j))
                    load_ple(0, lambda j: split_used(DENSE_BLOCKS + 3 + j) if j < 3 else None)
                with sp.Else():
                    for j in range(RING):
                        load_block(sp, j, we[j], first_used(j))
                    def load_round(i, n):
                        for j in range(FIRST_BLOCKS, FIRST_BLOCKS + RING):
                            load_block(sp, j, we[i * RING + j], split_used(i * RING + (n * RING + DENSE_BLOCKS + j)))

                    for j in range(RING, RING + FIRST_BLOCKS):
                        load_block(sp, j, we[j], split_used(DENSE_BLOCKS + j))
                    with sp.Fori(1, N_EXPERTS * PASS_ROUNDS) as i:
                        load_round(i, 0)

                    def finish(n):
                        at = DENSE_BLOCKS + n * PASS_ROUNDS * RING
                        for j in range(FIRST_BLOCKS, RING):
                            skip_block(sp, j, split_used(at + j))
                        load_ple(1, lambda j: split_used(at + RING + j) if j < FIRST_BLOCKS else None)

                    sp.wait_ge(s_rr, 1)
                    n = sp.value_load(passes_sb[0:1, 0:1], min_val=N_EXPERTS, max_val=MAX_PASSES)
                    with sp.If(n > N_EXPERTS):
                        with sp.Fori(0, N_EXPERTS * PASS_ROUNDS) as i:
                            load_round(i, N_EXPERTS * PASS_ROUNDS)
                        finish(MAX_PASSES)
                    with sp.Else():
                        finish(N_EXPERTS)
            sp.wait_ge(s_xn, KT * (2 * DEPTH + 1))
            sp.dma_start(out, xn[:, :, :]).then_inc(s_out, 16)
            sp.wait_ge(s_out, 16)

        @block.tensor
        def _(pe):
            def chain(dst, lhs, rhs):
                for k, (a, b) in enumerate(zip(lhs, rhs)):
                    m = pe.matmul(dst, a, b, start=k == 0, stop=k == len(lhs) - 1)
                return m

            def norm_sum(k, j):
                pe.wait_ge(s_sq, k * KT + (j + 1))
                m = pe.matmul(bank(7, 0, SEQ), con("ones"), mix[:, j, :], start=j == 0, stop=j == KT - 1,
                              skip_group_check=True)
                if j == KT - 1:
                    m.then_inc(s_ms, 1)

            def project(l):
                base = l * N_PROJ

                def room(t):
                    if t >= 4:
                        pe.wait_ge(s_pf, base + (t - 3))

                def weights(j, k, lo, n):
                    at = (k % 4) * COLS + lo
                    return (whi[:, (2 * j + k // 4) % SLOTS, at:at + n],
                            ring_lo[:, j % RING, k * COLS + lo:k * COLS + lo + n])

                def product(dst, j, operands, first):
                    for k in range(KT):
                        if first and k % 4 == 0:
                            if (j, k // 4) in EARLY_POOL:
                                pe.wait_ge(s_ep, l * len(EARLY_POOL) + (EARLY_POOL.index((j, k // 4)) + 1))
                            else:
                                pe.wait_ge(s_ed, l * EARLY_DVE + (j // 2 + 1))
                        if first and j == 0 and k % 2 == 0:
                            pe.wait_ge(s_eil, l * 4 + (k // 2 + 1))
                        m = three(dst, *operands(k), k == 0, k == KT - 1)
                    m.then_inc(s_pj, 1)

                def feature_major(j, t):
                    for half in range(2):
                        room(t + half)
                        product(bank((t + half) % 4, 0, SEQ), j,
                                lambda k: (weights(j, k, half * P, P), (xn_high(k), xlo[:, k, :])), half == 0)

                def token_major(j, t):
                    for tt in range(TT):
                        room(t + tt)
                        sl = slice(tt * P, tt * P + P)
                        product(bank((t + tt) % 4, 0, COLS), j,
                                lambda k: ((xn_high(k)[:, sl], xlo[:, k, sl]), weights(j, k, 0, COLS)), tt == 0)

                pe.wait_ge(s_xn, l * (2 * KT) + KT)
                t = 0
                for j in range(7):
                    feature_major(j, t)
                    t += 2
                for j in range(7, 9):
                    token_major(j, t)
                    t += 2
                room(t)
                pe.wait_ge(s_pk, l * 16 + 16)
                for tt in range(TT):
                    m = chain(bank(t % 4, tt * DT, DT), [xn[:, k, tt * P:tt * P + P] for k in range(KT)],
                              [par("w_dt", k * DT, DT) for k in range(KT)])
                m.then_inc(s_pj, 1)
                t += 1
                for j in range(9, 11):
                    feature_major(j, t)
                    t += 2
                assert t == T_V
                for j in range(11, 17):
                    token_major(j, t)
                    t += 2
                assert t == T_Q

            def query_key(l, i, t):
                j = 17 + t // 2
                if t % 2 == 0:
                    wait_block(pe, l * LAYER0_ROUNDS + i, j)
                pe.wait_ge(s_pf, l * N_PROJ + i * 12 + (T_Q + t - 3))
                chain(bank(4 + t % 4, 0, SEQ), tile_w(j, t % 2),
                      [xn[:, k, :] for k in range(KT)]).then_inc(s_pj, 1)

            def fnet(l):
                pe.wait_ge(s_pf, l * N_PROJ + T_Q)
                for g in range(FNET_GROUPS):
                    if g >= 2:
                        pe.wait_ge(s_f1c, l * FNET_GROUPS + (g - 1))
                    for tt in range(TT):
                        m = pe.matmul(bank(4 + g % 2, tt * 2 * P, 2 * P), fu[:, g, tt * P:tt * P + P],
                                      con("dft_ch", 0, 2 * P), start=True, stop=True)
                    m.then_inc(s_f1, 1)
                    if g >= 1:
                        fnet_tokens(l, g - 1)
                fnet_tokens(l, FNET_GROUPS - 1)

            def fnet_tokens(l, g):
                pe.wait_ge(s_f1c, l * FNET_GROUPS + (g + 1))
                if g >= 2:
                    pe.wait_ge(s_f2c, l * FNET_GROUPS + (g - 1))
                lhs = [fa[:, g % 2, tt, part * P:part * P + P] for part in range(2) for tt in range(TT)]
                rhs = [con(name, tt * SEQ, SEQ) for name in ("dft_cos", "dft_sin") for tt in range(TT)]
                chain(bank(6 if g % 2 == 0 else 3, 0, SEQ), lhs, rhs).then_inc(s_f2, 1)

            def conv_norm(l, second):
                if second:
                    pe.wait_ge(s_lnc, l * 5 + 2)
                else:
                    pe.wait_ge(s_cvw, l * (CT * CONV_K) + CT * CONV_K)
                chain(bank(7, second * SEQ, SEQ), [con("ones")] * CT, [cv[:, t, :] for t in range(CT)]).then_inc(s_lns, 1)

            def x_token_major(l):
                pe.wait_ge(s_xa, l * XT + XT)
                pe.wait_ge(s_f1c, l * FNET_GROUPS + FNET_GROUPS)
                for tt in range(TT):
                    for c in range(CT):
                        m = pe.transpose(bank(4 + tt, c * P, P), xbc[:, c, tt * P:tt * P + P], con("ident"))
                    m.then_inc(s_xt, 1)

            def ssm_prep(l):
                pe.wait_ge(s_f2c, l * FNET_GROUPS + FNET_GROUPS)
                for g in range(SSM_GROUPS):
                    if g == 1:
                        pe.wait_ge(s_lnc, l * 5 + 3)
                    lo = g * SSM_STATE
                    for tt in range(TT):
                        m = pe.matmul(bank(6 + g, tt * SEQ, SEQ), xbc[lo:lo + SSM_STATE, CT, tt * P:tt * P + P],
                                      xbc[lo:lo + SSM_STATE, CT + 1, :], start=True, stop=True)
                    m.then_inc(s_bc, 1)

            def ssm_heads(l):
                with pe.Fori(0, 2) as i:
                    pe.wait_ge(s_pf, l * N_PROJ + T_Q)
                    pe.wait_ge(s_xtc, l * TT + TT)
                    pe.wait_ge(s_sc, l * 2 + 2)
                    for step in range(2):
                        n = l * SSM_HEADS + i * 4 + 2 * step
                        for g in range(SSM_GROUPS):
                            pe.wait_ge(s_ua, n + (g + 1))
                            for part in range(4):
                                m = pe.matmul(bank(g, part * P, P), con("ones"), ua[:, g, part, :], start=True, stop=True)
                            m.then_inc(s_r, 1)
                        for t in range(4):
                            query_key(l, i, 4 * step + t)
                        for g in range(SSM_GROUPS):
                            pe.wait_ge(s_mm, n + (g + 1))
                            for tt, parts in enumerate((((0, 0), (3, 0), (4, 1)), ((1, 0), (2, 1), (5, 1)))):
                                m = chain(bank(2 + g, tt * 64, 64), [mm_[:, g, b, :] for b, _ in parts],
                                          [xs[:, s, bass.ds(i * P + (step * 64 + g * 256), 64)] for _, s in parts])
                            m.then_inc(s_y, 1)
                    for t in range(8, 12):
                        query_key(l, i, t)

            def ssm_out(l):
                pe.wait_ge(s_yc, l * SSM_YC + SSM_YC)
                pe.wait_ge(s_pf, l * N_PROJ + N_PROJ)
                for c in range(CT):
                    for tt in range(TT):
                        m = pe.transpose(bank(4 + c // 2, (c % 2) * SEQ + tt * P, P), ys[:, tt, c * P:c * P + P],
                                         con("ident"))
                m.then_inc(s_yt, 1)

            def branch_tile(l, b, m_):
                r = l * LAYER0_ROUNDS + b
                out_j = PROJ_BLOCKS + 3 * (m_ // 4) + 1
                j = out_j + (1 if m_ % 4 >= 2 else -1)
                if m_ % 2 == 0:
                    wait_block(pe, r, j)
                if m_ % 4 == 0:
                    wait_block(pe, r, out_j)
                pe.wait_ge(s_bm, l * (N_BRANCHES * KT) + b * KT + (m_ + 1))
                col = (m_ % 4) * P
                chain(bank(6 + m_ % 2, 0, SEQ),
                      [ring[:, out_j % RING, c * 512 + col:c * 512 + col + P] for c in range(CT)],
                      [ybr[:, b * CT + c, :] for c in range(CT)])
                chain(bank(6 + m_ % 2, SEQ, SEQ), tile_w(j, m_ % 2), [xn[:, k, :] for k in range(KT)]).then_inc(s_br, 1)

            def pair(l, i, half):
                n = l * UNITS + i * 8 + 4 * half
                pe.wait_ge(s_qkp, l * (2 * HP) + i * 4 + (2 * half + 2))

                def scores(u):
                    lo = 64 * (u // TT)
                    if u:
                        pe.wait_ge(s_sb, n + u)
                    for g in range(ATT_GROUPS):
                        m = pe.matmul(bank(4, g * SEQ, SEQ),
                                      qkp[lo:lo + 64, 0, g, (u % TT) * P:(u % TT) * P + P],
                                      qkp[lo:lo + 64, 1, g, :], start=True, stop=True)
                    m.then_inc(s_s, 1)

                def transposes(u):
                    pe.wait_ge(s_e, n + (u + 1))
                    if u >= 2:
                        pe.wait_ge(s_oc, n + (u - 1))
                    for b in range(2 * ATT_GROUPS):
                        m = pe.transpose(bank(2 * (u % 2), b * P, P), sa[:, u % 2, b * P:b * P + P], con("ident"))
                    m.then_inc(s_t, 1)

                def values(u):
                    pe.wait_ge(s_tc, n + (u + 1))
                    chain(bank(2 * (u % 2), GK, 64), [pt[:, u % 2, b * P:b * P + P] for b in range(6)],
                          [v[:, b % 2, bass.ds(i * (2 * P) + (half * P + b // 2 * ATT_WIDTH + 64 * (u // TT)), 64)]
                           for b in range(6)]).then_inc(s_o, 1)

                def tile(k):
                    branch_tile(l, i, 4 * half + k)

                scores(0)
                tile(0)
                scores(1)
                transposes(0)
                tile(1)
                scores(2)
                transposes(1)
                values(0)
                tile(2)
                scores(3)
                values(1)
                transposes(2)
                tile(3)
                transposes(3)
                values(2)
                values(3)

            def attention(l):
                with pe.Fori(0, HB) as i:
                    pe.wait_ge(s_ybs, l + 1)
                    pe.wait_ge(s_yc, l * SSM_YC + 1)
                    pe.wait_ge(s_lna, l * (CT + 1) + (CT + 1))
                    for half in range(2):
                        pair(l, i, half)
                pe.wait_ge(s_oc, l * UNITS + UNITS)
                for c in range(CT):
                    for tt in range(TT):
                        m = pe.transpose(bank(c // 2, (c % 2) * SEQ + tt * P, P), ao[:, tt, c * P:c * P + P],
                                         con("ident"))
                m.then_inc(s_ot, 1)

            def three(dst, lhs, rhs, first, last):
                pe.matmul(dst, lhs[0], rhs[0], start=first, stop=False, skip_group_check=True)
                pe.matmul(dst, lhs[0], rhs[1], start=False, stop=False, skip_group_check=True)
                return pe.matmul(dst, lhs[1], rhs[0], start=False, stop=last, skip_group_check=True)

            def both(hi, lo, *at):
                return hi[at], lo[at]

            def branches(l):
                with pe.Fori(HB, N_BRANCHES) as b:
                    units = l * LATE_UNITS + b * BRANCH_UNITS + (-HB * BRANCH_UNITS)
                    for m_ in range(KT):
                        if m_ >= 4:
                            pe.wait_ge(s_bm, l * (N_BRANCHES * KT) + b * KT + (m_ - 1))
                        else:
                            pe.wait_ge(s_bm, l * (N_BRANCHES * KT) + b * KT + 2)
                        first = m_ // 4 * 6 + (m_ % 4 // 2) * 4
                        for u in range(2):
                            pe.wait_ge(s_tl, units + (first + u + 1))
                            for k in range(4 * u, 4 * u + 4):
                                if k % 2 == 0:
                                    pe.wait_ge(s_il, l * KT + (k // 2 + 1))
                                col = (k % 4) * COLS + (m_ % 2) * P
                                three(bank(4 + m_ % 4, SEQ, SEQ),
                                      both(whi, wlo, slice(None), (first + u) % SLOTS, slice(col, col + P)),
                                      both(xhi, xlo, slice(None), k), k == 0, k == KT - 1)
                        pe.wait_ge(s_lbl, l * HB + b + (1 - HB))
                        for c in range(CT):
                            at = m_ // 4 * 6 + 2 + c // 2
                            pe.wait_ge(s_tl, units + (at + 1))
                            col = (c % 2) * 512 + (m_ % 4) * P
                            m = three(bank(4 + m_ % 4, 0, SEQ), both(whi, wlo, slice(None), at % SLOTS, slice(col, col + P)),
                                      both(hhi, hlo, slice(None), c // 2, c % 2), c == 0, c == CT - 1)
                        m.then_inc(s_br, 1)

            def mix_out(l):
                pe.wait_ge(s_bm, (l + 1) * (N_BRANCHES * KT) + 2)
                units = l * LATE_UNITS + HB * BRANCH_UNITS
                for m_ in range(KT):
                    if m_ >= 4:
                        pe.wait_ge(s_hr, l * (2 * KT) + (m_ - 3))
                    for u in range(2):
                        unit = m_ // 2 * 2 + u
                        pe.wait_ge(s_tl, units + (unit + 1))
                        for k in range(4 * u, 4 * u + 4):
                            if k % 2 == 0:
                                pe.wait_ge(s_il, l * KT + (4 + k // 2 + 1))
                            col = (k % 4) * COLS + (m_ % 2) * P
                            m = three(bank(m_ % 4, 0, SEQ), both(whi, wlo, slice(None), unit % SLOTS, slice(col, col + P)),
                                      both(xhi, xlo, slice(None), k), k == 0, k == KT - 1)
                    m.then_inc(s_wo, 1)
                    if m_ >= 2:
                        norm_sum(l * 2 + 1, m_ - 2)
                norm_sum(l * 2 + 1, KT - 2)
                norm_sum(l * 2 + 1, KT - 1)

            def dense():
                def up(c, slot, units):
                    if c is not None:
                        pe.wait_ge(s_hm, c)
                    for u in range(4):
                        pe.wait_ge(s_wl, units + (u + 1))
                        for k in (2 * u, 2 * u + 1):
                            if slot == 0 and c is None and k % 2 == 0:
                                pe.wait_ge(s_xl, u + 1)
                            for t in range(4):
                                col = (k % 2) * 512 + t * P
                                m = three(bank(t, 0, SEQ), both(whi, wlo, slice(None), (slot + u) % SLOTS,
                                                                slice(col, col + P)),
                                          both(xhi, xlo, slice(None), k), k == 0, k == KT - 1)
                        m.then_inc(s_wu, 1)

                def down(c, slot, units, par_, first=False, last=False):
                    pe.wait_ge(s_hl, c + 1)
                    for half in range(2):
                        pe.wait_ge(s_wl, units + (half + 1))
                        for m_ in range(KT):
                            m = three(bank(4 + m_ // 2, (m_ % 2) * SEQ, SEQ),
                                      both(whi, wlo, slice(None), (slot + half) % SLOTS, slice(m_ * P, m_ * P + P)),
                                      both(hhi, hlo, slice(None), par_, half),
                                      first and half == 0 and m_ % 2 == 0, last and half == 1)
                        m.then_inc(s_wu, 1)

                up(None, 0, 0)
                up(1, 4, 4)
                down(0, 2, 8, 0, first=True)
                with pe.Fori(0, (DENSE_CHUNKS - 3) // 2) as i:
                    for c in range(2):
                        up(i * 2 + (c + 2), 4, i * 12 + (10 + 6 * c))
                        down(i * 2 + (c + 1), 2, i * 12 + (14 + 6 * c), (c + 1) % 2)
                c = DENSE_CHUNKS - 2
                up(c + 1, 4, 6 * c + 4)
                down(c, 2, 6 * c + 8, c % 2)
                down(c + 1, 4, 6 * c + 10, (c + 1) % 2, last=True)

            def route():
                pe.wait_ge(s_xn, 4 * KT)
                for tt in range(TT):
                    m = chain(bank(4, tt * N_EXPERTS, N_EXPERTS), [xn[:, k, tt * P:tt * P + P] for k in range(KT)],
                              [par("router", k * N_EXPERTS, N_EXPERTS) for k in range(KT)])
                m.then_inc(s_rl, 1)
                for tt in range(TT):
                    for k in range(KT):
                        m = pe.transpose(bank(2 * tt + k // 4, (k % 4) * P, P), xn[:, k, tt * P:tt * P + P], con("ident"))
                        if k % 4 == 3:
                            m.then_inc(s_xq, 1)
                pe.wait_ge(s_rc, RC_MASK)
                chain(bank(5, 0, N_EXPERTS), [con("before")], [msk[:, 0, :]])
                chain(bank(5, N_EXPERTS, N_EXPERTS), [con("ones"), con("before")], [msk[:, 0, :], msk[:, 1, :]])
                chain(bank(5, 2 * N_EXPERTS, N_EXPERTS), [con("ones")] * 2,
                      [msk[:, 0, :], msk[:, 1, :]]).then_inc(s_rp, 1)
                pe.wait_ge(s_xqc, 4)

            def experts(passes):
                pe.wait_ge(s_rr, 1)
                n_p = pe.value_load(passes_sb[0:1, 0:1], min_val=N_EXPERTS, max_val=MAX_PASSES)
                pe.reg_mov(passes, n_p)

                def gather(n):
                    pe.wait_ge(s_gw, n + 1)
                    for k in range(KT):
                        m = chain(bank(6 + k // 4, (k % 4) * P, P),
                                  [mix[:, tt * 4 + k // 2, (k % 2) * P:(k % 2) * P + P] for tt in range(TT)],
                                  [gat[:, tt, :] for tt in range(TT)])
                        if k % 4 == 3:
                            m.then_inc(s_xg, 1)

                def up_unit(cc, u, slot, units):
                    pe.wait_ge(s_wl, units + (u + 1))
                    for k in (2 * u, 2 * u + 1):
                        col = (k % 2) * 512
                        m = three(bank(cc % 2), both(xhi, xlo, slice(None), k, slice(0, P)),
                                  both(whi, wlo, slice(None), (slot + u) % SLOTS, slice(col, col + 512)),
                                  k == 0, k == KT - 1)
                    m.then_inc(s_wu, 1)

                def scatter(n, m_):
                    pe.wait_ge(s_ea, n * KT + (m_ + 1))
                    pe.matmul(bank(6 + m_ % 2, 0, SEQ), yx[:, m_ * P:m_ * P + P], sca[:, :],
                              start=True, stop=True).then_inc(s_eo, 1)

                gather(0)
                pe.wait_ge(s_stc, 1)
                for q in range(4):
                    pe.matmul(bank(4 + q // 2, (q % 2) * SEQ, SEQ), con("ident"), sca[:, :], start=True, stop=True)
                for u in range(4):
                    if u % 2 == 0:
                        pe.wait_ge(s_xl, 4 + u // 2 + 1)
                    up_unit(0, u, 0, DENSE_UNITS)
                with pe.Fori(0, n_p) as q:
                    c0 = q * EXP_CHUNKS + DENSE_CHUNKS
                    u0 = q * PASS_UNITS + (DENSE_UNITS + FIRST_UNITS)

                    def step(k, cc, between=None):
                        units = u0 + k * 6
                        pe.wait_ge(s_hm, c0 + k)
                        for u in range(4):
                            if cc == EXP_CHUNKS - 1 and u % 2 == 0:
                                pe.wait_ge(s_xl, q * 2 + (6 + u // 2 + 1))
                            up_unit(cc + 1, u, 4, units)
                            if cc == 1:
                                scatter(q, 2 + u)
                            if u == 1:
                                pe.wait_ge(s_hm, c0 + k + 1)
                                for half in range(2):
                                    m = pe.transpose(bank(2 + cc % 2, half * P, P), gt[:, 0, half * P:half * P + P],
                                                     con("ident"))
                                m.then_inc(s_ht, 1)
                        if cc == EXP_CHUNKS - 2:
                            pe.wait_ge(s_stc, q + 2)
                            gather(q + 1)
                        if cc == 0:
                            pe.wait_ge(s_edc, q + 1)
                        pe.wait_ge(s_hl, c0 + k + 1)
                        for half in range(2):
                            pe.wait_ge(s_wl, units + (5 + half))
                            for col in range(0, D_MODEL, 512):
                                m = three(bank(4 + col // 512), both(hhi, hlo, slice(None), cc % 2, half, slice(0, P)),
                                          both(whi, wlo, slice(None), 2 + half, slice(col, col + 512)),
                                          cc == 0 and half == 0, cc == EXP_CHUNKS - 1 and half == 1)
                            m.then_inc(s_wu, 1)

                    step(0, 0)
                    pe.wait_ge(s_stc, q + 1)
                    scatter(q, 0)
                    scatter(q, 1)
                    step(1, 1)
                    scatter(q, 6)
                    scatter(q, 7)
                    step(2, 2)
                    step(3, 3)
                    with pe.Fori(2, EXP_CHUNKS // 2 - 1) as i:
                        for c in range(2):
                            step(i * 2 + c, 4 + c)
                    pe.wait_ge(s_ea, q * KT + (KT + 2))
                    for tt in range(TT):
                        m = pe.transpose(bank(6, tt * P, P), gatw[:, tt, :], con("ident"))
                    m.then_inc(s_st, 1)
                    step(EXP_CHUNKS - 2, EXP_CHUNKS - 2)
                    step(EXP_CHUNKS - 1, EXP_CHUNKS - 1)
                done = pe.snap(passes, min_val=N_EXPERTS, max_val=MAX_PASSES)
                pe.wait_ge(s_edc, done + 1)
                pe.wait_ge(s_stc, done + 1)
                for m_ in range(KT):
                    scatter(done, m_)

            def ple(l, passes):
                pe.wait_ge(s_h, l + 1)
                r = l * (LAYER0_ROUNDS - DENSE_ROUNDS) + pe.snap(passes, min_val=0, max_val=MAX_PASSES) * PASS_ROUNDS \
                    + l + (MIX_ROUNDS + DENSE_ROUNDS)
                wait_block(pe, r, 4)
                for m_ in range(KT):
                    if m_ % 2 == 0:
                        wait_block(pe, r, m_ // 2)
                    if m_ >= 2:
                        pe.wait_ge(s_pt, l * KT + (m_ - 1))
                    chain(bank(2 * (m_ % 2), 0, SEQ), [ring[:, 4, c * D_MODEL + m_ * P:c * D_MODEL + m_ * P + P]
                                                      for c in range(PLE_DIM // P)],
                          [par("p", c * SEQ, SEQ) for c in range(PLE_DIM // P)])
                    m = chain(bank(2 * (m_ % 2) + 1, 0, SEQ), tile_w(m_ // 2, m_ % 2), [h[:, k, :] for k in range(KT)])
                    m.then_inc(s_pl, 1)

            pe.sem_inc(s_pl, KT)
            pe.sem_inc(s_wu, SLOTS)
            pe.sem_inc(s_r, 2)
            pe.sem_inc(s_s, 1)
            passes = pe.alloc_register("passes_pe")
            pe.wait_ge(s_relL, 32)
            for g in range(ATT_GROUPS):
                m = pe.matmul(ps[0:ATT_HEADS, g * 512:g * 512 + 512],
                              relb_sb[:, g * ATT_HEADS:(g + 1) * ATT_HEADS],
                              onehot_sb[:, g, :], start=True, stop=True)
            m.then_inc(s_relT, 1)
            pe.wait_ge(s_cst, 16)
            for j in range(KT):
                norm_sum(0, j)
            with pe.Fori(0, DEPTH) as l:
                project(l)
                fnet(l)
                conv_norm(l, 0)
                x_token_major(l)
                conv_norm(l, 1)
                ssm_prep(l)
                ssm_heads(l)
                ssm_out(l)
                attention(l)
                branches(l)
                mix_out(l)
                pe.reg_mov(passes, 0)
                with pe.If(l < 1):
                    dense()
                with pe.Else():
                    route()
                    experts(passes)
                ple(l, passes)
                for j in range(KT):
                    norm_sum(l * 2 + 2, j)

        @block.scalar
        def _(act):
            def squares(ready):
                for j in range(KT):
                    if ready is not None:
                        act.wait_ge(s_hr, ready + (j + 1))
                    act.activation(mix[:, j, :], h[:, j, :], ACT.Square).then_inc(s_sq, 1)

            def norm_root(k):
                act.wait_ge(s_var, k + 1)
                act.activation(rms_t[:, 1, :], rms_t[:, 0, :], ACT.Sqrt).then_inc(s_sd, 1)

            def project(l):
                base = l * N_PROJ

                def tile(t, dst, func=ACT.Copy, rows=(0, SEQ)):
                    act.wait_ge(s_pj, base + (t + 1))
                    act.activation(dst, bank(t % 4, *rows), func).then_inc(s_pf, 1)

                def early_highs(j):
                    if j < EARLY_BLOCKS:
                        if j >= 3:
                            act.wait_ge(s_pj, base + proj_tiles(j - 3))
                        act.wait_ge(s_loaded[j % RING], (l * LAYER0_ROUNDS + (j // RING + 1)) * 16)
                        for u in range(2):
                            act.activation(whi[:, (2 * j + u) % SLOTS, :], ring[:, j % RING, u * UNIT:u * UNIT + UNIT],
                                           ACT.Copy).then_inc(s_eh, 1)

                early_highs(0)
                early_highs(1)
                for k in range(4):
                    act.wait_ge(s_xn, l * (2 * KT) + (2 * k + 2))
                    act.activation((hhi if k < 2 else hlo)[:, k % 2, :, :], xn[:, 2 * k:2 * k + 2, :],
                                   ACT.Copy).then_inc(s_eih, 1)
                early_highs(2)
                act.wait_ge(s_pk, l * 16 + 16)
                for pair in range(2):
                    for c in range(2):
                        tile(4 * pair + c, glu_a[:, pair, c, :])
                    early_highs(2 * pair + 3)
                    for c in range(2):
                        tile(4 * pair + 2 + c, glu_s[:, pair, c, :], ACT.Sigmoid)
                    early_highs(2 * pair + 4)
                for c in range(XT):
                    tile(T_XBC + c, xbcp[:, c, SPAD:SPAD + SEQ])
                    if c % 2:
                        early_highs(7 + c // 2)
                act.wait_ge(s_relW, 16)
                for j in range(2):
                    for tt in range(TT):
                        tile(T_Z + 2 * j + tt, z[:, tt, j * COLS:(j + 1) * COLS], ACT.Silu)
                    early_highs(10 + j)
                tile(T_DT, dts[:, 0, :], rows=(0, TT * DT))
                for g in range(FNET_GROUPS):
                    tile(T_FN + g, fu[:, g, :])
                    if g % 2:
                        early_highs(12 + g // 2)
                for j in range(6):
                    if j == 4:
                        ssm(l)
                        dt_exps(l)
                    for tt in range(TT):
                        tile(T_V + 2 * j + tt, v[:, tt, j * COLS:(j + 1) * COLS])
                    early_highs(14 + j)

            def dt_exps(l):
                act.wait_ge(s_dtc, l * DTC + 3)
                act.activation(dts[:, 3, :], dts[:, 2, :], ACT.Exp).then_inc(s_dta, 1)
                act.activation(a_neg[:, :], par("a_log", 0, DT), ACT.Exp).then_inc(s_dta, 1)

            def fnet(l):
                for g in range(FNET_GROUPS):
                    act.wait_ge(s_f1, l * FNET_GROUPS + (g + 1))
                    if g >= 2:
                        act.wait_ge(s_f2, l * FNET_GROUPS + (g - 1))
                    act.activation(fa[:, g % 2, :, :], bank(4 + g % 2).rearrange("p (t c) -> p t c", t=TT),
                                   ACT.Copy).then_inc(s_f1c, 1)
                    if g >= 1:
                        fnet_tokens(l, g - 1)
                fnet_tokens(l, FNET_GROUPS - 1)

            def fnet_tokens(l, g):
                act.wait_ge(s_f2, l * FNET_GROUPS + (g + 1))
                act.activation(ybr[:, FNET * CT + g, :], bank(6 if g % 2 == 0 else 3, 0, SEQ),
                               ACT.Copy).then_inc(s_f2c, 1)

            def ssm(l):
                for c in range(XT):
                    act.wait_ge(s_xc, l * (XT * SSM_CONV) + (c + 1) * SSM_CONV)
                    act.activation(xbc[:, c, :], xbc[:, c, :], ACT.Silu).then_inc(s_xa, 1)

            def conv_norm(l):
                act.wait_ge(s_lnc, l * 5 + 3)
                act.activation(rms_t[:, 1, :], rms_t[:, 0, :], ACT.Sqrt).then_inc(s_lna, 1)
                act.wait_ge(s_lnc, l * 5 + 5)
                for c in range(CT):
                    act.activation(ybr[:, CONV * CT + c, :], cvx[:, c, :], ACT.Silu, bias=par("ln_b", c),
                                   scale=par("ln_g", c)).then_inc(s_lna, 1)

            def ssm_heads(l):
                for tt in range(TT):
                    act.wait_ge(s_xt, l * TT + (tt + 1))
                    act.activation(xs[:, tt, :], bank(4 + tt), ACT.Copy).then_inc(s_xtc, 1)
                with act.Fori(0, 2) as i:
                    def query_key(t):
                        act.wait_ge(s_pj, l * N_PROJ + i * 12 + (T_Q + t + 1))
                        act.activation(qk[:, bass.ds(i * ATT_GROUPS + t // HP, 1), t % HP, :], bank(4 + t % 4, 0, SEQ),
                                       ACT.Copy).then_inc(s_pf, 1)

                    for step in range(2):
                        n = l * SSM_HEADS + i * 4 + 2 * step
                        for g in range(SSM_GROUPS):
                            query_key(4 * step + g)
                            act.wait_ge(s_hc, (n + g) * SSM_HC + SSM_HC)
                            act.activation(ex[:, g, :, :], ex[:, g, :, :], ACT.Exp).then_inc(s_ex, 1)
                        query_key(4 * step + 2)
                        query_key(4 * step + 3)
                    for t in range(8, 12):
                        query_key(t)
                act.wait_ge(s_yc, l * SSM_YC + 4)
                act.activation(yst[:, 4:6], yst[:, 2:4], ACT.Sqrt).then_inc(s_ya, 1)
                act.wait_ge(s_yt, l + 1)
                for c in range(CT):
                    m = act.activation(ybr[:, SSM * CT + c, :], bank(4 + c // 2, (c % 2) * SEQ, SEQ), ACT.Copy,
                                       scale=par("ssm_norm", c))
                m.then_inc(s_ybs, 1)
                act.wait_ge(s_lna, l * (CT + 1) + (CT + 1))
                late_inputs(l)

            def gate(l, b, m_, first_bank=6, banks=2):
                n = l * (N_BRANCHES * KT) + b * KT
                act.wait_ge(s_br, n + (m_ + 1))
                act.wait_ge(s_bm, n + (m_ + 1))
                act.activation(gs[:, m_ % 2, :], bank(first_bank + m_ % banks, SEQ, SEQ), ACT.Sigmoid,
                               bias=pk[:, bass.ds(b * KT + (AT["b_gate"] + m_), 1)]).then_inc(s_sg, 1)

            def pair(l, i, half):
                n = l * UNITS + i * 8 + 4 * half

                def probs(u):
                    act.wait_ge(s_am, n + (u + 1))
                    act.activation(sa[:, u % 2, :], sa[:, u % 2, :], ACT.Exp, bias=ast[:, u % 2, 0:1],
                                   accum_out=ast[:, u % 2, 1:2]).then_inc(s_e, 1)

                def copy_t(u):
                    act.wait_ge(s_t, n + (u + 1))
                    act.activation(pt[:, u % 2, :], bank(2 * (u % 2), 0, GK), ACT.Copy).then_inc(s_tc, 1)

                def tile(k):
                    gate(l, i, 4 * half + k)

                probs(0)
                tile(0)
                probs(1)
                copy_t(0)
                tile(1)
                copy_t(1)
                probs(2)
                tile(2)
                probs(3)
                copy_t(2)
                tile(3)
                copy_t(3)

            def attention(l):
                with act.Fori(0, HB) as i:
                    for half in range(2):
                        pair(l, i, half)
                late_first(l)
                act.wait_ge(s_ot, l + 1)
                for j in range(2):
                    m = act.activation(ybr[:, ATT * CT + 2 * j:ATT * CT + 2 * j + 2, ::-1],
                                       bank(j).rearrange("p (c t) -> p c t", c=2), ACT.Copy)
                m.then_inc(s_yba, 1)

            def late_high(u, r, j):
                act.wait_ge(s_loaded[j % RING], (r + (j // RING + 1)) * 16)
                lo = u % 2 * UNIT
                act.activation(whi[:, u % SLOTS, :], ring[:, j % RING, lo:lo + UNIT], ACT.Copy).then_inc(s_th, 1)

            def late_inputs(l):
                for k in range(4):
                    act.activation(xhi[:, 2 * k:2 * k + 2, :], xn[:, 2 * k:2 * k + 2, :], ACT.Copy).then_inc(s_ih, 1)

            def late_first(l):
                act.wait_ge(s_o, l * UNITS + UNITS)
                for u in range(2):
                    late_high(u, l * LAYER0_ROUNDS + HB, PROJ_BLOCKS)

            def branches(l):
                free_after = (2, 2, 4, 4, 4, 4, 6, 6, 8, 8, 8, 8)
                with act.Fori(HB, N_BRANCHES) as b:
                    done = l * (N_BRANCHES * KT) + b * KT

                    def highs_of(first, n):
                        for u in range(first, first + n):
                            act.wait_ge(s_br, done + (free_after[u - SLOTS] if u >= SLOTS else free_after[u + SLOTS] - KT))
                            late_high(u, l * LAYER0_ROUNDS + b, PROJ_BLOCKS + u // 2)

                    act.wait_ge(s_yba, l + 1)
                    act.wait_ge(s_br, done)
                    act.activation(hhi[:, :, :, :].rearrange("p a b t -> p (a b) t"),
                                   ybr[:, bass.ds(b * CT, CT), :], ACT.Copy).then_inc(s_lbh, 1)
                    highs_of(2, 4)
                    for m_ in range(0, KT, 2):
                        gate(l, b, m_, 4, 4)
                        gate(l, b, m_ + 1, 4, 4)
                        if m_ < 6:
                            highs_of(6 + (0, 2, 6)[m_ // 2], (2, 4, 2)[m_ // 2])
                act.wait_ge(s_br, (l + 1) * (N_BRANCHES * KT))
                for k in range(4):
                    act.wait_ge(s_bm, l * (N_BRANCHES * KT) + ((N_BRANCHES - 1) * KT + 2 * k + 4))
                    act.activation(xhi[:, 2 * k:2 * k + 2, :], mix[:, 2 * k:2 * k + 2, :], ACT.Copy).then_inc(s_ih, 1)
                for u in range(2, 8):
                    if u >= SLOTS:
                        act.wait_ge(s_wo, l * KT + 2)
                    late_high(u, l * LAYER0_ROUNDS + N_BRANCHES, PROJ_BLOCKS + u // 2)

            def high(units, first, u, r, j):
                slot = (first + u) % SLOTS
                act.wait_ge(s_loaded[j % RING], (r + (j // RING + 1)) * 16)
                act.wait_ge(s_wu, units + (u + 1))
                lo = (first + u) % 2 * UNIT
                act.activation(whi[:, slot, :], ring[:, j % RING, lo:lo + UNIT], ACT.Copy).then_inc(s_wh, 1)

            def highs(units, first, n, r, j):
                for u in range(n):
                    high(units, first, u, r, j + (first % 2 + u) // 2)

            def dense():
                for k in range(4):
                    act.wait_ge(s_xn, KT + 2 * k + 2)
                    act.activation(xhi[:, 2 * k:2 * k + 2, :], xn[:, 2 * k:2 * k + 2, :], ACT.Copy).then_inc(s_xh, 1)
                highs(0, 0, 8, MIX_ROUNDS, 0)

                def chunk(c, par_, n, units, r, j, first=False):
                    act.wait_ge(s_wu, (4 if first else c * 6 + 2) + SLOTS)
                    if not first:
                        act.wait_ge(s_hm, c)
                    act.activation(hs[:, :, :], ps[:, 0:1024].rearrange("p (b t) -> p b t", b=2)[:, :, 0:SEQ],
                                   ACT.Silu).then_inc(s_si, 1)
                    if n:
                        highs(units, 2, 1, r, j)
                    act.wait_ge(s_hm, c + 1)
                    act.activation(hhi[:, par_, :, :], hid[:, :, :], ACT.Copy).then_inc(s_hh, 1)
                    for u in range(1, n):
                        high(units, 2, u, r, j + u // 2)

                chunk(0, 0, 6, 8, MIX_ROUNDS, 4, first=True)
                with act.Fori(0, (DENSE_CHUNKS - 3) // 2) as i:
                    for c in range(2):
                        chunk(i * 2 + (c + 1), (c + 1) % 2, 6, i * 12 + (14 + 6 * c), i + MIX_ROUNDS, 7 + 3 * c)
                c = DENSE_CHUNKS - 2
                chunk(c, c % 2, 4, 8 + 6 * c, MIX_ROUNDS, 4 + 3 * c)
                chunk(c + 1, (c + 1) % 2, 0, 0, 0, 0)

            def route():
                act.wait_ge(s_rc, RC_EXP)
                act.activation(rt[:, :, 1:2], rt[:, :, 0:1], ACT.Exp).then_inc(s_re, 1)
                for j in range(4):
                    act.wait_ge(s_xq, j + 1)
                    tt, half = j // 2, j % 2
                    act.activation(mix[:, tt * 4 + half * 2:tt * 4 + half * 2 + 2, :],
                                   bank(2 * tt + half).rearrange("p (c t) -> p c t", c=2), ACT.Copy).then_inc(s_xqc, 1)

            def experts():
                act.wait_ge(s_rr, 1)
                n_p = act.value_load(passes_sb[0:1, 0:1], min_val=N_EXPERTS, max_val=MAX_PASSES)

                def tokens(n):
                    for j in range(2):
                        act.wait_ge(s_xg, n * 2 + (j + 1))
                        act.activation(xhi[:, 4 * j:4 * j + 4, 0:P], bank(6 + j).rearrange("p (c t) -> p c t", c=4),
                                       ACT.Copy).then_inc(s_xgc, 1)

                def sums(n):
                    act.wait_ge(s_wu, n * PASS_UNITS + (DENSE_UNITS + FIRST_UNITS + SLOTS))
                    act.activation(yx[:, :], ps[:, 4 * 512:6 * 512], ACT.Copy).then_inc(s_edc, 1)

                r0 = LAYER0_ROUNDS + MIX_ROUNDS
                tokens(0)
                highs(DENSE_UNITS, 0, 4, r0, 0)
                highs(DENSE_UNITS + 4, 4, 4, r0, 2)
                with act.Fori(0, n_p) as q:
                    c0 = q * EXP_CHUNKS + DENSE_CHUNKS
                    u0 = q * PASS_UNITS + (DENSE_UNITS + FIRST_UNITS)
                    r = q * PASS_ROUNDS + r0

                    def chunk(k, cc, j, rr):
                        act.wait_ge(s_wu, u0 + (SLOTS if cc == 0 else k * 6 + (SLOTS - 2)))
                        act.wait_ge(s_hm, c0 + k)
                        act.activation(hs[:, 0, :], bank(cc % 2, 0, SEQ), ACT.Silu).then_inc(s_si, 1)
                        highs(u0 + (k * 6 + 4), 2, 2, rr, j)
                        if cc == EXP_CHUNKS - 2:
                            act.wait_ge(s_st, q + 1)
                            act.activation(sca[:, :], bank(6, 0, SEQ), ACT.Copy).then_inc(s_stc, 1)
                        act.wait_ge(s_ht, c0 + k + (1 - DENSE_CHUNKS))
                        act.activation(hhi[:, cc % 2, :, 0:P], bank(2 + cc % 2, 0, SEQ).rearrange(
                            "p (h t) -> p h t", h=2), ACT.Copy).then_inc(s_hh, 1)
                        if cc == 0:
                            sums(q)
                        for u in range(2, 6):
                            high(u0 + (k * 6 + 4), 2, u, rr, j + u // 2)

                    for k in range(4):
                        chunk(k, k, 4 + 3 * k, r)
                    with act.Fori(2, EXP_CHUNKS // 2 - 1) as i:
                        for c in range(2):
                            chunk(i * 2 + c, 4 + c, 4 + 3 * c, r + i)
                    k = EXP_CHUNKS - 2
                    chunk(k, k, 4 + 3 * k, r)
                    tokens(q + 1)
                    chunk(k + 1, k + 1, 7 + 3 * k, r)
                sums(n_p)

            def ple(l):
                for m_ in range(KT):
                    act.wait_ge(s_pl, l * KT + (KT + m_ + 1))
                    if m_ >= 2:
                        act.wait_ge(s_pt, l * KT + (m_ - 1))
                    act.activation(gs[:, m_ % 2, :], bank(2 * (m_ % 2) + 1, 0, SEQ), ACT.Sigmoid).then_inc(s_pg, 1)

            act.dma_start(relb_sb, relb).then_inc(s_relL, 16)
            act.wait_ge(s_x, 16)
            squares(None)
            act.wait_ge(s_relT, 1)
            act.activation(rows_sb, ps[0:ATT_HEADS, 0:3 * 512].rearrange("p (g c) -> p g c", g=3),
                           ACT.Copy).then_inc(s_relC, 1)
            act.wait_ge(s_relC, 1)
            act.dma_start(scratch.ap(), rows_sb).then_inc(s_relW, 16)
            with act.Fori(0, DEPTH) as l:
                norm_root(l * 2)
                project(l)
                fnet(l)
                conv_norm(l)
                ssm_heads(l)
                attention(l)
                branches(l)
                squares(l * (2 * KT))
                norm_root(l * 2 + 1)
                with act.If(l < 1):
                    dense()
                with act.Else():
                    route()
                    experts()
                ple(l)
                squares(l * (2 * KT) + KT)
                with act.If(l < DEPTH - 1):
                    act.dma_start(pk[:, :], pk_in[DEPTH - 1]).then_inc(s_pk, 16)
            norm_root(2 * DEPTH)

        @block.vector
        def _(dve):
            def gain(k, j):
                return cst[:, bass.ds(k * KT + (CAT["gains"] + j), 1)]

            def norm(k):
                dve.wait_ge(s_ms, k + 1)
                dve.tensor_scalar(rms_t[:, 0, :], bank(7, 0, SEQ), 1.0 / D_MODEL, EPS, ALU.mult,
                                  ALU.add).then_inc(s_var, 1)
                dve.wait_ge(s_sd, k + 1)
                dve.reciprocal(rstd[:, :], rms_t[:, 1, :]).then_inc(s_rs, 1)
                dve.wait_ge(s_rs, k + 1)
                for j in range(KT):
                    dve.scalar_tensor_tensor(out=xn[:, j, :], in0=h[:, j, :], scalar=gain(k, j), in1=rstd[:, :],
                                             op0=ALU.mult, op1=ALU.mult).then_inc(s_xn, 1)

            def early_low(l, j):
                dve.wait_ge(s_eh, l * (2 * EARLY_BLOCKS) + (2 * j + 1))
                dve.tensor_tensor(ring_lo[:, j % RING, 0:UNIT], ring[:, j % RING, 0:UNIT], whi[:, 2 * j % SLOTS, :],
                                  ALU.subtract).then_inc(s_ed, 1)

            def early(l):
                for k in range(4):
                    dve.wait_ge(s_eih, l * 4 + (k + 1))
                    dve.tensor_tensor(xlo[:, 2 * k:2 * k + 2, :], xn[:, 2 * k:2 * k + 2, :],
                                      (hhi if k < 2 else hlo)[:, k % 2, :, :], ALU.subtract).then_inc(s_eil, 1)
                    if k == 0:
                        early_low(l, 0)
                early_low(l, 2)
                early_low(l, 4)

            def depthwise(l, dst, src, taps, w, b, tiles, s, n):
                for tap in range(taps):
                    if tap in (5, 10, 15, 20, 25):
                        early_low(l, 4 + 2 * (tap // 5))
                    for c in range(tiles):
                        col = par(w, tap * tiles + c)
                        if tap == 0:
                            i = dve.tensor_scalar(dst[:, c, :], src[:, c, 0:SEQ], col, par(b, c), ALU.mult, ALU.add)
                        else:
                            dve.wait_ge(s, n + ((tap - 1) * tiles + c + 1))
                            i = dve.scalar_tensor_tensor(out=dst[:, c, :], in0=src[:, c, tap:tap + SEQ], scalar=col,
                                                         in1=dst[:, c, :], op0=ALU.mult, op1=ALU.add)
                        i.then_inc(s, 1)

            def ssm_conv(l):
                n = l * (XT * SSM_CONV)
                for c in range(XT):
                    dve.wait_ge(s_pf, l * N_PROJ + (T_XBC + c + 1))
                    for tap in range(SSM_CONV):
                        col = par("ssm_w", tap * XT + c)
                        if tap == 0:
                            i = dve.tensor_scalar(xbc[:, c, :], xbcp[:, c, 0:SEQ], col, par("ssm_b", c), ALU.mult, ALU.add)
                        else:
                            dve.wait_ge(s_xc, n + (c * SSM_CONV + tap))
                            i = dve.scalar_tensor_tensor(out=xbc[:, c, :], in0=xbcp[:, c, tap:tap + SEQ], scalar=col,
                                                         in1=xbc[:, c, :], op0=ALU.mult, op1=ALU.add)
                        i.then_inc(s_xc, 1)

            def time_steps(l):
                dve.wait_ge(s_pf, l * N_PROJ + (T_DT + 1))
                done = 0

                def link(i):
                    nonlocal done
                    done += 1
                    i.then_inc(s_dtc, 1)
                    dve.wait_ge(s_dtc, l * DTC + done)

                raw = dts[:, 0, :].rearrange("p (t d) -> p t d", t=TT)
                bias_t = par("dt_bias", 0, DT)
                for tt in range(TT):
                    i = dve.tensor_tensor(raw[:, tt, :], raw[:, tt, :], bias_t, ALU.add)
                    if tt == 0:
                        i.then_inc(s_dtc, 1)
                        done += 1
                    else:
                        link(i)
                link(dve.scalar_tensor_tensor(out=dts[:, 2, :], in0=dts[:, 0, :], scalar=-1.0, in1=dts[:, 0, :],
                                              op0=ALU.mult, op1=ALU.min))
                dve.wait_ge(s_dta, l * 2 + 1)
                link(dve.tensor_scalar(dts[:, 4, :], dts[:, 3, :], 2.0, None, ALU.add))
                link(dve.reciprocal(dts[:, 5, :], dts[:, 4, :]))
                link(dve.tensor_tensor(dts[:, 6, :], dts[:, 3, :], dts[:, 5, :], ALU.mult))
                link(dve.tensor_tensor(dts[:, 7, :], dts[:, 6, :], dts[:, 6, :], ALU.mult))
                link(dve.tensor_scalar(dts[:, 1, :], dts[:, 7, :], 1.0 / 17, None, ALU.mult))
                for c in range(15, 1, -2):
                    link(dve.scalar_tensor_tensor(out=dts[:, 1, :], in0=dts[:, 1, :], scalar=1.0 / c,
                                                  in1=dts[:, 7, :], op0=ALU.add, op1=ALU.mult))
                link(dve.scalar_tensor_tensor(out=dts[:, 1, :], in0=dts[:, 1, :], scalar=1.0, in1=dts[:, 6, :],
                                              op0=ALU.add, op1=ALU.mult))
                link(dve.tensor_scalar(dts[:, 2, :], dts[:, 0, :], 0.0, None, ALU.max))
                dt_flat = dt_[:, :, :].rearrange("p t d -> p (t d)")
                link(dve.scalar_tensor_tensor(out=dt_flat, in0=dts[:, 1, :], scalar=2.0, in1=dts[:, 2, :],
                                              op0=ALU.mult, op1=ALU.add))
                dve.wait_ge(s_dta, l * 2 + 2)
                for tt in range(TT):
                    i = dve.scalar_tensor_tensor(out=dta[:, tt, :], in0=dt_[:, tt, :], scalar=-1.0, in1=a_neg[:, :],
                                                 op0=ALU.mult, op1=ALU.mult)
                    i.then_inc(s_dtc, 1)
                    done += 1
                assert done == DTC, done

            def conv(l):
                dve.wait_ge(s_glu, l * 2 + 2)
                depthwise(l, cv, glu, CONV_K, "conv_dw", "conv_b", CT, s_cvw, l * (CT * CONV_K))

            def conv_norm(l):
                dve.wait_ge(s_lns, l * 2 + 1)
                for c in range(CT):
                    i = dve.scalar_tensor_tensor(out=cvx[:, c, :], in0=bank(7, 0, SEQ), scalar=-1.0 / CONV_CH,
                                                 in1=cv[:, c, :], op0=ALU.mult, op1=ALU.add)
                i.then_inc(s_lnc, 1)
                dve.wait_ge(s_lnc, l * 5 + 1)
                dve.tensor_tensor(cv[:, :, :], cvx[:, :, :], cvx[:, :, :], ALU.mult).then_inc(s_lnc, 1)
                dve.wait_ge(s_lns, l * 2 + 2)
                dve.tensor_scalar(rms_t[:, 0, :], bank(7, SEQ, SEQ), 1.0 / CONV_CH, EPS, ALU.mult,
                                  ALU.add).then_inc(s_lnc, 1)
                dve.wait_ge(s_lna, l * (CT + 1) + 1)
                dve.reciprocal(rstd[:, :], rms_t[:, 1, :]).then_inc(s_lnc, 1)
                dve.wait_ge(s_lnc, l * 5 + 4)
                for c in range(CT):
                    i = dve.tensor_tensor(cvx[:, c, :], cvx[:, c, :], rstd[:, :], ALU.mult)
                i.then_inc(s_lnc, 1)

            def ssm_scores(l):
                for g in range(SSM_GROUPS):
                    dve.wait_ge(s_bc, l * 2 + (g + 1))
                    src = bank(6 + g)
                    dve.tensor_tensor(sc[:, g, 0, :], src[:, 0:P], con("upto"), ALU.mult)
                    dve.tensor_copy(sc[:, g, 1, :], src[:, P:2 * P])
                    dve.tensor_tensor(sc[:, g, 2, :], src[:, 3 * P:4 * P], con("upto"), ALU.mult)
                    dve.tensor_tensor(sc[:, g, 3, :], src[:, 0:P], con("from"), ALU.mult)
                    dve.tensor_copy(sc[:, g, 4, :], src[:, 2 * P:3 * P])
                    dve.tensor_tensor(sc[:, g, 5, :], src[:, 3 * P:4 * P], con("from"), ALU.mult).then_inc(s_sc, 1)

            def ssm_heads(l):
                with dve.Fori(0, SSM_HEADS // SSM_GROUPS) as hh:
                    dve.wait_ge(s_sc, l * 2 + 2)
                    dve.wait_ge(s_xtc, l * TT + TT)
                    n = l * SSM_HEADS + hh * 2
                    for g in range(SSM_GROUPS):
                        c0 = (n + g) * SSM_HC
                        dve.wait_ge(s_r, n + (g + 3))
                        for part in range(4):
                            dve.tensor_tensor_reduce(dg[:, part, :], bank(g, part * P, P), con("ident"), -1.0, 0.0, ALU.mult,
                                                     ALU.add, nb[:, g, part:part + 1]).then_inc(s_hc, 1)
                        dve.wait_ge(s_hc, c0 + 4)
                        dve.tensor_tensor(nb[:, g, 4:5], bank(g, P - 1, 1), nb[:, g, 0:1], ALU.add).then_inc(s_hc, 1)
                        dve.tensor_tensor(nb[:, g, 5:6], bank(g, 3 * P, 1), nb[:, g, 3:4], ALU.add).then_inc(s_hc, 1)
                        dve.wait_ge(s_hc, c0 + 6)
                        for b, (row, col) in enumerate(((0, 0), (1, 4), (1, 1), (2, 2), (2, 5), (3, 3))):
                            i = dve.tensor_scalar(ex[:, g, b, :], bank(g, row * P, P), nb[:, g, col:col + 1], 0.0,
                                                  ALU.add, ALU.min)
                        i.then_inc(s_hc, 1)
                        if g == 1:
                            head_mix(l, hh, n, 0)
                    head_mix(l, hh, n, 1)
                    for g in range(SSM_GROUPS):
                        head_y(l, hh, n, g)

            def head_mix(l, hh, n, g):
                dve.wait_ge(s_ex, n + (g + 1))
                for lo, hi, tt, d in ((0, 2, 0, 0), (2, 3, 1, 0), (3, 4, 0, 1), (4, 6, 1, 1)):
                    i = dve.scalar_tensor_tensor(out=mm_[:, g, lo:hi, :], in0=ex[:, g, lo:hi, :],
                                                 scalar=dt_[:, tt, bass.ds(hh + (d * SSM_HEADS + g * 4), 1)],
                                                 in1=sc[:, g, lo:hi, :], op0=ALU.mult, op1=ALU.mult)
                i.then_inc(s_mm, 1)
                dve.wait_ge(s_mm, n + (g + 1))

            def head_y(l, hh, n, g):
                dve.wait_ge(s_y, n + (g + 1))
                for tt in range(TT):
                    i = dve.scalar_tensor_tensor(out=ys[:, tt, bass.ds(hh * 64 + g * 256, 64)],
                                                 in0=xs[:, tt, bass.ds(hh * 64 + g * 256, 64)],
                                                 scalar=pk[:, bass.ds(hh + (AT["ssm_d"] + g * 4), 1)],
                                                 in1=bank(2 + g, tt * 64, 64), op0=ALU.mult, op1=ALU.add)
                i.then_inc(s_yh, 1)

            def ssm_out(l):
                c0 = l * SSM_YC
                dve.wait_ge(s_yh, l * SSM_HEADS + SSM_HEADS)
                dve.tensor_tensor(ys[:, :, :], ys[:, :, :], z[:, :, :], ALU.mult).then_inc(s_yc, 1)
                dve.wait_ge(s_yc, c0 + 1)
                for tt in range(TT):
                    if tt:
                        dve.wait_ge(s_yc, c0 + 1 + tt)
                    dve.tensor_tensor_reduce(ysq[:, :], ys[:, tt, :], ys[:, tt, :], 1.0, 0.0, ALU.mult, ALU.add,
                                             yst[:, tt:tt + 1]).then_inc(s_yc, 1)
                dve.wait_ge(s_yc, c0 + 3)
                dve.tensor_scalar(yst[:, 2:4], yst[:, 0:2], 1.0 / SSM_INNER, EPS, ALU.mult, ALU.add).then_inc(s_yc, 1)
                dve.wait_ge(s_ya, l + 1)
                dve.reciprocal(yst[:, 6:8], yst[:, 4:6]).then_inc(s_yc, 1)
                dve.wait_ge(s_yc, c0 + 5)
                for tt in range(TT):
                    i = dve.tensor_scalar(ys[:, tt, :], ys[:, tt, :], yst[:, 6 + tt:7 + tt], None, ALU.mult)
                i.then_inc(s_yc, 1)

            def gated(l, b, m_, first_bank=6, banks=2):
                n = l * (N_BRANCHES * KT) + b * KT
                dve.wait_ge(s_sg, n + (m_ + 1))
                dve.tensor_tensor(gt[:, m_ % 2, :], gs[:, m_ % 2, :], bank(first_bank + m_ % banks, 0, SEQ), ALU.mult).then_inc(s_bt, 1)
                dve.wait_ge(s_bt, n + (m_ + 1))
                dve.tensor_tensor(mix[:, m_, :], mix[:, m_, :], gt[:, m_ % 2, :], ALU.add).then_inc(s_bm, 1)

            def pair(l, i, half):
                n = l * UNITS + i * 8 + 4 * half

                def biased(u):
                    dve.wait_ge(s_s, n + (u + 2))
                    if u % TT == 0:
                        dve.wait_ge(s_bia[u // TT], (l * HP + i * 2 + (half + 1)) * (16 * TT))
                    if u >= 2:
                        dve.wait_ge(s_t, n + (u - 1))
                    dve.scalar_tensor_tensor(out=sa[:, u % 2, :], in0=bank(4, 0, GK),
                                             scalar=float(ATT_HEAD_DIM) ** -0.5, in1=bias[u // TT][:, u % TT, :],
                                             op0=ALU.mult, op1=ALU.add).then_inc(s_sb, 1)
                    dve.wait_ge(s_sb, n + (u + 1))
                    dve.tensor_reduce(ast[:, u % 2, 2:3], sa[:, u % 2, :], AX_X, ALU.max).then_inc(s_mx, 1)
                    dve.wait_ge(s_mx, n + (u + 1))
                    dve.tensor_scalar(ast[:, u % 2, 0:1], ast[:, u % 2, 2:3], -1.0, None, ALU.mult).then_inc(s_am, 1)

                def inverse(u):
                    dve.wait_ge(s_e, n + (u + 1))
                    dve.reciprocal(ast[:, u % 2, 3:4], ast[:, u % 2, 1:2]).then_inc(s_dn, 1)

                def scaled(u):
                    dve.wait_ge(s_dn, n + (u + 1))
                    dve.wait_ge(s_o, n + (u + 1))
                    dve.tensor_scalar(ao[:, u % TT, bass.ds(i * (2 * P) + (half * P + 64 * (u // TT)), 64)],
                                      bank(2 * (u % 2), GK, 64), ast[:, u % 2, 3:4], None,
                                      ALU.mult).then_inc(s_oc, 1)

                def tile(k):
                    gated(l, i, 4 * half + k)

                biased(0)
                tile(0)
                biased(1)
                inverse(0)
                tile(1)
                biased(2)
                scaled(0)
                inverse(1)
                tile(2)
                biased(3)
                scaled(1)
                inverse(2)
                tile(3)
                scaled(2)
                inverse(3)
                scaled(3)

            def attention(l):
                dve.memset(mix[:, :, :], 0.0).then_inc(s_mz, 1)
                with dve.Fori(0, HB) as i:
                    dve.wait_ge(s_mz, l + 1)
                    for half in range(2):
                        pair(l, i, half)

            def late_low(units, u, j):
                dve.wait_ge(s_th, units + (u + 1))
                lo = u % 2 * UNIT
                dve.tensor_tensor(wlo[:, u % SLOTS, :], ring[:, j % RING, lo:lo + UNIT], whi[:, u % SLOTS, :],
                                  ALU.subtract).then_inc(s_tl, 1)

            def input_low(l, first, src):
                for k in range(4):
                    dve.wait_ge(s_ih, l * KT + (first + k + 1))
                    dve.tensor_tensor(xlo[:, 2 * k:2 * k + 2, :], src[:, 2 * k:2 * k + 2, :], xhi[:, 2 * k:2 * k + 2, :],
                                      ALU.subtract).then_inc(s_il, 1)

            def branches(l):
                input_low(l, 0, xn)
                for u in range(2):
                    late_low(l * LATE_UNITS, u, PROJ_BLOCKS)
                with dve.Fori(HB, N_BRANCHES) as b:
                    units = l * LATE_UNITS + b * BRANCH_UNITS + (-HB * BRANCH_UNITS)

                    def lows_of(first, n):
                        for u in range(first, first + n):
                            late_low(units, u, PROJ_BLOCKS + u // 2)

                    dve.wait_ge(s_lbh, l * HB + b + (1 - HB))
                    dve.tensor_tensor(hlo[:, :, :, :].rearrange("p a b t -> p (a b) t"),
                                      ybr[:, bass.ds(b * CT, CT), :],
                                      hhi[:, :, :, :].rearrange("p a b t -> p (a b) t"), ALU.subtract).then_inc(s_lbl, 1)
                    lows_of(2, 4)
                    for m_ in range(0, KT, 2):
                        gated(l, b, m_, 4, 4)
                        gated(l, b, m_ + 1, 4, 4)
                        if m_ < 6:
                            lows_of(6 + (0, 2, 6)[m_ // 2], (2, 4, 2)[m_ // 2])
                dve.wait_ge(s_bm, (l + 1) * (N_BRANCHES * KT) + 2)
                input_low(l, 4, mix)
                for u in range(2, 8):
                    late_low(l * LATE_UNITS + HB * BRANCH_UNITS, u, PROJ_BLOCKS + u // 2)

            def mix_out(l):
                for m_ in range(KT):
                    dve.wait_ge(s_wo, l * KT + (m_ + 1))
                    dve.tensor_tensor(h[:, m_, :], h[:, m_, :], bank(m_ % 4, 0, SEQ), ALU.add).then_inc(s_hr, 1)

            def low(units, first, u, r, j):
                slot = (first + u) % SLOTS
                dve.wait_ge(s_wh, units + (u + 1))
                lo = (first + u) % 2 * UNIT
                dve.tensor_tensor(wlo[:, slot, :], ring[:, j % RING, lo:lo + UNIT], whi[:, slot, :],
                                  ALU.subtract).then_inc(s_wl, 1)

            def lows(units, first, n, j):
                for u in range(n):
                    low(units, first, u, 0, j + (first % 2 + u) // 2)

            def dense():
                for k in range(4):
                    dve.wait_ge(s_xh, k + 1)
                    dve.tensor_tensor(xlo[:, 2 * k:2 * k + 2, :], xn[:, 2 * k:2 * k + 2, :], xhi[:, 2 * k:2 * k + 2, :],
                                      ALU.subtract).then_inc(s_xl, 1)
                lows(0, 0, 8, 0)

                def chunk(c, par_, n, units, j, first=False):
                    dve.wait_ge(s_si, c + 1)
                    if not first:
                        dve.wait_ge(s_hl, c)
                    dve.tensor_tensor(hid[:, :, :], hs[:, :, :],
                                      ps[:, 1024:2048].rearrange("p (b t) -> p b t", b=2)[:, :, 0:SEQ],
                                      ALU.mult).then_inc(s_hm, 1)
                    if n:
                        lows(units, 2, 1, j)
                    dve.wait_ge(s_hh, c + 1)
                    dve.tensor_tensor(hlo[:, par_, :, :], hid[:, :, :], hhi[:, par_, :, :],
                                      ALU.subtract).then_inc(s_hl, 1)
                    for u in range(1, n):
                        low(units, 2, u, 0, j + u // 2)

                chunk(0, 0, 6, 8, 4, first=True)
                with dve.Fori(0, (DENSE_CHUNKS - 3) // 2) as i:
                    for c in range(2):
                        chunk(i * 2 + (c + 1), (c + 1) % 2, 6, i * 12 + (14 + 6 * c), 7 + 3 * c)
                c = DENSE_CHUNKS - 2
                chunk(c, c % 2, 4, 8 + 6 * c, 4 + 3 * c)
                chunk(c + 1, (c + 1) % 2, 0, 0, 0)
                dve.wait_ge(s_wu, DENSE_UNITS + SLOTS)
                for m_ in range(KT):
                    i = dve.tensor_tensor(h[:, m_, :], h[:, m_, :], bank(4 + m_ // 2, (m_ % 2) * SEQ, SEQ), ALU.add)
                i.then_inc(s_h, 1)

            def route():
                done = 0

                def link(i, s=s_rc):
                    nonlocal done
                    done += 1
                    i.then_inc(s_rc, 1)
                    dve.wait_ge(s_rc, done)

                dve.wait_ge(s_rl, 1)
                link(dve.tensor_copy(lg[:, :, :], bank(4, 0, TT * N_EXPERTS).rearrange("p (t e) -> p t e", t=TT)))
                for tt in range(TT):
                    link(dve.max(top[:, tt, :], lg[:, tt, :]))
                    link(dve.max_index(topi[:, tt, :], top[:, tt, :], lg[:, tt, :]))
                link(dve.tensor_tensor(rt[:, :, 0:1], top[:, :, 1:2], top[:, :, 0:1], ALU.subtract))
                assert done == RC_EXP
                link(dve.tensor_copy(topf[:, :, :], topi[:, :, :]))
                for tt in range(TT):
                    for c in range(2):
                        link(dve.tensor_scalar(oh[:, tt, c, :], con("experts", 0, N_EXPERTS), topf[:, tt, c:c + 1], None,
                                               ALU.is_equal))
                    link(dve.tensor_tensor(msk[:, tt, :], oh[:, tt, 0, :], oh[:, tt, 1, :], ALU.add))
                assert done == RC_MASK, done
                dve.wait_ge(s_re, 1)
                link(dve.tensor_scalar(rt[:, :, 2:3], rt[:, :, 1:2], 1.0, None, ALU.add))
                link(dve.reciprocal(rt[:, :, 3:4], rt[:, :, 2:3]))
                link(dve.tensor_tensor(rt[:, :, 4:5], rt[:, :, 3:4], rt[:, :, 1:2], ALU.mult))
                for tt in range(TT):
                    link(dve.tensor_scalar(comb[:, tt, 0:N_EXPERTS], oh[:, tt, 0, :], rt[:, tt, 3:4], None, ALU.mult))
                    link(dve.scalar_tensor_tensor(out=comb[:, tt, 0:N_EXPERTS], in0=oh[:, tt, 1, :], scalar=rt[:, tt, 4:5],
                                                  in1=comb[:, tt, 0:N_EXPERTS], op0=ALU.mult, op1=ALU.add))
                by_pass = comb[:, :, 0:MAX_PASSES].rearrange("p t (r e) -> p t r e", r=2)
                link(dve.tensor_copy(by_pass[:, :, 1, :], by_pass[:, :, 0, :]))
                link(dve.memset(comb[:, :, MAX_PASSES:], 0.0))
                link(dve.memset(pos[:, :, :], -1.0))
                dve.memset(sca[:, :], 0.0).then_inc(s_stc, 1)
                dve.wait_ge(s_rp, 1)
                first = pos[:, :, 0:N_EXPERTS]
                link(dve.tensor_scalar(first, bank(5, 0, TT * N_EXPERTS).rearrange("p (t e) -> p t e", t=TT),
                                       1.0, None, ALU.add))
                link(dve.tensor_tensor(first, first, msk[:, :, :], ALU.mult))
                link(dve.tensor_scalar(first, first, -1.0, None, ALU.add))
                link(dve.tensor_scalar(pos[:, :, N_EXPERTS:MAX_PASSES], first, -float(P), None, ALU.add))
                link(dve.tensor_reduce(cnt[:, 0:1], bank(5, 2 * N_EXPERTS, N_EXPERTS), AX_X, ALU.max))
                link(dve.tensor_scalar(cnt[:, 1:2], cnt[:, 0:1], float(P), float(N_EXPERTS), ALU.is_gt, ALU.mult))
                link(dve.tensor_scalar(cnt[:, 1:2], cnt[:, 1:2], float(N_EXPERTS), None, ALU.add))
                dve.tensor_copy(passes_sb[:, :], cnt[:, 1:2]).then_inc(s_rr, 1)
                dve.wait_ge(s_rr, 1)

            def experts():
                n_p = dve.value_load(passes_sb[0:1, 0:1], min_val=N_EXPERTS, max_val=MAX_PASSES)

                def one_hots(n):
                    for tt in range(TT):
                        i = dve.tensor_scalar(gat[:, tt, :], con("slots"), pos[:, tt, bass.ds(n, 1)], None, ALU.is_equal)
                    i.then_inc(s_g, 1)
                    dve.wait_ge(s_g, n + 1)
                    for tt in range(TT):
                        i = dve.tensor_scalar(gatw[:, tt, :], gat[:, tt, :], comb[:, tt, bass.ds(n, 1)], None, ALU.mult)
                    i.then_inc(s_gw, 1)

                def tokens(n):
                    for j in range(2):
                        dve.wait_ge(s_xgc, n * 2 + (j + 1))
                        dve.tensor_tensor(xlo[:, 4 * j:4 * j + 4, 0:P], bank(6 + j).rearrange("p (c t) -> p c t", c=4),
                                          xhi[:, 4 * j:4 * j + 4, 0:P], ALU.subtract).then_inc(s_xl, 1)

                def add(n, m_):
                    dve.wait_ge(s_eo, n * KT + (m_ + 1))
                    if m_ == 0:
                        dve.wait_ge(s_ea, n * KT + 2)
                    dve.tensor_tensor(h[:, m_, :], h[:, m_, :], bank(6 + m_ % 2, 0, SEQ), ALU.add).then_inc(s_ea, 1)

                one_hots(0)
                tokens(0)
                lows(DENSE_UNITS, 0, 8, 0)
                with dve.Fori(0, n_p) as q:
                    c0 = q * EXP_CHUNKS + DENSE_CHUNKS
                    u0 = q * PASS_UNITS + (DENSE_UNITS + FIRST_UNITS)

                    def chunk(k, cc, j):
                        dve.wait_ge(s_si, c0 + k + 1)
                        dve.tensor_tensor(hid[:, 0, :], hs[:, 0, :], bank(cc % 2, SEQ, SEQ), ALU.mult).then_inc(s_hm, 1)
                        lows(u0 + (k * 6 + 4), 2, 2, j)
                        for m_ in {1: (0, 1, 2, 3), 2: (6, 7)}.get(k if k is cc else None, ()):
                            add(q, m_)
                        dve.wait_ge(s_hh, c0 + k + 1)
                        dve.tensor_tensor(hlo[:, cc % 2, :, 0:P], bank(2 + cc % 2, 0, SEQ).rearrange(
                            "p (h t) -> p h t", h=2), hhi[:, cc % 2, :, 0:P], ALU.subtract).then_inc(s_hl, 1)
                        if cc == EXP_CHUNKS - 2:
                            dve.wait_ge(s_st, q + 1)
                            one_hots(q + 1)
                        for u in range(2, 6):
                            low(u0 + (k * 6 + 4), 2, u, 0, j + u // 2)
                            if k is cc and k == 1 and u in (3, 4):
                                add(q, u + 1)

                    for k in range(4):
                        chunk(k, k, 4 + 3 * k)
                    with dve.Fori(2, EXP_CHUNKS // 2 - 1) as i:
                        for c in range(2):
                            chunk(i * 2 + c, 4 + c, 4 + 3 * c)
                    k = EXP_CHUNKS - 2
                    chunk(k, k, 4 + 3 * k)
                    tokens(q + 1)
                    chunk(k + 1, k + 1, 7 + 3 * k)
                for m_ in range(KT):
                    add(n_p, m_)
                dve.memset(cnt[:, 3:4], 0.0).then_inc(s_h, 1)

            def ple(l):
                dve.wait_ge(s_h, l + 1)
                for m_ in range(KT):
                    dve.wait_ge(s_pg, l * KT + (m_ + 1))
                    dve.tensor_tensor(mix[:, m_, :], gs[:, m_ % 2, :], bank(2 * (m_ % 2), 0, SEQ),
                                      ALU.mult).then_inc(s_pt, 1)
                dve.wait_ge(s_pt, l * KT + KT)
                for m_ in range(KT):
                    dve.tensor_tensor(h[:, m_, :], h[:, m_, :], mix[:, m_, :], ALU.add).then_inc(s_hr, 1)

            dve.sem_inc(s_bm, 2)
            dve.sem_inc(s_ea, 2)
            dve.wait_ge(s_zero, 2)
            dve.wait_ge(s_cst, 16)
            with dve.Fori(0, DEPTH) as l:
                norm(l * 2)
                dve.wait_ge(s_pk, l * 16 + 16)
                early(l)
                conv(l)
                early_low(l, 16)
                ssm_conv(l)
                time_steps(l)
                conv_norm(l)
                ssm_scores(l)
                ssm_heads(l)
                ssm_out(l)
                attention(l)
                branches(l)
                mix_out(l)
                norm(l * 2 + 1)
                with dve.If(l < 1):
                    dense()
                with dve.Else():
                    route()
                    experts()
                ple(l)
            norm(2 * DEPTH)

        @block.gpsimd
        def _(pool):
            for t in (glu, xbcp):
                pad = PAD if t is glu else SPAD
                pool.memset(t[:, :, 0:pad], 0.0)
                pool.memset(t[:, :, SEQ + pad:SEQ + 2 * pad], 0.0).then_inc(s_zero, 1)
            pool.wait_ge(s_zero, 2)
            pool.wait_ge(s_relW, 16)
            pool.wait_ge(s_cst, 16)

            def load_bias(l, i, slot):
                for tt in range(TT):
                    src = bass.AP(tensor=scratch.ap().tensor,
                                  offset=(i * 2 + slot) * (ATT_GROUPS * 2 * SEQ) + tt * P,
                                  ap=[[1, P], [2 * SEQ, ATT_GROUPS], [1, SEQ]])
                    dst = bias[slot][:, tt, :].rearrange("p (g k) -> p g k", g=ATT_GROUPS)
                    pool.dma_start(dst, src).then_inc(s_bia[slot], 16)

            with pool.Fori(0, DEPTH) as l:
                def early_lows(first, last):
                    for j, u in EARLY_POOL:
                        if first <= j < last:
                            pool.wait_ge(s_eh, l * (2 * EARLY_BLOCKS) + (2 * j + u + 1))
                            cols = slice(u * UNIT, u * UNIT + UNIT)
                            pool.tensor_tensor(ring_lo[:, j % RING, cols], ring[:, j % RING, cols],
                                               whi[:, (2 * j + u) % SLOTS, :], ALU.subtract).then_inc(s_ep, 1)

                for pair in range(2):
                    early_lows(3 * pair, 3 * pair + 3)
                    pool.wait_ge(s_pf, l * N_PROJ + (4 * pair + 4))
                    pool.tensor_tensor(glu[:, 2 * pair:2 * pair + 2, PAD:PAD + SEQ], glu_a[:, pair, :, :],
                                       glu_s[:, pair, :, :], ALU.mult).then_inc(s_glu, 1)
                load_bias(l, 0, 0)
                early_lows(6, EARLY_BLOCKS)
                pool.wait_ge(s_pj, l * N_PROJ + T_Q)
                pool.sem_inc(s_step, 1)
                with pool.Fori(0, SSM_HEADS // SSM_GROUPS) as hh:
                    pool.wait_ge(s_dtc, l * DTC + DTC)
                    n = l * SSM_HEADS + hh * 2
                    for g in range(SSM_GROUPS):
                        pool.wait_ge(s_r, n + (g + 1))
                        for d in range(2):
                            for tt in range(TT):
                                col = dta[:, tt, bass.ds(hh + (d * SSM_HEADS + g * 4), 1)]
                                k = pool.tensor_tensor(ua[:, g, 2 * d + tt, :], con("upto" if d == 0 else "from"),
                                                       col.to_broadcast([P, P]), ALU.mult)
                        k.then_inc(s_ua, 1)
                pool.wait_ge(s_lns, l * 2 + 2)
                pool.sem_inc(s_step, 1)
                load_bias(l, 0, 1)
                with pool.Fori(0, HP) as i:
                    pool.wait_ge(s_pf, l * N_PROJ + N_PROJ)
                    n = l * UNITS + i * 4
                    pool.wait_ge(s_s, n + 1)
                    pool.wait_ge(s_yc, l * SSM_YC + 1)
                    for which in range(2):
                        src = qk[:, which * ATT_GROUPS:(which + 1) * ATT_GROUPS, bass.ds(i, 1), :]
                        dst = qkp[:, which, :, :].rearrange("p g (o t) -> p g o t", o=1)
                        pool.tensor_copy(dst[:, :, :, ::-1] if which == 0 else dst, src).then_inc(s_qkp, 1)
                    with pool.If(i < HP - 1):
                        for slot in range(2):
                            pool.wait_ge(s_sb, n + (2 * slot + 2))
                            pool.sem_inc(s_step, 1)
                            load_bias(l, i + 1, slot)


def _cols(w, c0, c1, width=COLS):
    k = w.shape[0] // P
    return w[:, c0:c1].reshape(k, P, (c1 - c0) // width, width).transpose(2, 1, 0, 3).reshape(-1, P, k * width)


def _rows(w):
    return w.reshape(-1, 2, P, D_MODEL).transpose(0, 2, 1, 3).reshape(-1, P, BLK)


def _swiglu_blocks(w1, w3, w2):
    f = w1.shape[1]
    up = np.stack([_cols(w, 0, f).reshape(-1, P, KT, COLS) for w in (w1, w3)], axis=3)
    return up.reshape(-1, P, 2, BLK).transpose(0, 2, 1, 3), _rows(w2)


def _dense_blocks(w1, w3, w2):
    up, down = _swiglu_blocks(w1, w3, w2)
    return np.concatenate([up[0]] + [b for c in range(1, len(up)) for b in (up[c], down[c - 1:c])] + [down[-1:]])


def _expert_blocks(w1, w3, w2):
    parts = [_swiglu_blocks(*w) for w in zip(w1, w3, w2)]
    up = [u for p in parts for u in p[0]]
    down = [d for p in parts for d in p[1]]
    return np.concatenate(up[0:2] + [b for c in range(len(up)) for b in (down[c][None], up[(c + 2) % len(up)])])


def _mixer_blocks(w_in, w_gate, branch_out, w_out):
    c = OFF_CONV
    conv = [_cols(w_in, c + o, c + o + COLS) for o in (0, CONV_CH, COLS, CONV_CH + COLS)]
    xbc = OFF_SSM + SSM_INNER
    parts = conv + [_cols(w_in, xbc, OFF_DT), _cols(w_in, OFF_SSM, xbc),
                    _cols(w_in, OFF_FNET, OFF_FNET + FNET_WIDTH), _cols(w_in, 2 * OFF_CONV // 3, OFF_CONV),
                    _cols(w_in, 0, 2 * OFF_CONV // 3)]
    for b, where in enumerate(BRANCH_OF):
        gate = _cols(w_gate[where], 0, D_MODEL)
        o = _cols(branch_out[b], 0, D_MODEL, 512)
        parts += [gate[0:1], o[0:1], gate[1:3], o[1:2], gate[3:4]]
    return np.concatenate(parts + [_cols(w_out, 0, D_MODEL)])


def _per_partition(a):
    return a.reshape(-1, P).T


def _everywhere(a):
    return np.broadcast_to(a.reshape(1, -1), (P, a.size))


def _constants():
    t = np.arange(P)
    s = np.arange(SEQ)
    ch = 2 * np.pi * np.outer(t, t) / FNET_GROUP_DIM
    tk = 2 * np.pi * (np.outer(s, s) % SEQ) / SEQ
    norm = 1.0 / math.sqrt(SEQ * FNET_GROUP_DIM)

    def tokens(m):
        return m.reshape(TT, P, SEQ).transpose(1, 0, 2).reshape(P, TT * SEQ)

    parts = {"ident": np.eye(P), "upto": t[:, None] <= t[None], "from": t[:, None] >= t[None],
             "before": t[:, None] < t[None], "ones": np.ones((P, P)), "slots": np.tile(t, (P, 1)),
             "dft_ch": np.concatenate([np.cos(ch), np.sin(ch)], 1), "dft_cos": tokens(np.cos(tk)) * norm,
             "dft_sin": -tokens(np.sin(tk)) * norm, "experts": np.tile(np.arange(N_EXPERTS), (P, 1))}
    return np.concatenate([np.asarray(parts[n], np.float64) for n, _ in _CONSTS if n in parts], 1).astype(np.float32)


def _bucket_rows():
    oh = np.zeros((REL_BUCKETS + 1, ATT_GROUPS, 2 * SEQ), np.float32)
    for g, (window, dil) in enumerate(ATT_PATTERNS):
        half, hb = window // (2 * dil), REL_BUCKETS // 2
        for c in range(2 * SEQ):
            rel = c - (SEQ - 1)
            if rel % dil or abs(rel) > half * dil or rel >= SEQ:
                oh[REL_BUCKETS, g, c] = MASKED
                continue
            n, exact = abs(rel), hb // 2
            large = min(hb - 1, exact + int(math.log(max(n, 1) / exact) / math.log(REL_MAX_DIST / exact) * (hb - exact)))
            oh[(hb if rel > 0 else 0) + (n if n < exact else large), g, c] = 1.0
    return oh


def kernel(x, p, rel_bias, norm_mix, w_in, conv_dw, conv_dw_b, conv_ln_g, conv_ln_b, conv_out, ssm_conv_w,
           ssm_conv_b, ssm_a_log, ssm_dt_bias, ssm_d, ssm_norm, ssm_out, attn_out, fnet_out, w_gate, b_gate,
           w_out, norm_ffn, ffn_w1, ffn_w3, ffn_w2, moe_router, moe_w1, moe_w3, moe_w2, ple_gate, ple_proj,
           final_norm):
    from concourse import bacc
    from concourse.bass_utils import run_bass_kernel_spmd

    (x, p, rel_bias, norm_mix, w_in, conv_dw, conv_dw_b, conv_ln_g, conv_ln_b, conv_out, ssm_conv_w,
     ssm_conv_b, ssm_a_log, ssm_dt_bias, ssm_d, ssm_norm, ssm_out, attn_out, fnet_out, w_gate, b_gate,
     w_out, norm_ffn, ffn_w1, ffn_w3, ffn_w2, moe_router, moe_w1, moe_w3, moe_w2, ple_gate, ple_proj,
     final_norm) = [np.asarray(a) for a in (
         x, p, rel_bias, norm_mix, w_in, conv_dw, conv_dw_b, conv_ln_g, conv_ln_b, conv_out, ssm_conv_w,
         ssm_conv_b, ssm_a_log, ssm_dt_bias, ssm_d, ssm_norm, ssm_out, attn_out, fnet_out, w_gate, b_gate,
         w_out, norm_ffn, ffn_w1, ffn_w3, ffn_w2, moe_router, moe_w1, moe_w3, moe_w2, ple_gate, ple_proj,
         final_norm)]

    def by_token(a):
        return a.reshape(SEQ, -1, P).transpose(2, 1, 0)

    def params(l):
        parts = {
            "b_gate": _per_partition(b_gate[l][list(BRANCH_OF)]),
            "conv_dw": _per_partition(conv_dw[l]), "conv_b": _per_partition(conv_dw_b[l]),
            "ln_g": _per_partition(conv_ln_g[l]), "ln_b": _per_partition(conv_ln_b[l]),
            "ssm_w": _per_partition(ssm_conv_w[l]), "ssm_b": _per_partition(ssm_conv_b[l]),
            "ssm_norm": _per_partition(ssm_norm[l]), "ssm_d": _everywhere(ssm_d[l]),
            "a_log": _everywhere(ssm_a_log[l]), "dt_bias": _everywhere(ssm_dt_bias[l]),
            "w_dt": _cols(w_in[l], OFF_DT, OFF_FNET, DT)[0],
            "router": _cols(moe_router[0], 0, N_EXPERTS, N_EXPERTS)[0],
            "p": by_token(p[l, 0]).reshape(P, -1)}
        return np.concatenate([parts[n] for n, _ in _PARAMS], 1)

    gains = np.concatenate([np.stack([norm_mix, norm_ffn], 1).reshape(-1, D_MODEL), final_norm[None]])
    relb = np.concatenate([rel_bias, np.ones((1, rel_bias.shape[1]), rel_bias.dtype)])
    arrays = {
        "x_in": by_token(x[0]),
        "w_mixers": np.stack([_mixer_blocks(w_in[l], w_gate[l], (fnet_out[l], conv_out[l], ssm_out[l], attn_out[l]),
                                            w_out[l]) for l in range(DEPTH)]),
        "w_dense": _dense_blocks(ffn_w1[0], ffn_w3[0], ffn_w2[0]),
        "w_experts": _expert_blocks(moe_w1[0], moe_w3[0], moe_w2[0]),
        "w_ple": np.stack([np.concatenate([_cols(ple_gate[l], 0, D_MODEL), _rows(ple_proj[l])]) for l in range(DEPTH)]),
        "params": np.stack([params(l) for l in range(DEPTH)]),
        "constants": np.concatenate([_constants(), _per_partition(gains)], 1),
        "buckets": _bucket_rows(),
        "bias_table": relb,
    }
    arrays = {n: np.ascontiguousarray(a) for n, a in arrays.items()}
    nc = bacc.Bacc("TRN2", target_bir_lowering=False, num_devices=1)
    ins = [nc.dram_tensor(n, a.shape, mybir.dt.from_np(a.dtype), kind="ExternalInput").ap() for n, a in arrays.items()]
    out = nc.dram_tensor("trunk_out", (P, KT, SEQ), F32, kind="ExternalOutput").ap()
    trunk_program(nc, *ins, out)
    got = run_bass_kernel_spmd(nc, [arrays], core_ids=[0]).results[0]["trunk_out"]
    return got.transpose(2, 1, 0).reshape(1, SEQ, D_MODEL)
```
